# Optimizing a Trainium2 kernel written in Bass

```python
import math
import jax, jax.numpy as jnp
from jax import lax
import numpy as np
import jax
import jax.numpy as jnp

D_MODEL = 1024
BATCH = 1
SEQ = 512
DEPTH = 2

GRID_W = 64
HEAD_DIM = 64
NA_HEADS = D_MODEL // 128
NA_WIDTH = NA_HEADS * HEAD_DIM
NA_KH_MAX = 8
NA_KW = 16
GQA_HEADS = D_MODEL // 128
GQA_KV_HEADS = max(1, GQA_HEADS // 4)
GQA_WIDTH = GQA_HEADS * HEAD_DIM
GQA_KV_WIDTH = GQA_KV_HEADS * HEAD_DIM
Q_BLOCK = 128
ROPE_THETA = 10000.0
ROPE_AXIS_DIM = HEAD_DIM // 2
SG_WIDTH = D_MODEL // 2
SG_GROUPS = SG_WIDTH // HEAD_DIM
SG_CHUNK = 128
N_BRANCH = 3
LN_EPS = 1e-5
RMS_EPS = 1e-6
DEEPNORM_ALPHA = (2.0 * DEPTH) ** 0.25
DEEPNORM_BETA = (8.0 * DEPTH) ** -0.25
IN_SPLITS = (NA_WIDTH, NA_WIDTH, NA_WIDTH, NA_WIDTH,
             GQA_WIDTH, GQA_KV_WIDTH, GQA_KV_WIDTH, GQA_WIDTH,
             SG_WIDTH, SG_WIDTH, SG_WIDTH,
             N_BRANCH * D_MODEL)
IN_WIDTH = 4 * NA_WIDTH + 2 * GQA_WIDTH + 2 * GQA_KV_WIDTH + 3 * SG_WIDTH + N_BRANCH * D_MODEL


def _split_points():
    pts, acc = [], 0
    for w in IN_SPLITS[:-1]:
        acc += w
        pts.append(acc)
    return pts

def layer_norm(x, g, b):
    xf = x.astype(jnp.float32)
    mu = jnp.mean(xf, axis=-1, keepdims=True)
    var = jnp.mean(jnp.square(xf - mu), axis=-1, keepdims=True)
    return ((xf - mu) * lax.rsqrt(var + LN_EPS)).astype(x.dtype) * g + b

def rms_norm(x, g):
    xf = x.astype(jnp.float32)
    ms = jnp.mean(jnp.square(xf), axis=-1, keepdims=True)
    return (xf * lax.rsqrt(ms + RMS_EPS)).astype(x.dtype) * g

def axial_rope_tables(s):
    t = jnp.arange(s)
    row = (t // GRID_W).astype(jnp.float32)
    col = (t % GRID_W).astype(jnp.float32)
    freqs = ROPE_THETA ** (-jnp.arange(0, ROPE_AXIS_DIM, 2, dtype=jnp.float32) / ROPE_AXIS_DIM)
    ang = jnp.concatenate([row[:, None] * freqs, col[:, None] * freqs], axis=-1)
    return jnp.cos(ang), jnp.sin(ang)

def apply_rope(x, cos, sin):
    xf = x.astype(jnp.float32).reshape(*x.shape[:-1], HEAD_DIM // 2, 2)
    x0, x1 = xf[..., 0], xf[..., 1]
    c = cos[None, :, None, :]
    s = sin[None, :, None, :]
    out = jnp.stack([x0 * c - x1 * s, x0 * s + x1 * c], axis=-1)
    return out.reshape(x.shape).astype(x.dtype)

def neighbourhood_attention(q, k, v, rpb):
    b, s, h, dh = q.shape
    rows = s // GRID_W
    kh = min(NA_KH_MAX, rows)
    r = jnp.arange(rows)
    row_start = jnp.clip(r - kh // 2, 0, rows - kh)
    key_rows = row_start[:, None] + jnp.arange(kh)[None, :]
    c = jnp.arange(GRID_W)
    col_start = jnp.clip(c - NA_KW // 2, 0, GRID_W - NA_KW)
    col_valid = (c[None, :] >= col_start[:, None]) & (c[None, :] < col_start[:, None] + NA_KW)
    qg = q.reshape(b, rows, GRID_W, h, dh)
    kg = k.reshape(b, rows, GRID_W, h, dh)[:, key_rows]
    vg = v.reshape(b, rows, GRID_W, h, dh)[:, key_rows]
    scores = jnp.einsum('brqhd,brjkhd->bhrqjk', qg, kg).astype(jnp.float32) * (dh ** -0.5)
    row_off = key_rows - r[:, None] + (NA_KH_MAX - 1)
    col_off = jnp.clip(c[None, :] - c[:, None] + (NA_KW - 1), 0, 2 * NA_KW - 2)
    bias = rpb[:, row_off[:, None, :, None], col_off[None, :, None, :]]
    scores = scores + bias.astype(jnp.float32)
    scores = jnp.where(col_valid[:, None, :], scores, jnp.float32(-1e30))
    shp = scores.shape
    p = jax.nn.softmax(scores.reshape(b, h, rows, GRID_W, kh * GRID_W), axis=-1)
    p = p.reshape(shp).astype(v.dtype)
    out = jnp.einsum('bhrqjk,brjkhd->brqhd', p, vg)
    return out.reshape(b, s, h * dh)

def gqa_attention(q, k, v):
    b, s, hq, dh = q.shape
    hkv = k.shape[2]
    grp = hq // hkv
    nblk = s // Q_BLOCK
    qb = q.reshape(b, nblk, Q_BLOCK, hkv, grp, dh).transpose(1, 0, 2, 3, 4, 5)
    scale = dh ** -0.5

    def block(qi):
        sc = jnp.einsum('bqkgd,bskd->bkgqs', qi, k).astype(jnp.float32) * scale
        p = jax.nn.softmax(sc, axis=-1).astype(v.dtype)
        return jnp.einsum('bkgqs,bskd->bqkgd', p, v)

    out = lax.map(block, qb)
    return out.transpose(1, 0, 2, 3, 4, 5).reshape(b, s, hq * dh)

def spatial_gating(u, v, ln_g, ln_b, w_s, b_s):
    b, s, wc = u.shape
    vn = layer_norm(v, ln_g, ln_b)
    vc = vn.reshape(b, s // SG_CHUNK, SG_CHUNK, SG_GROUPS, wc // SG_GROUPS)
    mixed = jnp.einsum('gmn,bcngd->bcmgd', w_s, vc) + b_s.T[None, None, :, :, None]
    return u * mixed.reshape(b, s, wc)

def hybrid_layer(x, w_in, b_in, na_rpb, q_norm_g, k_norm_g, sg_ln_g, sg_ln_b, sg_w, sg_b,
                 w_br_a, w_br_b, w_br_c, w_out, b_out, ln_g, ln_b, rope_cos, rope_sin):
    b, s, d = x.shape
    hcat = x @ w_in + b_in
    (na_q, na_k, na_v, na_z, gq_q, gq_k, gq_v, gq_z,
     sg_u, sg_v, sg_z, gates) = jnp.split(hcat, _split_points(), axis=-1)

    y_a = neighbourhood_attention(na_q.reshape(b, s, NA_HEADS, HEAD_DIM),
                                  na_k.reshape(b, s, NA_HEADS, HEAD_DIM),
                                  na_v.reshape(b, s, NA_HEADS, HEAD_DIM), na_rpb)
    p_a = (y_a * jax.nn.silu(na_z)) @ w_br_a

    q = apply_rope(rms_norm(gq_q.reshape(b, s, GQA_HEADS, HEAD_DIM), q_norm_g), rope_cos, rope_sin)
    k = apply_rope(rms_norm(gq_k.reshape(b, s, GQA_KV_HEADS, HEAD_DIM), k_norm_g), rope_cos, rope_sin)
    y_b = gqa_attention(q, k, gq_v.reshape(b, s, GQA_KV_HEADS, HEAD_DIM))
    p_b = (y_b * jax.nn.silu(gq_z)) @ w_br_b

    y_c = spatial_gating(sg_u, sg_v, sg_ln_g, sg_ln_b, sg_w, sg_b)
    p_c = (y_c * jax.nn.silu(sg_z)) @ w_br_c

    g = jax.nn.sigmoid(gates.reshape(b, s, N_BRANCH, d))
    merged = g[:, :, 0] * p_a + g[:, :, 1] * p_b + g[:, :, 2] * p_c
    sub = merged @ w_out + b_out
    return layer_norm(DEEPNORM_ALPHA * x + sub, ln_g, ln_b)

def first_inputs(seed: int = 0) -> dict:
    key = jax.random.key(seed)
    ks = jax.random.split(key, 20)
    L, D = DEPTH, D_MODEL

    def nrm(k, shape, scale):
        return jax.random.normal(k, shape, jnp.float32) * scale

    return {
        "x": nrm(ks[0], (BATCH, SEQ, D), 1.0),
        "ln_in_g": 1.0 + nrm(ks[1], (D,), 0.02),
        "ln_in_b": nrm(ks[2], (D,), 0.02),
        "w_in": nrm(ks[3], (L, D, IN_WIDTH), D ** -0.5),
        "b_in": nrm(ks[4], (L, IN_WIDTH), 0.02),
        "na_rpb": nrm(ks[5], (L, NA_HEADS, 2 * NA_KH_MAX - 1, 2 * NA_KW - 1), 0.1),
        "q_norm_g": 1.0 + nrm(ks[6], (L, HEAD_DIM), 0.02),
        "k_norm_g": 1.0 + nrm(ks[7], (L, HEAD_DIM), 0.02),
        "sg_ln_g": 1.0 + nrm(ks[8], (L, SG_WIDTH), 0.02),
        "sg_ln_b": nrm(ks[9], (L, SG_WIDTH), 0.02),
        "sg_w": nrm(ks[10], (L, SG_GROUPS, SG_CHUNK, SG_CHUNK), SG_CHUNK ** -0.5),
        "sg_b": 1.0 + nrm(ks[11], (L, SG_GROUPS, SG_CHUNK), 0.02),
        "w_br_a": nrm(ks[12], (L, NA_WIDTH, D), NA_WIDTH ** -0.5),
        "w_br_b": nrm(ks[13], (L, GQA_WIDTH, D), GQA_WIDTH ** -0.5),
        "w_br_c": nrm(ks[14], (L, SG_WIDTH, D), SG_WIDTH ** -0.5),
        "w_out": nrm(ks[15], (L, D, D), (D ** -0.5) * DEEPNORM_BETA),
        "b_out": nrm(ks[16], (L, D), 0.02),
        "ln_post_g": 1.0 + nrm(ks[17], (L, D), 0.02),
        "ln_post_b": nrm(ks[18], (L, D), 0.02),
    }

def first_block(x, ln_in_g, ln_in_b, w_in, b_in, na_rpb, q_norm_g, k_norm_g, sg_ln_g, sg_ln_b,
              sg_w, sg_b, w_br_a, w_br_b, w_br_c, w_out, b_out, ln_post_g, ln_post_b):
    s = x.shape[1]
    rope_cos, rope_sin = axial_rope_tables(s)
    h = layer_norm(x, ln_in_g, ln_in_b)
    for l in range(DEPTH):
        h = hybrid_layer(h, w_in[l], b_in[l], na_rpb[l], q_norm_g[l], k_norm_g[l],
                         sg_ln_g[l], sg_ln_b[l], sg_w[l], sg_b[l],
                         w_br_a[l], w_br_b[l], w_br_c[l], w_out[l], b_out[l],
                         ln_post_g[l], ln_post_b[l], rope_cos, rope_sin)
    return h


N_GROUPS = 4
GROUP = D_MODEL // N_GROUPS
CHUNK = 64

HGRN_HEADS = 4
GLA_HEADS = 4
GLA_KEY = GROUP // (2 * GLA_HEADS)
GLA_GATE_RANK = 16
GLA_GATE_NORM = 16.0
RWKV_HEADS = 4
RWKV_HEAD = GROUP // RWKV_HEADS
RWKV_DECAY_RANK = 64
RWKV_A_RANK = 64
RWKV_V_RANK = 32
RWKV_GATE_RANK = 160
RWKV_LNX_EPS = 64e-5
RET_HEADS = 4
RET_KEY = GROUP // RET_HEADS
ROPE_BASE = 10000.0

HGRN_COLS = (GROUP, GROUP, GROUP, GROUP)
GLA_COLS = (GLA_HEADS * GLA_KEY, GLA_HEADS * GLA_KEY, GROUP, GLA_GATE_RANK, GROUP)
RWKV_COLS = (GROUP, GROUP, GROUP, RWKV_DECAY_RANK, RWKV_A_RANK, RWKV_GATE_RANK)
RET_COLS = (GROUP, GROUP, GROUP, GROUP)
MIXER_COLS = (sum(HGRN_COLS), sum(GLA_COLS), sum(RWKV_COLS), sum(RET_COLS))
IN_COLS = sum(MIXER_COLS)

FFN_DENSE = 2816
N_EXPERTS = 8
TOP_K = 2
FFN_EXPERT = 1408
N_DENSE = (DEPTH + 1) // 2
N_MOE = DEPTH // 2

DN_ALPHA = (2.0 * DEPTH) ** 0.25
DN_BETA = (8.0 * DEPTH) ** -0.25
F32 = jnp.float32


def _split(p, sizes):
    return jnp.split(p, np.cumsum(sizes)[:-1].tolist(), axis=-1)

def _heads(t, n):
    return t.reshape(t.shape[:-1] + (n, t.shape[-1] // n))

def _merge(t):
    return t.reshape(t.shape[:-2] + (t.shape[-2] * t.shape[-1],))

def _layer_norm(x, g, b):
    x = x.astype(F32)
    mu = jnp.mean(x, -1, keepdims=True)
    var = jnp.mean(jnp.square(x - mu), -1, keepdims=True)
    return (x - mu) * lax.rsqrt(var + LN_EPS) * g + b

def _rms_norm(x, g, eps=1e-6):
    return x * lax.rsqrt(jnp.mean(jnp.square(x), -1, keepdims=True) + eps) * g

def _group_norm(x, eps):
    mu = jnp.mean(x, -1, keepdims=True)
    var = jnp.mean(jnp.square(x - mu), -1, keepdims=True)
    return (x - mu) * lax.rsqrt(var + eps)

def _to_chunks(t):
    b, s, h, d = t.shape
    return t.reshape(b, s // CHUNK, CHUNK, h, d).transpose(1, 0, 3, 2, 4)

def _from_chunks(t):
    n, b, h, c, d = t.shape
    return t.transpose(1, 0, 3, 2, 4).reshape(b, n * c, h, d)

def _chunked_gated_linear(q, k, v, log_f):
    b, _, h, kd = q.shape
    vd = v.shape[-1]
    qc, kc, vc, gc = (_to_chunks(t.astype(F32)) for t in (q, k, v, log_f))
    causal = jnp.tril(jnp.ones((CHUNK, CHUNK), dtype=bool))

    def step(state, inp):
        qi, ki, vi, gi = inp
        cum = jnp.cumsum(gi, axis=2)
        diff = cum[:, :, :, None, :] - cum[:, :, None, :, :]
        decay = jnp.exp(jnp.where(causal[:, :, None], diff, -jnp.inf))
        scores = jnp.einsum('bhik,bhjk,bhijk->bhij', qi, ki, decay)
        out = (jnp.einsum('bhij,bhjv->bhiv', scores, vi)
               + jnp.einsum('bhik,bhkv->bhiv', qi * jnp.exp(cum), state))
        cum_end = cum[:, :, -1:, :]
        state = (jnp.exp(cum_end[:, :, 0, :])[..., None] * state
                 + jnp.einsum('bhjk,bhjv->bhkv', ki * jnp.exp(cum_end - cum), vi))
        return state, out

    _, o = lax.scan(step, jnp.zeros((b, h, kd, vd), F32), (qc, kc, vc, gc))
    return _from_chunks(o)

def _retention_chunkwise(q, k, v, log_gamma):
    b, _, h, kd = q.shape
    vd = v.shape[-1]
    qc, kc, vc = (_to_chunks(t.astype(F32)) for t in (q, k, v))
    idx = jnp.arange(CHUNK, dtype=F32)
    rel = idx[:, None] - idx[None, :]
    intra = jnp.exp(jnp.where(rel >= 0, rel * log_gamma[:, None, None], -jnp.inf))
    q_dec = jnp.exp((idx + 1.0)[None, :] * log_gamma[:, None])
    k_dec = jnp.exp((CHUNK - 1.0 - idx)[None, :] * log_gamma[:, None])
    c_dec = jnp.exp(CHUNK * log_gamma)

    def step(state, inp):
        qi, ki, vi = inp
        scores = jnp.einsum('bhik,bhjk->bhij', qi, ki) * intra
        out = (jnp.einsum('bhij,bhjv->bhiv', scores, vi)
               + jnp.einsum('bhik,bhkv->bhiv', qi * q_dec[..., None], state))
        state = (c_dec[:, None, None] * state
                 + jnp.einsum('bhjk,bhjv->bhkv', ki * k_dec[..., None], vi))
        return state, out

    _, o = lax.scan(step, jnp.zeros((b, h, kd, vd), F32), (qc, kc, vc))
    return _from_chunks(o)

def _rotary(t, positions):
    half = t.shape[-1] // 2
    inv_freq = ROPE_BASE ** (-jnp.arange(half, dtype=F32) / half)
    ang = positions.astype(F32)[:, :, None, None] * inv_freq
    cos, sin = jnp.cos(ang), jnp.sin(ang)
    t1, t2 = t[..., :half], t[..., half:]
    return jnp.concatenate([t1 * cos - t2 * sin, t1 * sin + t2 * cos], axis=-1)

def _rwkv7_scan(r, w, k, v, kk, a):
    b, _, h, n = r.shape
    xs = tuple(jnp.moveaxis(t, 1, 0) for t in (r, w, k, v, kk, a))

    def step(state, inp):
        rt, wt, kt, vt, kkt, at = inp
        sa = jnp.einsum('bhvk,bhk->bhv', state, -kkt)
        state = (state * wt[:, :, None, :]
                 + sa[..., None] * (kkt * at)[:, :, None, :]
                 + vt[..., None] * kt[:, :, None, :])
        return state, jnp.einsum('bhvk,bhk->bhv', state, rt)

    _, o = lax.scan(step, jnp.zeros((b, h, n, n), F32), xs)
    return jnp.moveaxis(o, 0, 1)

def _hgrn2_mixer(p, lb, norm_g):
    q_raw, f_raw, i_raw, g_raw = _split(p, HGRN_COLS)
    f = lb + (1.0 - lb) * jax.nn.sigmoid(f_raw)
    hd = lambda t: _heads(t, HGRN_HEADS)
    o = _chunked_gated_linear(hd(jax.nn.silu(q_raw)), hd(1.0 - f), hd(i_raw), hd(jnp.log(f)))
    o = _rms_norm(o, norm_g) * jax.nn.silu(hd(g_raw))
    return _merge(o)

def _gla_mixer(p, gate_w2, gate_b, norm_g):
    q, k, v, g_lr, r = _split(p, GLA_COLS)
    log_f = jax.nn.log_sigmoid(g_lr @ gate_w2 + gate_b) / GLA_GATE_NORM
    hd = lambda t: _heads(t, GLA_HEADS)
    o = _chunked_gated_linear(hd(q) * GLA_KEY ** -0.5, hd(k), hd(v), hd(log_f))
    o = _rms_norm(o, norm_g) * jax.nn.silu(hd(r))
    return _merge(o)

def _rwkv7_mixer(p, v_first, v_mix, mu, w0, w2, a0, a2, g2, k_k, k_a, r_k, lnx_g, lnx_b):
    p_prev = jnp.pad(p, ((0, 0), (1, 0), (0, 0)))[:, :-1]
    p = p + (p_prev - p) * mu
    r, k, v, w_lr, a_lr, g_lr = _split(p, RWKV_COLS)
    w = -jax.nn.softplus(-(w0 + jnp.tanh(w_lr) @ w2)) - 0.5
    decay = jnp.exp(-jnp.exp(w))
    a = jax.nn.sigmoid(a0 + a_lr @ a2)
    g = jax.nn.sigmoid(g_lr) @ g2
    if v_mix is None:
        v_first = v
    else:
        v0, v1, v2 = v_mix
        v = v + (v_first - v) * jax.nn.sigmoid(v0 + (v @ v1) @ v2)
    hd = lambda t: _heads(t, RWKV_HEADS)
    kk = hd(k * k_k)
    kk = kk / jnp.maximum(jnp.sqrt(jnp.sum(jnp.square(kk), -1, keepdims=True)), 1e-12)
    k = k * (1.0 + (a - 1.0) * k_a)
    rh, kh, vh = hd(r), hd(k), hd(v)
    o = _rwkv7_scan(rh, hd(decay), kh, vh, kk, hd(a))
    o = _group_norm(o, RWKV_LNX_EPS) * hd(lnx_g) + hd(lnx_b)
    o = o + jnp.sum(rh * kh * r_k, -1, keepdims=True) * vh
    return _merge(o) * g, v_first

def _retnet_mixer(p, positions, log_gamma):
    q, k, v, g = _split(p, RET_COLS)
    hd = lambda t: _heads(t, RET_HEADS)
    qh = _rotary(hd(q), positions)
    kh = _rotary(hd(k), positions) * RET_KEY ** -0.5
    o = _group_norm(_retention_chunkwise(qh, kh, hd(v), log_gamma), LN_EPS)
    return jax.nn.silu(g) * _merge(o)

def _swiglu(h, wg, wu, wd):
    return (jax.nn.silu(h @ wg) * (h @ wu)) @ wd

def _moe(h, router, wg, wu, wd):
    b, s, d = h.shape
    hf = h.reshape(b * s, d)
    probs = jax.nn.softmax((hf @ router).astype(F32), axis=-1)
    top_p, top_i = lax.top_k(probs, TOP_K)
    top_p = top_p / jnp.sum(top_p, -1, keepdims=True)
    gates = jnp.sum(jax.nn.one_hot(top_i, N_EXPERTS, dtype=F32) * top_p[..., None], axis=1)
    out = jnp.zeros_like(hf)
    for e in range(N_EXPERTS):
        out = out + gates[:, e:e + 1] * _swiglu(hf, wg[e], wu[e], wd[e])
    return out.reshape(b, s, d)

def second_inputs(seed: int = 0) -> dict:
    key = jax.random.key(seed)
    ks = iter(jax.random.split(key, 48))

    def nrm(shape, scale):
        return scale * jax.random.normal(next(ks), shape, F32)

    D = D_MODEL
    decay_base = -6.0 + 5.0 * (jnp.arange(GROUP, dtype=F32) / (GROUP - 1)) ** 0.9
    return {
        'x': nrm((BATCH, SEQ, D), 1.0),
        'positions': jnp.broadcast_to(jnp.arange(SEQ, dtype=jnp.int32)[None, :], (BATCH, SEQ)),
        'w_in': nrm((DEPTH, D, IN_COLS), D ** -0.5),
        'w_out': nrm((DEPTH, D, D), DN_BETA * D ** -0.5),
        'ln1_g': 1.0 + nrm((DEPTH, D), 0.01),
        'ln1_b': nrm((DEPTH, D), 0.01),
        'ln2_g': 1.0 + nrm((DEPTH, D), 0.01),
        'ln2_b': nrm((DEPTH, D), 0.01),
        'hgrn_lb_logits': nrm((DEPTH, GROUP), 0.5),
        'hgrn_norm_g': 1.0 + nrm((DEPTH, GROUP // HGRN_HEADS), 0.01),
        'gla_gate_w2': nrm((DEPTH, GLA_GATE_RANK, GLA_HEADS * GLA_KEY), GLA_GATE_RANK ** -0.5),
        'gla_gate_b': nrm((DEPTH, GLA_HEADS * GLA_KEY), 0.1),
        'gla_norm_g': 1.0 + nrm((DEPTH, GROUP // GLA_HEADS), 0.01),
        'rwkv_mu': jax.random.uniform(next(ks), (DEPTH, sum(RWKV_COLS)), F32),
        'rwkv_w0': decay_base[None, :] + nrm((DEPTH, GROUP), 0.1),
        'rwkv_w2': nrm((DEPTH, RWKV_DECAY_RANK, GROUP), 0.5 * RWKV_DECAY_RANK ** -0.5),
        'rwkv_a0': nrm((DEPTH, GROUP), 0.1),
        'rwkv_a2': nrm((DEPTH, RWKV_A_RANK, GROUP), 0.5 * RWKV_A_RANK ** -0.5),
        'rwkv_g2': nrm((DEPTH, RWKV_GATE_RANK, GROUP), RWKV_GATE_RANK ** -0.5),
        'rwkv_k_k': 0.85 + nrm((DEPTH, GROUP), 0.02),
        'rwkv_k_a': 1.0 + nrm((DEPTH, GROUP), 0.02),
        'rwkv_r_k': -0.04 + nrm((DEPTH, RWKV_HEADS, RWKV_HEAD), 0.02),
        'rwkv_lnx_g': 1.0 + nrm((DEPTH, GROUP), 0.01),
        'rwkv_lnx_b': nrm((DEPTH, GROUP), 0.01),
        'rwkv_v0': 1.0 + nrm((DEPTH - 1, GROUP), 0.1),
        'rwkv_v1': nrm((DEPTH - 1, GROUP, RWKV_V_RANK), GROUP ** -0.5),
        'rwkv_v2': nrm((DEPTH - 1, RWKV_V_RANK, GROUP), 0.5 * RWKV_V_RANK ** -0.5),
        'ffn_w_gate': nrm((N_DENSE, D, FFN_DENSE), D ** -0.5),
        'ffn_w_up': nrm((N_DENSE, D, FFN_DENSE), D ** -0.5),
        'ffn_w_down': nrm((N_DENSE, FFN_DENSE, D), DN_BETA * FFN_DENSE ** -0.5),
        'moe_router': nrm((N_MOE, D, N_EXPERTS), D ** -0.5),
        'moe_w_gate': nrm((N_MOE, N_EXPERTS, D, FFN_EXPERT), D ** -0.5),
        'moe_w_up': nrm((N_MOE, N_EXPERTS, D, FFN_EXPERT), D ** -0.5),
        'moe_w_down': nrm((N_MOE, N_EXPERTS, FFN_EXPERT, D), DN_BETA * FFN_EXPERT ** -0.5),
    }

def second_block(x, positions, w_in, w_out, ln1_g, ln1_b, ln2_g, ln2_b, hgrn_lb_logits, hgrn_norm_g,
              gla_gate_w2, gla_gate_b, gla_norm_g, rwkv_mu, rwkv_w0, rwkv_w2, rwkv_a0, rwkv_a2,
              rwkv_g2, rwkv_k_k, rwkv_k_a, rwkv_r_k, rwkv_lnx_g, rwkv_lnx_b, rwkv_v0, rwkv_v1,
              rwkv_v2, ffn_w_gate, ffn_w_up, ffn_w_down, moe_router, moe_w_gate, moe_w_up,
              moe_w_down):
    out_dtype = x.dtype
    h = x.astype(F32)
    lb_all = jnp.cumsum(jax.nn.softmax(hgrn_lb_logits.astype(F32), axis=0), axis=0)
    lb_all = lb_all - lb_all[:1]
    log_gamma = jnp.log(1.0 - 2.0 ** (-5.0 - jnp.arange(RET_HEADS, dtype=F32)))
    v_first = None
    for l in range(DEPTH):
        p = jnp.einsum('btd,dc->btc', h, w_in[l]).astype(F32)
        pa, pb, pc, pd = _split(p, MIXER_COLS)
        ya = _hgrn2_mixer(pa, lb_all[l], hgrn_norm_g[l])
        yb = _gla_mixer(pb, gla_gate_w2[l], gla_gate_b[l], gla_norm_g[l])
        v_mix = None if l == 0 else (rwkv_v0[l - 1], rwkv_v1[l - 1], rwkv_v2[l - 1])
        yc, v_first = _rwkv7_mixer(pc, v_first, v_mix, rwkv_mu[l], rwkv_w0[l], rwkv_w2[l],
                                   rwkv_a0[l], rwkv_a2[l], rwkv_g2[l], rwkv_k_k[l], rwkv_k_a[l],
                                   rwkv_r_k[l], rwkv_lnx_g[l], rwkv_lnx_b[l])
        yd = _retnet_mixer(pd, positions, log_gamma)
        mix = jnp.einsum('btc,cd->btd', jnp.concatenate([ya, yb, yc, yd], axis=-1), w_out[l])
        h = _layer_norm(DN_ALPHA * h + mix, ln1_g[l], ln1_b[l])
        if l % 2 == 0:
            i = l // 2
            f = _swiglu(h, ffn_w_gate[i], ffn_w_up[i], ffn_w_down[i])
        else:
            i = l // 2
            f = _moe(h, moe_router[i], moe_w_gate[i], moe_w_up[i], moe_w_down[i])
        h = _layer_norm(DN_ALPHA * h + f, ln2_g[l], ln2_b[l])
    return h.astype(out_dtype)


def setup_inputs(seed=0):
    out = dict(first_inputs(seed))
    for name, value in second_inputs(seed + 1).items():
        if name != "x":
            out[name + "_2"] = value
    return out


def reference(
    x, ln_in_g, ln_in_b, w_in, b_in, na_rpb, q_norm_g, k_norm_g, sg_ln_g, sg_ln_b, sg_w, sg_b,
    w_br_a, w_br_b, w_br_c, w_out, b_out, ln_post_g, ln_post_b, positions_2, w_in_2, w_out_2,
    ln1_g_2, ln1_b_2, ln2_g_2, ln2_b_2, hgrn_lb_logits_2, hgrn_norm_g_2, gla_gate_w2_2,
    gla_gate_b_2, gla_norm_g_2, rwkv_mu_2, rwkv_w0_2, rwkv_w2_2, rwkv_a0_2, rwkv_a2_2,
    rwkv_g2_2, rwkv_k_k_2, rwkv_k_a_2, rwkv_r_k_2, rwkv_lnx_g_2, rwkv_lnx_b_2, rwkv_v0_2,
    rwkv_v1_2, rwkv_v2_2, ffn_w_gate_2, ffn_w_up_2, ffn_w_down_2, moe_router_2, moe_w_gate_2,
    moe_w_up_2, moe_w_down_2,
):
    x = first_block(
        x, ln_in_g, ln_in_b, w_in, b_in, na_rpb, q_norm_g, k_norm_g, sg_ln_g, sg_ln_b, sg_w,
        sg_b, w_br_a, w_br_b, w_br_c, w_out, b_out, ln_post_g, ln_post_b,
    )
    return second_block(
        x, positions_2, w_in_2, w_out_2, ln1_g_2, ln1_b_2, ln2_g_2, ln2_b_2, hgrn_lb_logits_2,
        hgrn_norm_g_2, gla_gate_w2_2, gla_gate_b_2, gla_norm_g_2, rwkv_mu_2, rwkv_w0_2,
        rwkv_w2_2, rwkv_a0_2, rwkv_a2_2, rwkv_g2_2, rwkv_k_k_2, rwkv_k_a_2, rwkv_r_k_2,
        rwkv_lnx_g_2, rwkv_lnx_b_2, rwkv_v0_2, rwkv_v1_2, rwkv_v2_2, ffn_w_gate_2, ffn_w_up_2,
        ffn_w_down_2, moe_router_2, moe_w_gate_2, moe_w_up_2, moe_w_down_2,
    )


_drawn_inputs = setup_inputs


def setup_inputs(seed=0):
    import zlib

    import numpy as np

    out = dict(_drawn_inputs(seed))
    spreads = {}
    factors = {'b_in': 4.33,
     'na_rpb': 8.0,
     'q_norm_g': 8.0,
     'k_norm_g': 8.0,
     'sg_ln_g': 8.0,
     'sg_ln_b': 8.0,
     'sg_b': 8.0,
     'w_br_b': 2.959,
     'ln1_g_2': 3.01,
     'ln1_b_2': 3.04,
     'ln2_g_2': 3.436,
     'ln2_b_2': 3.371,
     'hgrn_lb_logits_2': 4.635,
     'hgrn_norm_g_2': 8.0,
     'gla_gate_w2_2': 3.397,
     'gla_gate_b_2': 6.887,
     'gla_norm_g_2': 8.0,
     'rwkv_w2_2': 7.446,
     'rwkv_a0_2': 6.412,
     'rwkv_k_k_2': 8.0,
     'rwkv_k_a_2': 8.0,
     'rwkv_r_k_2': 8.0,
     'rwkv_lnx_g_2': 8.0,
     'rwkv_lnx_b_2': 8.0,
     'rwkv_v0_2': 8.0,
     'rwkv_v1_2': 3.709,
     'rwkv_v2_2': 3.435}
    for name, (base, spread) in spreads.items():
        noise = np.random.default_rng([zlib.crc32(name.encode()), seed]).standard_normal(out[name].shape)
        drawn = base * np.exp(spread * noise) if base else spread * noise
        out[name] = jnp.asarray(drawn.astype(out[name].dtype))
    for name, factor in factors.items():
        out[name] = (out[name] * factor).astype(out[name].dtype)
    return out
```

```python
from contextlib import ExitStack

import numpy as np

import concourse.bass as bass
from concourse import mybir

P = 128
F32 = mybir.dt.float32
I32 = mybir.dt.int32
ALU = mybir.AluOpType
ACT = mybir.ActivationFunctionType
AX = mybir.AxisListType

SEQ, D = 512, 1024
TT = SEQ // P
KT = D // P
DEPTH = 2
HD = 64
ALPHA = (2.0 * DEPTH) ** 0.25
LN_EPS = 1e-5
RMS_EPS = 1e-6
SLOT = 4 * D
RING = 3

NA_Q, NA_K, NA_V, NA_Z, GQ_Q, GQ_KV, GQ_Z = 0, 512, 1024, 1536, 2048, 2560, 2816
SG_U, SG_V, SG_Z, GATES, IN_WIDTH = 3328, 3840, 4352, 4864, 7936
GRID_W, NA_KW, HEADS = 64, 16, 8

TABLES = {}


def make_tables():
    parts, at = [], 0

    def put(name, a):
        nonlocal at
        a = np.asarray(a, np.float32).reshape(P, -1)
        TABLES[name] = (at, a.shape[1])
        parts.append(a)
        at += a.shape[1]

    i = np.arange(P)
    put("ident", np.eye(P))
    tok = np.arange(SEQ)
    freqs = (np.float32(10000.0) ** (-np.arange(0, 32, 2, dtype=np.float32) / np.float32(32))).astype(np.float32)
    ang = np.concatenate([(tok // GRID_W).astype(np.float32)[:, None] * freqs,
                          (tok % GRID_W).astype(np.float32)[:, None] * freqs], -1).astype(np.float32)
    for name, f in (("rope_cos", np.cos), ("rope_sin", np.sin)):
        put(name, f(ang).astype(np.float32).reshape(TT, P, 32).transpose(1, 0, 2))
    c = np.arange(GRID_W)
    start = np.clip(c - NA_KW // 2, 0, GRID_W - NA_KW)
    ok = (c[None] >= start[:, None]) & (c[None] < start[:, None] + NA_KW)
    put("window", np.tile(np.where(ok, 0.0, -1e30), (2, 1)))
    put("halves", (i[:, None] // HD == i[None] // HD))
    put("quarters", i[:, None] // 32 == np.arange(256)[None] // HD)
    same = i[:, None] // HD == i[None] // HD
    put("before", same & (i[:, None] < i[None]))
    put("upto", same & (i[:, None] <= i[None]))
    lv = [(i[:, None] // (2 * s) == i[None] // (2 * s)) & (i[:, None] // s % 2 == 0) & (i[None] // s % 2 == 1)
          for s in (1, 2, 4, 8, 16, 32)]
    put("levels", np.stack(lv, 1))
    put("keep", np.tile((tok % HD != 0)[None], (P, 1)))
    inv = (np.float32(10000.0) ** (-np.arange(32, dtype=np.float32) / np.float32(32))).astype(np.float32)
    put("inv_freq", np.tile(inv[None], (P, 1)))
    return np.concatenate(parts, 1)


def make_decay_table():
    gamma = np.log(1.0 - 2.0 ** (-5.0 - np.arange(4, dtype=np.float64)))
    rel = np.arange(SEQ)[None] - np.arange(P)[:, None]
    d = np.where(rel[:, None, :] >= 0, np.exp(np.maximum(rel, 0)[:, None, :] * gamma[None, :, None]), 0.0)
    return d.astype(np.float32)


class Step:

    def __init__(self, eng, sem):
        self.eng, self.sem, self.n = eng, sem, 0

    def __call__(self, ins):
        self.n += 1
        ins.then_inc(self.sem, 1)
        self.eng.wait_ge(self.sem, self.n)


class Machine:

    def __init__(self, nc, ctx, tables):
        self.nc, self.ctx, self.tables = nc, ctx, tables
        self.sets = [[ctx.enter_context(nc.semaphore(f"set{k}_{i}")) for i in range(28)] for k in range(2)]
        self.turn = 0
        self.slot_landed = [ctx.enter_context(nc.semaphore(f"slot_landed{i}")) for i in range(RING)]
        self.slots_used = ctx.enter_context(nc.semaphore("slots_used"))
        self.out_stored = ctx.enter_context(nc.semaphore("out_stored"))
        sb = self.sbuf
        self.ps = ctx.enter_context(nc.psum_tensor("ps", [P, 8, 512], F32))
        self.ident = sb(ctx, "ident", [P, P])
        self.h = sb(ctx, "h", [P, TT, D])
        self.hT = sb(ctx, "hT", [P, KT, SEQ])
        self.mixT = sb(ctx, "mixT", [P, KT, SEQ])
        self.ring = sb(ctx, "ring", [P, RING, SLOT])
        self.plan, self.fed, self.taken, self.released_to = [], 0, 0, 0

    def sbuf(self, ctx, name, shape, dt=F32):
        return ctx.enter_context(self.nc.sbuf_tensor(f"{name}_{self.nc.next_id()}", shape, dt))

    def stage(self):
        self.turn ^= 1
        return self.sets[self.turn]

    def clear_previous(self, sp):
        nums = [s.num for s in self.sets[self.turn ^ 1]]
        sp.sem_clear(range(min(nums), max(nums) + 1))

    def table(self, name):
        at, n = TABLES[name]
        return self.tables[:, at:at + n]

    def feed(self, sp, n_taken):
        self.released_to += n_taken
        end = min(len(self.plan), self.released_to + RING)
        while self.fed < end:
            n = self.fed
            if n >= RING:
                sp.wait_ge(self.slots_used, n - RING + 1)
            for src, lo, size, shape in self.plan[n]:
                dst = self.ring[:, n % RING, lo:lo + size].rearrange("p (k c) -> p k c", k=shape)
                sp.dma_start(dst, src).then_inc(self.slot_landed[n % RING], 16)
            self.fed += 1

    def take(self, pe, k):
        n = self.taken
        self.taken += 1
        landed = sum(len(self.plan[m]) for m in range(n % RING, n + 1, RING))
        pe.wait_ge(self.slot_landed[n % RING], 16 * landed)
        size = sum(c[2] for c in self.plan[n])
        return self.ring[:, n % RING, 0:size].rearrange("p (k c) -> p k c", k=k)

    def end_plan(self):
        assert self.fed == self.taken == len(self.plan) == self.released_to
        self.plan, self.fed, self.taken, self.released_to = [], 0, 0, 0


def rows_chunk(w, cols, k=KT):
    lo, hi = cols
    return [(w.rearrange("(k p) c -> p k c", p=P)[:, :, lo:hi], 0, k * (hi - lo), k)]


def project_T(m, pe, w, rhs, k, ntiles, banks, first, ready, kept, last_cols=P):
    for i in range(ntiles):
        n = first + i
        if n >= len(banks):
            pe.wait_ge(kept, n - len(banks) + 1)
        cols = P if i < ntiles - 1 else last_cols
        for j in range(k):
            mm = pe.matmul(m.ps[0:cols, banks[n % len(banks)], :], w[:, j, i * P:i * P + cols], rhs[:, j, :],
                           start=(j == 0), stop=(j == k - 1))
        mm.then_inc(ready, 1)
    return mm


def project_tok(m, pe, w, lhs, cols, banks, first, ready, kept):
    lo, hi = cols
    for tt in range(TT):
        n = first + tt
        if n >= len(banks):
            pe.wait_ge(kept, n - len(banks) + 1)
        for j in range(KT):
            mm = pe.matmul(m.ps[:, banks[n % len(banks)], 0:hi - lo], lhs[:, j, tt * P:(tt + 1) * P], w[:, j, lo:hi],
                           start=(j == 0), stop=(j == KT - 1))
        mm.then_inc(ready, 1)
    return mm


def spread(ap, n=P):
    return ap.partition_broadcast(n)


def backwards(ap):
    *outer, (step, n) = [list(x) for x in ap.ap]
    return bass.AP(ap.tensor, ap.offset + step * (n - 1), outer + [[-step, n]])


def layer(ap, l):
    if isinstance(l, int):
        return ap[l]
    names = "bcdef"[:len(ap.shape) - 1]
    return ap[bass.ds(l, 1)].rearrange(f"a {' '.join(names)} -> (a {names[0]}) {' '.join(names[1:])}")


def columns_stage(m, rows_ap, n, out):
    nc = m.nc
    loaded, turned, *_ = m.stage()
    with ExitStack() as ctx:
        rows = m.sbuf(ctx, "rows", [n, P])
        with nc.Block() as block:
            @block.sync
            def _(sp):
                m.clear_previous(sp)
                for (r0, r1, src) in rows_ap:
                    sp.dma_start(rows[r0:r1, :], src).then_inc(loaded, 16)

            @block.tensor
            def _(pe):
                pe.wait_ge(loaded, 16 * len(rows_ap))
                pe.transpose(m.ps[:, 0, 0:n], rows[:, :], m.ident[0:n, 0:n]).then_inc(turned, 1)

            @block.vector
            def _(dve):
                dve.wait_ge(turned, 1)
                dve.tensor_copy(out, m.ps[:, 0, 0:n])


def norm_stage(m, gain, shift, feed=0, store=None, add_from=None):
    nc = m.nc
    loaded, step, var_ready, rstd_ready, normed, turned, half_ready, *_ = m.stage()
    with ExitStack() as ctx:
        g = m.sbuf(ctx, "g", [P, D])
        b = m.sbuf(ctx, "b", [P, D])
        stats = m.sbuf(ctx, "stats", [P, TT, 2, 6])
        mv = m.sbuf(ctx, "mv", [P, TT, 2])
        rstd = m.sbuf(ctx, "rstd", [P, TT])
        half = m.sbuf(ctx, "half", [P, TT])
        with nc.Block() as block:
            @block.sync
            def _(sp):
                m.clear_previous(sp)
                sp.dma_start(g[:], spread(gain)).then_inc(loaded, 16)
                sp.dma_start(b[:], spread(shift)).then_inc(loaded, 16)
                m.feed(sp, feed)
                if store is not None:
                    for tt in range(TT):
                        sp.wait_ge(normed, tt + 1)
                        sp.dma_start(store[tt * P:(tt + 1) * P, :], m.h[:, tt, :]).then_inc(m.out_stored, 16)
                    sp.wait_ge(m.out_stored, 16 * TT)

            @block.gpsimd
            def _(pool):
                nc.gpsimd.memset(half[:], -0.5).then_inc(half_ready, 1)
                pool.wait_ge(half_ready, 1)
                pool.wait_ge(var_ready, 1)
                nc.gpsimd.tensor_tensor(rstd[:], mv[:, :, 1], half[:], ALU.pow).then_inc(rstd_ready, 1)

            @block.vector
            def _(dve):
                do = Step(dve, step)
                for tt in range(TT):
                    for q in range(2):
                        do(dve.bn_stats(stats[:, tt, q, :], m.h[:, tt, q * 512:(q + 1) * 512]))
                    do(dve.bn_aggr(mv[:, tt, :], stats[:, tt, :, :]))
                dve.tensor_scalar(mv[:, :, 1], mv[:, :, 1], LN_EPS, None, ALU.add).then_inc(var_ready, 1)
                dve.wait_ge(rstd_ready, 1)
                dve.wait_ge(loaded, 32)
                for tt in range(TT):
                    do(dve.tensor_scalar(m.h[:, tt, :], m.h[:, tt, :], mv[:, tt, 0:1], rstd[:, tt:tt + 1],
                                         ALU.subtract, ALU.mult))
                    do(dve.tensor_tensor(m.h[:, tt, :], m.h[:, tt, :], g[:], ALU.mult))
                    dve.tensor_tensor(m.h[:, tt, :], m.h[:, tt, :], b[:], ALU.add).then_inc(normed, 1)

            if store is None:
                @block.tensor
                def _(pe):
                    for tt in range(TT):
                        pe.wait_ge(normed, tt + 1)
                        for q in range(2):
                            for j in range(4):
                                mm = pe.transpose(m.ps[:, 2 * tt + q, j * P:(j + 1) * P],
                                                  m.h[:, tt, (4 * q + j) * P:(4 * q + j + 1) * P], m.ident[:])
                            mm.then_inc(turned, 1)

                @block.scalar
                def _(act):
                    for n in range(2 * TT):
                        tt, q = n // 2, n % 2
                        act.wait_ge(turned, n + 1)
                        act.copy(m.hT[:, 4 * q:4 * q + 4, tt * P:(tt + 1) * P],
                                 m.ps[:, n, :].rearrange("p (j t) -> p j t", j=4))


def attention_stage(m, qT, kT, place, v, v_col, zT, yT, bias, scale, feed=0):
    nc = m.nc
    (scores_ready, scores_read, max_ready, probs_ready, probs_turned, probs_kept, pv_ready, y_ready,
     y_turned, y_kept, step, *_) = m.stage()
    NH = HEADS * TT
    with ExitStack() as ctx:
        s_sum = m.sbuf(ctx, "s_sum", [P, 2, SEQ])
        probs = m.sbuf(ctx, "probs", [P, 2, SEQ])
        probsT = m.sbuf(ctx, "probsT", [P, 2, SEQ])
        y = m.sbuf(ctx, "y", [P, SEQ])
        rowmax = m.sbuf(ctx, "rowmax", [P, 2])
        negmax = m.sbuf(ctx, "negmax", [P, 2])
        total = m.sbuf(ctx, "total", [P, 2, HEADS])
        inv = m.sbuf(ctx, "inv", [P, HEADS])

        S = lambda n: m.ps[:, n % 2, :]
        PT = lambda n: m.ps[:, 2 + n % 2, :]
        Y = lambda qt: m.ps[:, 4 + qt % 2, :]
        YT = m.ps[:, 6, :]
        with nc.Block() as block:
            @block.sync
            def _(sp):
                m.clear_previous(sp)
                m.feed(sp, feed)

            @block.tensor
            def _(pe):
                for i in range(NH + 3):
                    if i < NH:
                        qt, hd = divmod(i, HEADS)
                        tq, tk, at = place(hd)
                        if i >= 2:
                            pe.wait_ge(scores_read, i - 1)
                        pe.matmul(S(i), qT[at:at + HD, tq, qt * P:(qt + 1) * P], kT[at:at + HD, tk, :],
                                  start=True, stop=True).then_inc(scores_ready, 1)
                    if 1 <= i <= NH:
                        n = i - 1
                        pe.wait_ge(probs_ready, n + 1)
                        if n >= 2:
                            pe.wait_ge(probs_kept, n - 1)
                        for j in range(TT):
                            mm = pe.transpose(PT(n)[:, j * P:(j + 1) * P], probs[:, n % 2, j * P:(j + 1) * P],
                                              m.ident[:])
                        mm.then_inc(probs_turned, 1)
                    if 2 <= i <= NH + 1:
                        n = i - 2
                        qt, hd = divmod(n, HEADS)
                        pe.wait_ge(probs_kept, n + 1)
                        if hd == 0 and qt >= 2:
                            pe.wait_ge(y_ready, qt - 1)
                        for j in range(TT):
                            mm = pe.matmul(Y(qt)[:, hd * HD:(hd + 1) * HD], probsT[:, n % 2, j * P:(j + 1) * P],
                                           v[:, j, v_col(hd):v_col(hd) + HD], start=(j == 0), stop=(j == TT - 1))
                        mm.then_inc(pv_ready, 1)
                    if i >= 3 and (i - 3) % HEADS == HEADS - 1:
                        qt = (i - 3) // HEADS
                        pe.wait_ge(y_ready, qt + 1)
                        if qt >= 1:
                            pe.wait_ge(y_kept, qt)
                        for j in range(4):
                            mm = pe.transpose(YT[:, j * P:(j + 1) * P], y[:, j * P:(j + 1) * P], m.ident[:])
                        mm.then_inc(y_turned, 1)

            @block.scalar
            def _(act):
                for n in range(NH):
                    qt, hd = divmod(n, HEADS)
                    act.wait_ge(max_ready, n + 1)
                    if n >= 2:
                        act.wait_ge(probs_turned, n - 1)
                    if hd == 0 and qt >= 2:
                        act.wait_ge(y_ready, qt - 1)
                    src = S(n) if bias is None else s_sum[:, n % 2, :]
                    act.activation(probs[:, n % 2, :], src, ACT.Exp, bias=negmax[:, n % 2:n % 2 + 1],
                                   scale=scale, accum_out=total[:, qt % 2, hd:hd + 1]).then_inc(probs_ready, 1)
                    if bias is None:
                        act.wait_ge(probs_ready, n + 1)
                        act.sem_inc(scores_read, 1)

            @block.vector
            def _(dve):
                do = Step(dve, step)
                for i in range(NH + 3):
                    if i < NH:
                        n = i
                        qt, hd = divmod(n, HEADS)
                        dve.wait_ge(scores_ready, n + 1)
                        if n >= 2:
                            dve.wait_ge(probs_ready, n - 1)
                        if bias is None:
                            do(dve.reduce_max(rowmax[:, n % 2:n % 2 + 1], S(n), AX.X))
                        else:
                            dve.tensor_tensor_reduce(
                                out=s_sum[:, n % 2, :], in0=S(n), in1=bias(qt, hd), scale=1.0, scalar=-3e38,
                                op0=ALU.add, op1=ALU.max, accum_out=rowmax[:, n % 2:n % 2 + 1]
                            ).then_inc(scores_read, 1)
                            dve.wait_ge(scores_read, n + 1)
                        dve.tensor_scalar(negmax[:, n % 2:n % 2 + 1], rowmax[:, n % 2:n % 2 + 1], -scale, None,
                                          ALU.mult).then_inc(max_ready, 1)
                    if 1 <= i <= NH:
                        n = i - 1
                        dve.wait_ge(probs_turned, n + 1)
                        if n >= 2:
                            dve.wait_ge(pv_ready, n - 1)
                        dve.tensor_copy(probsT[:, n % 2, :], PT(n)).then_inc(probs_kept, 1)
                    if i >= 2 and (i - 2) % HEADS == HEADS - 1:
                        qt = (i - 2) // HEADS
                        dve.wait_ge(probs_ready, (qt + 1) * HEADS)
                        do(dve.reciprocal(inv[:], total[:, qt % 2, :]))
                        dve.wait_ge(pv_ready, (qt + 1) * HEADS)
                        if qt >= 1:
                            dve.wait_ge(y_turned, qt)
                        dve.tensor_tensor(y[:].rearrange("p (h d) -> p h d", h=HEADS),
                                          Y(qt).rearrange("p (h d) -> p h d", h=HEADS),
                                          inv[:].unsqueeze(2).to_broadcast([P, HEADS, HD]),
                                          ALU.mult).then_inc(y_ready, 1)
                    if i >= 3 and (i - 3) % HEADS == HEADS - 1:
                        qt = (i - 3) // HEADS
                        dve.wait_ge(y_turned, qt + 1)
                        dve.tensor_tensor(yT[:, :, qt * P:(qt + 1) * P], YT.rearrange("p (j t) -> p j t", j=4),
                                          zT[:, :, qt * P:(qt + 1) * P], ALU.mult).then_inc(y_kept, 1)


def merge_stage(m, branch, b_col, yT):
    nc = m.nc
    gate_ready, gate_kept, p_ready, summed, step, *_ = m.stage()
    with ExitStack() as ctx:
        gate = m.sbuf(ctx, "gate", [P, 2, SEQ])
        part = m.sbuf(ctx, "part", [P, 2, SEQ])
        with nc.Block() as block:
            @block.sync
            def _(sp):
                m.clear_previous(sp)
                m.feed(sp, 3)

            @block.tensor
            def _(pe):
                wg = m.take(pe, KT)
                wb = m.take(pe, 4)
                for dt in range(KT):
                    if dt == 4:
                        wg = m.take(pe, KT)
                    if dt >= 2:
                        pe.wait_ge(gate_kept, dt - 1)
                    for j in range(KT):
                        mm = pe.matmul(m.ps[:, dt % 2, :], wg[:, j, dt % 4 * P:(dt % 4 + 1) * P], m.hT[:, j, :],
                                       start=(j == 0), stop=(j == KT - 1))
                    mm.then_inc(gate_ready, 1)
                    if dt >= 2:
                        pe.wait_ge(summed, dt - 1)
                    for j in range(4):
                        mm = pe.matmul(m.ps[:, 2 + dt % 2, :], wb[:, j, dt * P:(dt + 1) * P], yT[:, j, :],
                                       start=(j == 0), stop=(j == 3))
                    mm.then_inc(p_ready, 1)
                    if dt == 3:
                        pe.wait_ge(p_ready, dt + 1)
                        pe.sem_inc(m.slots_used, 1)
                pe.wait_ge(p_ready, KT)
                pe.sem_inc(m.slots_used, 2)

            @block.scalar
            def _(act):
                for dt in range(KT):
                    act.wait_ge(gate_ready, dt + 1)
                    if dt >= 2:
                        act.wait_ge(summed, dt - 1)
                    act.activation(gate[:, dt % 2, :], m.ps[:, dt % 2, :], ACT.Sigmoid,
                                   bias=b_col[:, branch * KT + dt:branch * KT + dt + 1]).then_inc(gate_kept, 1)

            @block.vector
            def _(dve):
                do = Step(dve, step)
                for dt in range(KT):
                    dve.wait_ge(gate_kept, dt + 1)
                    dve.wait_ge(p_ready, dt + 1)
                    if branch == 0:
                        dve.tensor_tensor(m.mixT[:, dt, :], m.ps[:, 2 + dt % 2, :], gate[:, dt % 2, :],
                                          ALU.mult).then_inc(summed, 1)
                    else:
                        do(dve.tensor_tensor(part[:, dt % 2, :], m.ps[:, 2 + dt % 2, :], gate[:, dt % 2, :],
                                             ALU.mult))
                        dve.tensor_tensor(m.mixT[:, dt, :], m.mixT[:, dt, :], part[:, dt % 2, :],
                                          ALU.add).then_inc(summed, 1)


def out_stage(m, b_out):
    nc = m.nc
    loaded, scaled, ready, step, *_ = m.stage()
    with ExitStack() as ctx:
        bias = m.sbuf(ctx, "b_out", [P, D])
        with nc.Block() as block:
            @block.sync
            def _(sp):
                m.clear_previous(sp)
                if b_out is not None:
                    sp.dma_start(bias[:], spread(b_out)).then_inc(loaded, 16)
                m.feed(sp, 2)

            @block.tensor
            def _(pe):
                for nh in range(2):
                    w = m.take(pe, KT)
                    project_out(m, pe, w, nh, ready)

            @block.vector
            def _(dve):
                do = Step(dve, step)
                if b_out is not None:
                    dve.wait_ge(loaded, 16)
                for tt in range(TT):
                    if b_out is not None:
                        do(dve.scalar_tensor_tensor(m.h[:, tt, :], m.h[:, tt, :], ALPHA, bias[:], ALU.mult, ALU.add))
                    else:
                        do(dve.tensor_scalar(m.h[:, tt, :], m.h[:, tt, :], ALPHA, None, ALU.mult))
                for n in range(2 * TT):
                    nh, tt = divmod(n, TT)
                    dve.wait_ge(ready, n + 1)
                    dve.tensor_tensor(m.h[:, tt, nh * 512:(nh + 1) * 512], m.h[:, tt, nh * 512:(nh + 1) * 512],
                                      m.ps[:, n, :], ALU.add)


def project_out(m, pe, w, nh, ready):
    for tt in range(TT):
        for j in range(KT):
            mm = pe.matmul(m.ps[:, nh * TT + tt, :], m.mixT[:, j, tt * P:(tt + 1) * P], w[:, j, :],
                           start=(j == 0), stop=(j == KT - 1))
        mm.then_inc(ready, 1)
    pe.wait_ge(ready, (nh + 1) * TT)
    pe.sem_inc(m.slots_used, 1)


def released(m, pe, sem, n):
    pe.wait_ge(sem, n)
    pe.sem_inc(m.slots_used, 1)


def first_load_stage(m, x):
    nc = m.nc
    loaded, *_ = m.stage()
    with nc.Block() as block:
        @block.sync
        def _(sp):
            m.clear_previous(sp)
            sp.dma_start(m.ident[:], m.table("ident")).then_inc(loaded, 16)
            sp.dma_start(m.h[:], x.rearrange("(t p) d -> p t d", p=P)).then_inc(loaded, 16)
            sp.wait_ge(loaded, 32)


def na_branch(m, l, A, b_cols):
    nc = m.nc
    rpb_pad = A["rpb_pad"]
    RO = 2 * HEADS - 1
    CO = 2 * NA_KW - 1
    PADDED = 2 * GRID_W - 1
    NS = RO - 1
    with ExitStack() as ctx:
        qT = m.sbuf(ctx, "na_qT", [P, 4, SEQ])
        kT = m.sbuf(ctx, "na_kT", [P, 4, SEQ])
        zT = m.sbuf(ctx, "na_zT", [P, 4, SEQ])
        v = m.sbuf(ctx, "na_v", [P, TT, 512])
        table = m.sbuf(ctx, "na_table", [P, HEADS, NS, GRID_W])

        loaded, rpb_loaded, padded, pad_stored, table_loaded, zeroed, tile_ready, tile_kept, tok_ready, tok_kept, *_ = m.stage()
        with ExitStack() as c2:
            rpb = m.sbuf(c2, "rpb", [HEADS * RO, CO])
            pad = m.sbuf(c2, "pad", [HEADS * RO, PADDED])
            skewed = m.sbuf(c2, "skewed", [P, HEADS, NS, GRID_W])
            v_bias = m.sbuf(c2, "v_bias", [P, 512])
            window = m.sbuf(c2, "window", [P, GRID_W])
            with nc.Block() as block:
                @block.sync
                def _(sp):
                    m.clear_previous(sp)
                    sp.dma_start(rpb[:], layer(A["na_rpb"], l).rearrange("h r c -> (h r) c")).then_inc(rpb_loaded, 16)
                    sp.dma_start(v_bias[:], spread(layer(A["b_in"], l)[NA_V:NA_V + 512])).then_inc(loaded, 16)
                    sp.dma_start(window[:], m.table("window")).then_inc(loaded, 16)
                    sp.wait_ge(padded, 1)
                    sp.dma_start(rpb_pad.rearrange("h r c -> (h r) c"), pad[:]).then_inc(pad_stored, 16)
                    m.feed(sp, 4)

                @block.gpsimd
                def _(pool):
                    nc.gpsimd.memset(pad[:], 0.0).then_inc(zeroed, 1)
                    pool.wait_ge(zeroed, 1)
                    pool.wait_ge(rpb_loaded, 16)
                    lo = GRID_W - NA_KW
                    nc.gpsimd.tensor_copy(pad[:, lo:lo + CO], backwards(rpb[:])).then_inc(padded, 1)
                    pool.wait_ge(table_loaded, 16 * 2 * HEADS)
                    pool.wait_ge(loaded, 32)
                    for h in range(HEADS):
                        nc.gpsimd.tensor_tensor(table[:, h], backwards(skewed[:, h]),
                                                window[:].unsqueeze(1).to_broadcast([P, NS, GRID_W]), ALU.add)

                @block.tensor
                def _(pe):
                    project_T(m, pe, m.take(pe, KT), m.hT, KT, 4, (0, 1, 2, 3), 0, tile_ready, tile_kept)
                    released(m, pe, tile_ready, 4)
                    project_T(m, pe, m.take(pe, KT), m.hT, KT, 4, (0, 1, 2, 3), 4, tile_ready, tile_kept)
                    released(m, pe, tile_ready, 8)
                    project_tok(m, pe, m.take(pe, KT), m.hT, (0, 512), (4, 5, 6, 7), 0, tok_ready, tok_kept)
                    released(m, pe, tok_ready, 4)
                    project_T(m, pe, m.take(pe, KT), m.hT, KT, 4, (0, 1, 2, 3), 8, tile_ready, tile_kept)
                    released(m, pe, tile_ready, 12)

                @block.scalar
                def _(act):
                    act.wait_ge(pad_stored, 16)
                    for h in range(HEADS):
                        for b in range(2):
                            src = bass.AP(rpb_pad.tensor, (h * RO + 1 - b) * PADDED,
                                          [[1, GRID_W], [PADDED, NS], [1, GRID_W]])
                            act.dma_start(skewed[GRID_W * b:GRID_W * (b + 1), h], src).then_inc(table_loaded, 16)
                    for n in range(12):
                        act.wait_ge(tile_ready, n + 1)
                        src = m.ps[:, n % 4, :]
                        if n < 4:
                            act.activation(qT[:, n, :], src, ACT.Identity, bias=b_cols["q8"][:, n:n + 1],
                                           scale=HD ** -0.5).then_inc(tile_kept, 1)
                        elif n < 8:
                            act.activation(kT[:, n - 4, :], src, ACT.Identity,
                                           bias=b_cols["all"][:, n:n + 1]).then_inc(tile_kept, 1)
                        else:
                            c = NA_Z // P + n - 8
                            act.activation(zT[:, n - 8, :], src, ACT.Silu,
                                           bias=b_cols["all"][:, c:c + 1]).then_inc(tile_kept, 1)

                @block.vector
                def _(dve):
                    dve.wait_ge(loaded, 32)
                    for tt in range(TT):
                        dve.wait_ge(tok_ready, tt + 1)
                        dve.tensor_tensor(v[:, tt, :], m.ps[:, 4 + tt, :], v_bias[:], ALU.add).then_inc(tok_kept, 1)

        def bias(qt, hd):
            s0 = NS // 2 - 1 - 2 * qt
            return table[:, hd, s0:s0 + HEADS, :].rearrange("p s c -> p (s c)")

        yT = m.sbuf(ctx, "na_yT", [P, 4, SEQ])
        attention_stage(m, qT, kT, lambda hd: (hd // 2, hd // 2, hd % 2 * HD), v, lambda hd: hd * HD, zT, yT,
                        bias, 1.0)
        merge_stage(m, 0, b_cols["gates"], yT)


def gqa_branch(m, l, A, b_cols):
    nc = m.nc
    NQK = 10
    with ExitStack() as ctx:
        zT = m.sbuf(ctx, "gq_zT", [P, 4, SEQ])
        qT = m.sbuf(ctx, "gq_qT", [P, 4, SEQ])
        kT = m.sbuf(ctx, "gq_kT", [P, 1, SEQ])
        v = m.sbuf(ctx, "gq_v", [P, TT, P])
        yT = m.sbuf(ctx, "gq_yT", [P, 4, SEQ])
        (loaded, tile_ready, tile_kept, tok_ready, tok_kept, ms_ready, rs_ready, turn_ready, turned, turn_kept,
         half_ready, step, *_) = m.stage()
        with ExitStack() as c2:
            qk = m.sbuf(c2, "qk", [P, TT, NQK * HD])
            rot = m.sbuf(c2, "rot", [P, 2, NQK * HD])
            tmp = m.sbuf(c2, "tmp", [P, NQK * HD])
            bias = m.sbuf(c2, "bias", [P, 768])
            gain = m.sbuf(c2, "gain", [P, 2 * HD])
            cos = m.sbuf(c2, "cos", [P, TT, 32])
            sin = m.sbuf(c2, "sin", [P, TT, 32])
            ms = m.sbuf(c2, "ms", [P, TT, NQK])
            rs = m.sbuf(c2, "rs", [P, TT, NQK])
            half = m.sbuf(c2, "half", [P, TT, NQK])
            with nc.Block() as block:
                @block.sync
                def _(sp):
                    m.clear_previous(sp)
                    sp.dma_start(bias[:], spread(layer(A["b_in"], l)[GQ_Q:GQ_Q + 768])).then_inc(loaded, 16)
                    sp.dma_start(gain[:, 0:HD], spread(layer(A["q_norm_g"], l))).then_inc(loaded, 16)
                    sp.dma_start(gain[:, HD:2 * HD], spread(layer(A["k_norm_g"], l))).then_inc(loaded, 16)
                    sp.dma_start(cos[:].rearrange("p t f -> p (t f)"), m.table("rope_cos")).then_inc(loaded, 16)
                    sp.dma_start(sin[:].rearrange("p t f -> p (t f)"), m.table("rope_sin")).then_inc(loaded, 16)
                    m.feed(sp, 3)

                @block.gpsimd
                def _(pool):
                    nc.gpsimd.memset(half[:], -0.5).then_inc(half_ready, 1)
                    pool.wait_ge(half_ready, 1)
                    pool.wait_ge(ms_ready, 1)
                    nc.gpsimd.tensor_tensor(rs[:], ms[:], half[:], ALU.pow).then_inc(rs_ready, 1)

                @block.tensor
                def _(pe):
                    project_tok(m, pe, m.take(pe, KT), m.hT, (0, 512), (4, 5, 6, 7), 0, tok_ready, tok_kept)
                    released(m, pe, tok_ready, 4)
                    project_tok(m, pe, m.take(pe, KT), m.hT, (0, 256), (4, 5, 6, 7), 4, tok_ready, tok_kept)
                    released(m, pe, tok_ready, 8)
                    project_T(m, pe, m.take(pe, KT), m.hT, KT, 4, (0, 1), 0, tile_ready, tile_kept)
                    released(m, pe, tile_ready, 4)
                    pe.wait_ge(tok_kept, 8)
                    for tt in range(TT):
                        pe.wait_ge(turn_ready, tt + 1)
                        if tt >= 2:
                            pe.wait_ge(turn_kept, tt - 1)
                        for j in range(5):
                            bank, at = 4 + 2 * (tt % 2) + j // 4, j % 4 * P
                            mm = pe.transpose(m.ps[:, bank, at:at + P], rot[:, tt % 2, j * P:(j + 1) * P], m.ident[:])
                        mm.then_inc(turned, 1)

                @block.scalar
                def _(act):
                    for n in range(4):
                        act.wait_ge(tile_ready, n + 1)
                        c = GQ_Z // P + n
                        act.activation(zT[:, n, :], m.ps[:, n % 2, :], ACT.Silu,
                                       bias=b_cols["all"][:, c:c + 1]).then_inc(tile_kept, 1)
                    for tt in range(TT):
                        act.wait_ge(turned, tt + 1)
                        b = 4 + 2 * (tt % 2)
                        act.copy(qT[:, :, tt * P:(tt + 1) * P], m.ps[:, b, :].rearrange("p (j t) -> p j t", j=4))
                        act.copy(kT[:, 0, tt * P:(tt + 1) * P], m.ps[:, b + 1, 0:P]).then_inc(turn_kept, 1)

                @block.vector
                def _(dve):
                    do = Step(dve, step)
                    dve.wait_ge(loaded, 80)
                    for n in range(8):
                        tt = n % 4
                        dve.wait_ge(tok_ready, n + 1)
                        if n < 4:
                            dve.tensor_tensor(qk[:, tt, 0:512], m.ps[:, 4 + tt, :], bias[:, 0:512],
                                              ALU.add).then_inc(tok_kept, 1)
                        else:
                            do(dve.tensor_tensor(qk[:, tt, 512:640], m.ps[:, 4 + tt, 0:P], bias[:, 512:640], ALU.add))
                            dve.tensor_tensor(v[:, tt, :], m.ps[:, 4 + tt, P:2 * P], bias[:, 640:768],
                                              ALU.add).then_inc(tok_kept, 1)
                    dve.wait_ge(tok_kept, 8)
                    for tt in range(TT):
                        do(dve.tensor_tensor(tmp[:], qk[:, tt, :], qk[:, tt, :], ALU.mult))
                        do(dve.reduce_sum(ms[:, tt, :], tmp[:].rearrange("p (h d) -> p h d", h=NQK), AX.X))
                    dve.tensor_scalar(ms[:], ms[:], 1.0 / HD, RMS_EPS, ALU.mult, ALU.add).then_inc(ms_ready, 1)
                    dve.wait_ge(rs_ready, 1)
                    for tt in range(TT):
                        x3 = qk[:, tt, :].rearrange("p (h d) -> p h d", h=NQK)
                        do(dve.tensor_tensor(x3, x3, rs[:, tt, :].unsqueeze(2).to_broadcast([P, NQK, HD]), ALU.mult))
                        do(dve.tensor_tensor(x3[:, 0:8], x3[:, 0:8],
                                             gain[:, 0:HD].unsqueeze(1).to_broadcast([P, 8, HD]), ALU.mult))
                        do(dve.tensor_tensor(x3[:, 8:10], x3[:, 8:10],
                                             gain[:, HD:].unsqueeze(1).to_broadcast([P, 2, HD]), ALU.mult))
                        if tt >= 2:
                            dve.wait_ge(turned, tt - 1)
                        src = qk[:, tt, 0:512].rearrange("p (g j e o) -> p g j e o", g=2, j=4, o=2)
                        dst = rot[:, tt % 2, 0:512].rearrange("p (j g e o) -> p g j e o", g=2, j=4, o=2)
                        t4 = tmp[:, 0:512].rearrange("p (g j e o) -> p g j e o", g=2, j=4, o=2)
                        ks = qk[:, tt, 512:640].rearrange("p (g e o) -> p g e o", g=2, o=2)
                        kd = rot[:, tt % 2, 512:640].rearrange("p (g e o) -> p g e o", g=2, o=2)
                        kt = tmp[:, 512:640].rearrange("p (g e o) -> p g e o", g=2, o=2)
                        for g in range(3):
                            s, d, t = (src[:, g], dst[:, g], t4[:, g]) if g < 2 else (ks, kd, kt)
                            nh = 4 if g < 2 else 2
                            c = cos[:, tt].unsqueeze(1).to_broadcast([P, nh, 32])
                            n_ = sin[:, tt].unsqueeze(1).to_broadcast([P, nh, 32])
                            do(dve.tensor_tensor(d[..., 0], s[..., 0], c, ALU.mult))
                            do(dve.tensor_tensor(t[..., 0], s[..., 1], n_, ALU.mult))
                            do(dve.tensor_tensor(d[..., 0], d[..., 0], t[..., 0], ALU.subtract))
                            do(dve.tensor_tensor(d[..., 1], s[..., 0], n_, ALU.mult))
                            do(dve.tensor_tensor(t[..., 1], s[..., 1], c, ALU.mult))
                            ins = dve.tensor_tensor(d[..., 1], d[..., 1], t[..., 1], ALU.add)
                            if g < 2:
                                do(ins)
                            else:
                                ins.then_inc(turn_ready, 1)

        attention_stage(m, qT, kT, lambda hd: (hd % 4, 0, hd // 4 * HD), v, lambda hd: hd // 4 * HD, zT, yT,
                        None, HD ** -0.5)
        merge_stage(m, 1, b_cols["gates"], yT)


def gating_branch(m, l, A, b_cols):
    nc = m.nc
    G = 8
    with ExitStack() as ctx:
        uT = m.sbuf(ctx, "sg_uT", [P, 4, SEQ])
        zT = m.sbuf(ctx, "sg_zT", [P, 4, SEQ])
        yT = m.sbuf(ctx, "sg_yT", [P, 4, SEQ])
        v = m.sbuf(ctx, "sg_v", [P, TT, 512])
        w = m.sbuf(ctx, "sg_w", [P, G, P])
        wT = m.sbuf(ctx, "sg_wT", [P, G, P])
        mix_b = m.sbuf(ctx, "sg_b", [P, 4, P])
        tmp = m.sbuf(ctx, "sg_tmp", [P, SEQ])
        bias = m.sbuf(ctx, "sg_bias", [P, 512])
        g = m.sbuf(ctx, "sg_g", [P, 512])
        b = m.sbuf(ctx, "sg_lb", [P, 512])
        stats = m.sbuf(ctx, "sg_stats", [P, TT, 6])
        mv = m.sbuf(ctx, "sg_mv", [P, TT, 2])
        rstd = m.sbuf(ctx, "sg_rstd", [P, TT])
        half = m.sbuf(ctx, "sg_half", [P, TT])
        (loaded, w_loaded, tile_ready, tile_kept, tok_ready, tok_kept, var_ready, rs_ready, half_ready, w_turned,
         wT_ready, v_ready, mixed, mix_read, step, *_) = m.stage()
        with nc.Block() as block:
            @block.sync
            def _(sp):
                m.clear_previous(sp)
                sp.dma_start(w[:], layer(A["sg_w"], l).rearrange("g m n -> m g n")).then_inc(w_loaded, 16)
                sp.dma_start(bias[:], spread(layer(A["b_in"], l)[SG_V:SG_V + 512])).then_inc(loaded, 16)
                sp.dma_start(g[:], spread(layer(A["sg_ln_g"], l))).then_inc(loaded, 16)
                sp.dma_start(b[:], spread(layer(A["sg_ln_b"], l))).then_inc(loaded, 16)
                pairs = layer(A["sg_b"], l).rearrange("(j o) m -> o j m", o=2)
                for o in range(2):
                    sp.dma_start(mix_b[o * HD:(o + 1) * HD], spread(pairs[o], HD)).then_inc(loaded, 16)
                m.feed(sp, 3)

            @block.gpsimd
            def _(pool):
                nc.gpsimd.memset(half[:], -0.5).then_inc(half_ready, 1)
                pool.wait_ge(half_ready, 1)
                pool.wait_ge(var_ready, 1)
                nc.gpsimd.tensor_tensor(rstd[:], mv[:, :, 1], half[:], ALU.pow).then_inc(rs_ready, 1)

            @block.tensor
            def _(pe):
                project_tok(m, pe, m.take(pe, KT), m.hT, (0, 512), (4, 5, 6, 7), 0, tok_ready, tok_kept)
                released(m, pe, tok_ready, 4)
                pe.wait_ge(w_loaded, 16)
                for gr in range(G):
                    mm = pe.transpose(m.ps[:, 2 + gr // 4, gr % 4 * P:(gr % 4 + 1) * P], w[:, gr, :], m.ident[:])
                mm.then_inc(w_turned, 1)
                project_T(m, pe, m.take(pe, KT), m.hT, KT, 4, (0, 1), 0, tile_ready, tile_kept)
                released(m, pe, tile_ready, 4)
                project_T(m, pe, m.take(pe, KT), m.hT, KT, 4, (0, 1), 4, tile_ready, tile_kept)
                released(m, pe, tile_ready, 8)
                pe.wait_ge(wT_ready, 1)
                pe.wait_ge(v_ready, 1)
                pe.wait_ge(tok_kept, 4)
                for j in range(4):
                    for c in range(TT):
                        for o in range(2):
                            gr = 2 * j + o
                            mm = pe.matmul(m.ps[o * HD:(o + 1) * HD, 4 + j, c * P:(c + 1) * P],
                                           v[:, c, gr * HD:(gr + 1) * HD], wT[:, gr, :], start=True, stop=True)
                    mm.then_inc(mixed, 1)

            @block.scalar
            def _(act):
                act.wait_ge(w_turned, 1)
                act.copy(wT[:, 0:4, :], m.ps[:, 2, :].rearrange("p (g m) -> p g m", g=4))
                act.copy(wT[:, 4:8, :], m.ps[:, 3, :].rearrange("p (g m) -> p g m", g=4)).then_inc(wT_ready, 1)
                for n in range(8):
                    act.wait_ge(tile_ready, n + 1)
                    if n < 4:
                        c = SG_U // P + n
                        act.activation(uT[:, n, :], m.ps[:, n % 2, :], ACT.Identity,
                                       bias=b_cols["all"][:, c:c + 1]).then_inc(tile_kept, 1)
                    else:
                        c = SG_Z // P + n - 4
                        act.activation(zT[:, n - 4, :], m.ps[:, n % 2, :], ACT.Silu,
                                       bias=b_cols["all"][:, c:c + 1]).then_inc(tile_kept, 1)

            @block.vector
            def _(dve):
                do = Step(dve, step)
                dve.wait_ge(loaded, 80)
                for tt in range(TT):
                    dve.wait_ge(tok_ready, tt + 1)
                    dve.tensor_tensor(v[:, tt, :], m.ps[:, 4 + tt, :], bias[:], ALU.add).then_inc(tok_kept, 1)
                    dve.wait_ge(tok_kept, tt + 1)
                    do(dve.bn_stats(stats[:, tt, :], v[:, tt, :]))
                    do(dve.bn_aggr(mv[:, tt, :], stats[:, tt, :]))
                dve.tensor_scalar(mv[:, :, 1], mv[:, :, 1], LN_EPS, None, ALU.add).then_inc(var_ready, 1)
                dve.wait_ge(rs_ready, 1)
                for tt in range(TT):
                    do(dve.tensor_scalar(v[:, tt, :], v[:, tt, :], mv[:, tt, 0:1], rstd[:, tt:tt + 1],
                                         ALU.subtract, ALU.mult))
                    do(dve.tensor_tensor(v[:, tt, :], v[:, tt, :], g[:], ALU.mult))
                    ins = dve.tensor_tensor(v[:, tt, :], v[:, tt, :], b[:], ALU.add)
                    if tt < TT - 1:
                        do(ins)
                ins.then_inc(v_ready, 1)
                dve.wait_ge(tile_kept, 8)
                for j in range(4):
                    dve.wait_ge(mixed, j + 1)
                    do(dve.tensor_tensor(tmp[:].rearrange("p (c m) -> p c m", c=TT),
                                         m.ps[:, 4 + j, :].rearrange("p (c m) -> p c m", c=TT),
                                         mix_b[:, j, :].unsqueeze(1).to_broadcast([P, TT, P]), ALU.add))
                    do(dve.tensor_tensor(tmp[:], tmp[:], uT[:, j, :], ALU.mult))
                    do(dve.tensor_tensor(yT[:, j, :], tmp[:], zT[:, j, :], ALU.mult))
        merge_stage(m, 2, b_cols["gates"], yT)


def first_block_plan(w_in, w_br, w_out):
    cols = lambda lo, n=512: rows_chunk(w_in, (lo, lo + n))
    branch = lambda i: [cols(GATES + i * D), rows_chunk(w_br[i], (0, D), 4), cols(GATES + i * D + 512)]
    plan = [cols(NA_Q), cols(NA_K), cols(NA_V), cols(NA_Z)] + branch(0)
    plan += [cols(GQ_Q), cols(GQ_KV, 256), cols(GQ_Z)] + branch(1)
    plan += [cols(SG_V), cols(SG_U), cols(SG_Z)] + branch(2)
    plan += [rows_chunk(w_out, (0, 512)), rows_chunk(w_out, (512, D))]
    return plan


def scale_stage(m, dst, src, factor):
    nc = m.nc
    m.stage()
    with nc.Block() as block:
        @block.sync
        def _(sp):
            m.clear_previous(sp)

        @block.vector
        def _(dve):
            dve.tensor_scalar(dst, src, factor, None, ALU.mult)


def first_block_layer(m, l, A):
    with ExitStack() as ctx:
        n = IN_WIDTH // P
        b_all = m.sbuf(ctx, "b_all", [P, n])
        b_q8 = m.sbuf(ctx, "b_q8", [P, 4])
        m.plan = first_block_plan(layer(A["w_in"], l), [layer(A["w_br_a"], l), layer(A["w_br_b"], l), layer(A["w_br_c"], l)], layer(A["w_out"], l))
        columns_stage(m, [(0, n, layer(A["b_in"], l).rearrange("(r c) -> r c", c=P))], n, b_all[:])
        scale_stage(m, b_q8[:], b_all[:, 0:4], HD ** -0.5)
        b_cols = {"all": b_all, "q8": b_q8, "gates": b_all[:, GATES // P:]}
        na_branch(m, l, A, b_cols)
        gqa_branch(m, l, A, b_cols)
        gating_branch(m, l, A, b_cols)
    out_stage(m, layer(A["b_out"], l))
    norm_stage(m, layer(A["ln_post_g"], l), layer(A["ln_post_b"], l))
    end_ring_stage(m)


def end_ring_stage(m):
    nc = m.nc
    m.stage()
    m.end_plan()
    with nc.Block() as block:
        @block.sync
        def _(sp):
            m.clear_previous(sp)
            nums = [s.num for s in m.slot_landed + [m.slots_used]]
            sp.sem_clear(range(min(nums), max(nums) + 1))


def idle_stage(m):
    m.stage()
    with m.nc.Block() as block:
        @block.sync
        def _(sp):
            m.clear_previous(sp)



GROUP = 256
HGRN, GLA, RWKV, RET, IN2 = 0, 1024, 1808, 2864, 3888
GLA_RANK, GLA_KEY = 16, 32
W_RANK, G_RANK, V_RANK = 64, 160, 32
CH = 64
NC = SEQ // CH
LEVELS = 6
FFN, EXPERTS, FFN_E = 2816, 8, 1408
(C_MU, C_W0, C_A0, C_KK, C_KA, C_RK, C_LG, C_LB, C_V0, C_GLAB, C_HN, C_GN, C_L0, C_L1, C_N) = (
    0, 9, 11, 13, 15, 17, 19, 21, 23, 25, 26, 27, 28, 30, 32)


def project_cols(m, pe, w, cols, banks, first, ready, kept):
    for i, (lo, hi) in enumerate(cols):
        n = first + i
        if n >= len(banks):
            pe.wait_ge(kept, n - len(banks) + 1)
        for j in range(KT):
            mm = pe.matmul(m.ps[0:hi - lo, banks[n % len(banks)], :], w[:, j, lo:hi], m.hT[:, j, :],
                           start=(j == 0), stop=(j == KT - 1))
        mm.then_inc(ready, 1)


def params_stage(m, l, A, cols, lb):
    nc = m.nc
    row = lambda ap: ap.rearrange("(r c) -> r c", c=P)
    one = lambda ap: ap.rearrange("(r c) -> r c", r=1)
    full = 8 * P
    src = [(C_MU, 8, P, row(A["rwkv_mu_2"][l, 0:full])),
           (C_MU + 8, 1, 32, one(A["rwkv_mu_2"][l, full:full + 32])),
           (C_W0, 2, P, row(A["rwkv_w0_2"][l])), (C_A0, 2, P, row(A["rwkv_a0_2"][l])),
           (C_KK, 2, P, row(A["rwkv_k_k_2"][l])), (C_KA, 2, P, row(A["rwkv_k_a_2"][l])),
           (C_RK, 2, P, row(A["rwkv_r_k_2"][l].rearrange("h d -> (h d)"))),
           (C_LG, 2, P, row(A["rwkv_lnx_g_2"][l])), (C_LB, 2, P, row(A["rwkv_lnx_b_2"][l])),
           (C_GLAB, 1, P, one(A["gla_gate_b_2"][l])),
           (C_L0, 2, P, row(A["hgrn_lb_logits_2"][0])), (C_L1, 2, P, row(A["hgrn_lb_logits_2"][1]))]
    if l > 0:
        src.append((C_V0, 2, P, row(A["rwkv_v0_2"][l - 1])))
    twice = [(C_HN, A["hgrn_norm_g_2"][l]), (C_GN, A["gla_norm_g_2"][l])]
    loaded, zeroed, turned, kept, diffed, lb_ready, *_ = m.stage()
    with ExitStack() as ctx:
        rows = m.sbuf(ctx, "prow", [C_N, P])
        diff = m.sbuf(ctx, "lb_diff", [P, 2])
        with nc.Block() as block:
            @block.sync
            def _(sp):
                m.clear_previous(sp)
                sp.wait_ge(zeroed, 1)
                for r, n, c, ap in src:
                    sp.dma_start(rows[r:r + n, 0:c], ap).then_inc(loaded, 16)
                for r, ap in twice:
                    for o in range(2):
                        sp.dma_start(rows[r:r + 1, o * HD:(o + 1) * HD], one(ap)).then_inc(loaded, 16)
                m.feed(sp, 0)

            @block.gpsimd
            def _(pool):
                nc.gpsimd.memset(rows[:], 0.0).then_inc(zeroed, 1)

            @block.tensor
            def _(pe):
                pe.wait_ge(loaded, 16 * (len(src) + 4))
                pe.transpose(m.ps[:, 0, 0:C_N], rows[:], m.ident[0:C_N, 0:C_N]).then_inc(turned, 1)

            @block.vector
            def _(dve):
                dve.wait_ge(turned, 1)
                dve.tensor_copy(cols[:], m.ps[:, 0, 0:C_N]).then_inc(kept, 1)
                dve.wait_ge(kept, 1)
                if l == 0:
                    dve.memset(lb[:, 0:2], 0.0)
                    dve.memset(lb[:, 2:4], 1.0)
                else:
                    dve.tensor_tensor(diff[:], cols[:, C_L1:C_L1 + 2], cols[:, C_L0:C_L0 + 2],
                                      ALU.subtract).then_inc(diffed, 1)
                    dve.wait_ge(lb_ready, 1)
                    dve.tensor_scalar(lb[:, 2:4], lb[:, 0:2], -1.0, 1.0, ALU.mult, ALU.add)

            if l > 0:
                @block.scalar
                def _(act):
                    act.wait_ge(diffed, 1)
                    act.activation(lb[:, 0:2], diff[:], ACT.Sigmoid).then_inc(lb_ready, 1)


def hgrn_project(m, qT, kT, gT, v, gate, lb):
    nc = m.nc
    ready, kept, tok_ready, tok_kept, f_ready, step, *_ = m.stage()
    with nc.Block() as block:
        @block.sync
        def _(sp):
            m.clear_previous(sp)
            m.feed(sp, 2)

        @block.tensor
        def _(pe):
            tile = [(i * P, (i + 1) * P) for i in range(4)]
            project_cols(m, pe, m.take(pe, KT), tile, (0, 1, 2, 3), 0, ready, kept)
            released(m, pe, ready, 4)
            w = m.take(pe, KT)
            project_tok(m, pe, w, m.hT, (0, GROUP), (4, 5, 6, 7), 0, tok_ready, tok_kept)
            project_cols(m, pe, w, tile[2:], (0, 1, 2, 3), 4, ready, kept)
            released(m, pe, ready, 6)

        @block.scalar
        def _(act):
            for n in range(6):
                act.wait_ge(ready, n + 1)
                dst, f = ((qT, ACT.Silu), (gT, ACT.Sigmoid), (gate, ACT.Silu))[n // 2]
                act.activation(dst[:, n % 2, :], m.ps[:, n % 4, :], f).then_inc(kept, 1)
            for j in range(2):
                act.wait_ge(f_ready, j + 1)
                act.activation(gT[:, j, :], gT[:, j, :], ACT.Ln)

        @block.vector
        def _(dve):
            do = Step(dve, step)
            for j in range(2):
                dve.wait_ge(kept, 3 + j)
                do(dve.tensor_scalar(gT[:, j, :], gT[:, j, :], lb[:, 2 + j:3 + j], lb[:, j:j + 1], ALU.mult, ALU.add))
                do(dve.tensor_scalar(kT[:, j, :], gT[:, j, :], -1.0, 1.0, ALU.mult, ALU.add))
                dve.tensor_scalar(gT[:, j, :], gT[:, j, :], 1e-19, None, ALU.max).then_inc(f_ready, 1)
            for tt in range(TT):
                dve.wait_ge(tok_ready, tt + 1)
                dve.tensor_copy(v[:, tt, :], m.ps[:, 4 + tt, 0:GROUP]).then_inc(tok_kept, 1)


def gla_project(m, qT, kT, gT, v, gate, w2, b_col):
    nc = m.nc
    (ready, kept, tok_ready, tok_kept, w_loaded, g_ready, x_ready, abs_ready, ln_ready, step, *_) = m.stage()
    with ExitStack() as ctx:
        lr = m.sbuf(ctx, "g_lr", [GLA_RANK, SEQ])
        w = m.sbuf(ctx, "gla_w2", [GLA_RANK, P])
        x = m.sbuf(ctx, "gla_x", [P, SEQ])
        e = m.sbuf(ctx, "gla_e", [P, SEQ])
        with nc.Block() as block:
            @block.sync
            def _(sp):
                m.clear_previous(sp)
                sp.dma_start(w[:], w2).then_inc(w_loaded, 16)
                m.feed(sp, 2)

            @block.tensor
            def _(pe):
                wa = m.take(pe, KT)
                project_cols(m, pe, wa, [(0, P), (P, 2 * P)], (0, 1, 2, 3), 0, ready, kept)
                project_tok(m, pe, wa, m.hT, (GROUP, 2 * GROUP), (4, 5, 6, 7), 0, tok_ready, tok_kept)
                released(m, pe, tok_ready, 4)
                r = GLA_RANK
                project_cols(m, pe, m.take(pe, KT), [(0, r), (r, r + P), (r + P, r + 2 * P)], (0, 1, 2, 3), 2,
                             ready, kept)
                released(m, pe, ready, 5)
                pe.wait_ge(w_loaded, 16)
                pe.wait_ge(kept, 3)
                pe.matmul(m.ps[:, 1, :], w[:], lr[:], start=True, stop=True).then_inc(g_ready, 1)

            @block.scalar
            def _(act):
                for n in range(5):
                    act.wait_ge(ready, n + 1)
                    src = m.ps[:, n % 4, :]
                    if n == 0:
                        act.mul(qT[:, 0, :], src, GLA_KEY ** -0.5).then_inc(kept, 1)
                    elif n == 1:
                        act.copy(kT[:, 0, :], src).then_inc(kept, 1)
                    elif n == 2:
                        act.copy(lr[:], m.ps[0:GLA_RANK, n, :]).then_inc(kept, 1)
                    else:
                        act.activation(gate[:, n - 3, :], src, ACT.Silu).then_inc(kept, 1)
                act.wait_ge(x_ready, 1)
                act.activation(e[:], x[:], ACT.Abs).then_inc(abs_ready, 1)
                act.wait_ge(abs_ready, 1)
                act.activation(e[:], e[:], ACT.Exp, scale=-1.0).then_inc(abs_ready, 1)
                act.wait_ge(abs_ready, 2)
                act.activation(e[:], e[:], ACT.Ln, bias=1.0).then_inc(ln_ready, 1)

            @block.vector
            def _(dve):
                for tt in range(TT):
                    dve.wait_ge(tok_ready, tt + 1)
                    dve.tensor_copy(v[:, tt, :], m.ps[:, 4 + tt, 0:GROUP]).then_inc(tok_kept, 1)
                do = Step(dve, step)
                dve.wait_ge(g_ready, 1)
                dve.tensor_scalar(x[:], m.ps[:, 1, :], b_col, None, ALU.add).then_inc(x_ready, 1)
                dve.wait_ge(ln_ready, 1)
                do(dve.tensor_scalar(x[:], x[:], 0.0, None, ALU.min))
                do(dve.tensor_tensor(x[:], x[:], e[:], ALU.subtract))
                do(dve.tensor_scalar(gT[:, 0, :], x[:], 1.0 / 16, None, ALU.mult))


def gated_linear_stage(m, nt, width, qT, kT, gT, v, gate, norm_col, out_tile):
    nc = m.nc
    (loaded, cum_ready, diff_ready, exp_ready, ql_ready, kl_ready, level_ready, level_kept, dec_ready, kdec_turned,
     kdec_kept, delta_ready, state_ready, o_ready, ms_ready, rs_ready, y_ready, y_turned, step, half_ready,
     edec_ready, *_) = m.stage()
    NV = GROUP // nt
    delta = lambda c, j: m.ps[:, 2 + 2 * (c % 2) + c // 4, (c // 2 % 2 * nt + j) * NV:(c // 2 % 2 * nt + j + 1) * NV]
    place = (lambda h: (h // 2, h % 2 * HD)) if width == HD else (lambda h: (0, h * width))
    with ExitStack() as ctx:
        keep = m.sbuf(ctx, "keep", [P, SEQ])
        masks = m.sbuf(ctx, "masks", [P, LEVELS, P])
        cum = m.sbuf(ctx, "cum", [P, nt, SEQ])
        diff = m.sbuf(ctx, "diff", [P, nt, SEQ])
        ex = m.sbuf(ctx, "ex", [P, nt, SEQ])
        ql = m.sbuf(ctx, "ql", [P, 2, nt, SEQ])
        kl = m.sbuf(ctx, "kl", [P, 2, nt, SEQ])
        scores = m.sbuf(ctx, "scores", [P, 4, TT, P])
        qd = m.sbuf(ctx, "qd", [P, nt, SEQ])
        kd_tok = m.sbuf(ctx, "kd_tok", [P, TT, nt * P])
        pend = m.sbuf(ctx, "pend", [P, nt, NC])
        state = m.sbuf(ctx, "state", [P, NC, nt, NV])
        own = m.sbuf(ctx, "own", [P, NV])
        y = m.sbuf(ctx, "y", [P, TT, GROUP])
        sq = m.sbuf(ctx, "sq", [P, GROUP])
        ms = m.sbuf(ctx, "ms", [P, TT, 4])
        rs = m.sbuf(ctx, "rs", [P, TT, 4])
        half = m.sbuf(ctx, "half", [P, TT, 4])
        kd = kl[:, 1]
        by_chunk = lambda t, j: t[:, j, :].rearrange("p (c t) -> p c t", c=NC)
        with nc.Block() as block:
            @block.sync
            def _(sp):
                m.clear_previous(sp)
                sp.dma_start(keep[:], m.table("keep")).then_inc(loaded, 16)
                sp.dma_start(masks[:].rearrange("p s t -> p (s t)"), m.table("levels")).then_inc(loaded, 16)
                sp.dma_start(own[:], m.table("halves" if nt == 2 else "quarters")).then_inc(loaded, 16)
                m.feed(sp, 0)

            @block.tensor
            def _(pe):
                for lv in range(-1, LEVELS):
                    if lv == 0:
                        pe.wait_ge(dec_ready, 1)
                        pe.wait_ge(level_kept, 4)
                        for tt in range(TT):
                            for j in range(nt):
                                n = tt * nt + j
                                mm = pe.transpose(m.ps[:, n // 4, n % 4 * P:(n % 4 + 1) * P],
                                                  kd[:, j, tt * P:(tt + 1) * P], m.ident[:])
                        mm.then_inc(kdec_turned, 1)
                        pe.wait_ge(kdec_kept, 1)
                        for c in range(NC):
                            o, tt = c % 2 * CH, c // 2
                            for j in range(nt):
                                mm = pe.matmul(delta(c, j), kd_tok[o:o + CH, tt, j * P:(j + 1) * P],
                                               v[o:o + CH, tt, j * NV:(j + 1) * NV], start=True, stop=True)
                        mm.then_inc(delta_ready, 1)
                        pe.wait_ge(state_ready, 1)
                    if lv >= 0:
                        pe.wait_ge(ql_ready, lv + 1)
                        pe.wait_ge(kl_ready, lv + 1)
                    for h in range(4):
                        j, at = place(h)
                        bank = 4 * ((lv + 1) % 2) + h
                        n = 4 * (lv + 1) + h
                        if n >= 8:
                            pe.wait_ge(level_kept, n - 7)
                        q_, k_ = (qT, kT) if lv < 0 else (ql[:, lv % 2], kl[:, lv % 2])
                        for tt in range(TT):
                            mm = pe.matmul(m.ps[:, bank, tt * P:(tt + 1) * P],
                                           k_[at:at + width, j, tt * P:(tt + 1) * P],
                                           q_[at:at + width, j, tt * P:(tt + 1) * P], start=True, stop=True)
                        mm.then_inc(level_ready, 1)
                pe.wait_ge(level_kept, 4 * (LEVELS + 1))
                for tt in range(TT):
                    for h in range(4):
                        pe.matmul(m.ps[:, tt, h * HD:(h + 1) * HD], scores[:, h, tt, :],
                                  v[:, tt, h * HD:(h + 1) * HD], start=(h == 0), stop=False,
                                  skip_group_check=True)
                    for c in (2 * tt, 2 * tt + 1):
                        o = c % 2 * CH
                        for j in range(nt):
                            mm = pe.matmul(m.ps[o:o + CH, tt, j * NV:(j + 1) * NV], qd[:, j, c * CH:(c + 1) * CH],
                                           state[:, c, j, :], start=False, stop=(j == nt - 1),
                                           skip_group_check=True)
                    mm.then_inc(o_ready, 1)
                for tt in range(TT):
                    pe.wait_ge(y_ready, tt + 1)
                    for j in range(2):
                        mm = pe.transpose(m.ps[:, 4 + j, tt * P:(tt + 1) * P], y[:, tt, j * P:(j + 1) * P], m.ident[:])
                    mm.then_inc(y_turned, 1)

            @block.scalar
            def _(act):
                act.wait_ge(cum_ready, 1)
                act.activation(ex[:], cum[:], ACT.Exp).then_inc(edec_ready, 1)
                act.activation(pend[:], cum[:].rearrange("p j (c t) -> p j c t", t=CH)[:, :, :, CH - 1],
                               ACT.Exp).then_inc(edec_ready, 1)
                act.wait_ge(diff_ready, 1)
                act.wait_ge(dec_ready, 1)
                act.activation(ex[:], diff[:], ACT.Exp).then_inc(edec_ready, 1)
                for lv in range(LEVELS):
                    act.wait_ge(diff_ready, lv + 2)
                    if lv == 0:
                        act.wait_ge(dec_ready, 2)
                    else:
                        act.wait_ge(ql_ready, lv)
                        act.wait_ge(kl_ready, lv)
                    act.activation(ex[:], diff[:], ACT.Exp).then_inc(exp_ready, 1)
                act.wait_ge(kdec_turned, 1)

            @block.gpsimd
            def _(pool):
                nc.gpsimd.memset(half[:], -0.5).then_inc(half_ready, 1)
                for lv in range(LEVELS):
                    pool.wait_ge(exp_ready, lv + 1)
                    if lv >= 1:
                        pool.wait_ge(level_ready, 4 * lv)
                    if lv == 1:
                        pool.wait_ge(kdec_turned, 1)
                    nc.gpsimd.tensor_tensor(kl[:, lv % 2], kT[:, 0:nt], ex[:], ALU.mult).then_inc(kl_ready, 1)
                pool.wait_ge(half_ready, 1)
                pool.wait_ge(ms_ready, 1)
                nc.gpsimd.tensor_tensor(rs[:], ms[:], half[:], ALU.pow).then_inc(rs_ready, 1)

            @block.vector
            def _(dve):
                do = Step(dve, step)

                def middle(lv):
                    s = 1 << lv
                    if lv == 0:
                        dve.wait_ge(edec_ready, 3)
                    else:
                        dve.wait_ge(exp_ready, lv)
                    for j in range(nt):
                        cb = cum[:, j, :].rearrange("p (b t) -> p b t", t=2 * s)
                        db = diff[:, j, :].rearrange("p (b t) -> p b t", t=2 * s)
                        mid = cb[:, :, s - 1:s].to_broadcast([P, SEQ // (2 * s), s])
                        dve.tensor_tensor(db[:, :, 0:s], mid, cb[:, :, 0:s], ALU.subtract)
                        ins = dve.tensor_tensor(db[:, :, s:2 * s], cb[:, :, s:2 * s], mid, ALU.subtract)
                    ins.then_inc(diff_ready, 1)

                def take(lv):
                    for h in range(4):
                        dve.wait_ge(level_ready, 4 * (lv + 1) + h + 1)
                        mask = m.ident[:] if lv < 0 else masks[:, lv, :]
                        dve.copy_predicated(scores[:, h], mask.bitcast(I32).unsqueeze(1).to_broadcast([P, TT, P]),
                                            m.ps[:, 4 * ((lv + 1) % 2) + h, :].rearrange("p (t i) -> p t i", t=TT)
                                            ).then_inc(level_kept, 1)

                do(dve.memset(scores[:], 0.0))
                do(dve.memset(state[:, 0], 0.0))
                dve.wait_ge(loaded, 48)
                for j in range(nt):
                    ins = dve.tensor_tensor_scan(cum[:, j, :], keep[:], gT[:, j, :], 0.0, ALU.mult, ALU.add)
                    if j < nt - 1:
                        do(ins)
                ins.then_inc(cum_ready, 1)
                dve.wait_ge(cum_ready, 1)
                for j in range(nt):
                    cb = by_chunk(cum, j)
                    ins = dve.tensor_tensor(by_chunk(diff, j), cb[:, :, CH - 1:CH].to_broadcast([P, NC, CH]), cb,
                                            ALU.subtract)
                ins.then_inc(diff_ready, 1)
                dve.wait_ge(edec_ready, 2)
                dve.tensor_tensor(qd[:], qT[:, 0:nt], ex[:], ALU.mult).then_inc(dec_ready, 1)
                dve.wait_ge(edec_ready, 3)
                dve.tensor_tensor(kd[:], kT[:, 0:nt], ex[:], ALU.mult).then_inc(dec_ready, 1)
                take(-1)
                middle(0)
                dve.wait_ge(kdec_turned, 1)
                for n in range((nt * TT + 3) // 4):
                    ins = dve.tensor_copy(kd_tok[:].rearrange("p t f -> p (t f)")[:, n * 512:(n + 1) * 512],
                                          m.ps[:, n, :])
                ins.then_inc(kdec_kept, 1)
                dve.wait_ge(delta_ready, 1)
                for c in range(NC - 1):
                    for j in range(nt):
                        do(dve.scalar_tensor_tensor(state[:, c + 1, j, :], state[:, c, j, :], pend[:, j, c:c + 1],
                                                    delta(c, j), ALU.mult, ALU.add))
                st = state[:].rearrange("p c j v -> p (c j) v")
                dve.tensor_tensor(st, st, own[:].unsqueeze(1).to_broadcast([P, NC * nt, NV]),
                                  ALU.mult).then_inc(state_ready, 1)
                for lv in range(LEVELS):
                    dve.wait_ge(exp_ready, lv + 1)
                    if lv >= 2:
                        dve.wait_ge(level_ready, 4 * lv)
                    dve.tensor_tensor(ql[:, lv % 2], qT[:, 0:nt], ex[:], ALU.mult).then_inc(ql_ready, 1)
                    if lv + 1 < LEVELS:
                        middle(lv + 1)
                    take(lv)
                for tt in range(TT):
                    dve.wait_ge(o_ready, tt + 1)
                    do(dve.tensor_copy(y[:, tt, :], m.ps[:, tt, 0:GROUP]))
                    do(dve.tensor_tensor(sq[:], y[:, tt, :], y[:, tt, :], ALU.mult))
                    do(dve.reduce_sum(ms[:, tt, :], sq[:].rearrange("p (h d) -> p h d", h=4), AX.X))
                dve.tensor_scalar(ms[:], ms[:], 1.0 / HD, RMS_EPS, ALU.mult, ALU.add).then_inc(ms_ready, 1)
                dve.wait_ge(rs_ready, 1)
                for tt in range(TT):
                    y3 = y[:, tt, :].rearrange("p (h d) -> p h d", h=4)
                    dve.tensor_tensor(y3, y3, rs[:, tt, :].unsqueeze(2).to_broadcast([P, 4, HD]),
                                      ALU.mult).then_inc(y_ready, 1)
                dve.wait_ge(y_turned, TT)
                for j in range(2):
                    dve.scalar_tensor_tensor(m.mixT[:, out_tile + j, :], m.ps[:, 4 + j, :], norm_col, gate[:, j, :],
                                             ALU.mult, ALU.mult)


def hgrn_mixer(m, cols, lb):
    with ExitStack() as ctx:
        qT, kT, gT, gate = (m.sbuf(ctx, n, [P, 2, SEQ]) for n in ("hg_qT", "hg_kT", "hg_gT", "hg_gate"))
        v = m.sbuf(ctx, "hg_v", [P, TT, GROUP])
        hgrn_project(m, qT, kT, gT, v, gate, lb)
        gated_linear_stage(m, 2, HD, qT, kT, gT, v, gate, cols[:, C_HN:C_HN + 1], 0)


def gla_mixer(m, l, A, cols):
    with ExitStack() as ctx:
        qT, kT, gT = (m.sbuf(ctx, n, [P, 1, SEQ]) for n in ("gl_qT", "gl_kT", "gl_gT"))
        gate = m.sbuf(ctx, "gl_gate", [P, 2, SEQ])
        v = m.sbuf(ctx, "gl_v", [P, TT, GROUP])
        gla_project(m, qT, kT, gT, v, gate, A["gla_gate_w2_2"][l], cols[:, C_GLAB:C_GLAB + 1])
        gated_linear_stage(m, 1, GLA_KEY, qT, kT, gT, v, gate, cols[:, C_GN:C_GN + 1], 2)


LNX_EPS = 64e-5
TWO_PI = 2 * np.pi


def persist2(m, ctx):
    m.v_first = m.sbuf(ctx, "v_first", [P, 2, SEQ])


def rwkv_project(m, mixed, cols):
    nc = m.nc
    ready, kept, raw_ready, raw_used, step, zeroed, *_ = m.stage()
    with ExitStack() as ctx:
        raw = m.sbuf(ctx, "rw_raw", [P, 2, SEQ + 1])
        d = m.sbuf(ctx, "rw_d", [P, SEQ])
        with nc.Block() as block:
            @block.sync
            def _(sp):
                m.clear_previous(sp)
                m.feed(sp, 3)

            @block.gpsimd
            def _(pool):
                nc.gpsimd.memset(raw[:, :, 0:1], 0.0).then_inc(zeroed, 1)

            @block.tensor
            def _(pe):
                tile = [(i * P, (i + 1) * P) for i in range(4)]
                for first, cs in ((0, tile), (4, tile), (8, [(0, 32)])):
                    project_cols(m, pe, m.take(pe, KT), cs, (0, 1, 2, 3), first, ready, kept)
                    released(m, pe, ready, first + len(cs))

            @block.scalar
            def _(act):
                for n in range(9):
                    p = P if n < 8 else 32
                    act.wait_ge(ready, n + 1)
                    if n >= 2:
                        act.wait_ge(raw_used, n - 1)
                    act.copy(raw[0:p, n % 2, 1:], m.ps[0:p, n % 4, :]).then_inc(kept, 1)

            @block.vector
            def _(dve):
                do = Step(dve, step)
                dve.wait_ge(zeroed, 1)
                for n in range(9):
                    p = P if n < 8 else 32
                    dve.wait_ge(kept, n + 1)
                    do(dve.tensor_tensor(d[0:p], raw[0:p, n % 2, 0:SEQ], raw[0:p, n % 2, 1:], ALU.subtract))
                    dve.scalar_tensor_tensor(mixed[0:p, n, :], d[0:p], cols[0:p, C_MU + n:C_MU + n + 1],
                                             raw[0:p, n % 2, 1:], ALU.mult, ALU.add).then_inc(raw_used, 1)
                    dve.wait_ge(raw_used, n + 1)


def rwkv_prepare(m, l, A, cols, mixed, rho, kap, bet, khat, gate, bonus, pend):
    nc = m.nc
    (w_loaded, low_ready, u_ready, a_ready, g_ready, v1_ready, t1_ready, v2_ready, vs_ready, sq_ready, ss_ready,
     floor_ready, sqrt_ready, ld_ready, a_kept, cum_ready, ex_ready, rk_ready, rk_summed, step, *_) = m.stage()
    with ExitStack() as ctx:
        wa = m.sbuf(ctx, "w2a2", [P, GROUP])
        g2 = m.sbuf(ctx, "g2", [P, 2, GROUP])
        v1 = m.sbuf(ctx, "v1", [P, 2, V_RANK])
        v2 = m.sbuf(ctx, "v2", [V_RANK, GROUP])
        halves = m.sbuf(ctx, "halves", [P, P])
        keep = m.sbuf(ctx, "keep", [P, SEQ])
        th = m.sbuf(ctx, "th", [W_RANK, SEQ])
        t1 = m.sbuf(ctx, "t1", [V_RANK, SEQ])
        kk, sq, ld, cum, a, nrm = (m.sbuf(ctx, n, [P, 2, SEQ]) for n in ("kk", "sq", "ld", "cum", "a", "nrm"))
        r, k, v = mixed[:, 0:2], mixed[:, 2:4], mixed[:, 4:6]
        n_loads = 6 + (2 if l else 0)
        col = lambda c, j: cols[:, c + j:c + j + 1]
        with nc.Block() as block:
            @block.sync
            def _(sp):
                m.clear_previous(sp)
                sp.dma_start(wa[0:W_RANK], A["rwkv_w2_2"][l]).then_inc(w_loaded, 16)
                sp.dma_start(wa[W_RANK:P], A["rwkv_a2_2"][l]).then_inc(w_loaded, 16)
                sp.dma_start(g2[:, 0], A["rwkv_g2_2"][l, 0:P]).then_inc(w_loaded, 16)
                sp.dma_start(g2[0:32, 1], A["rwkv_g2_2"][l, P:G_RANK]).then_inc(w_loaded, 16)
                sp.dma_start(halves[:], m.table("halves")).then_inc(w_loaded, 16)
                sp.dma_start(keep[:], m.table("keep")).then_inc(w_loaded, 16)
                if l:
                    sp.dma_start(v1[:], A["rwkv_v1_2"][l - 1].rearrange("(j p) c -> p j c", p=P)).then_inc(w_loaded, 16)
                    sp.dma_start(v2[:], A["rwkv_v2_2"][l - 1]).then_inc(w_loaded, 16)
                m.feed(sp, 0)

            @block.tensor
            def _(pe):
                pe.wait_ge(w_loaded, 16 * n_loads)
                for j in range(2):
                    mm = pe.matmul(m.ps[:, 2 + j, :], wa[W_RANK:P, j * P:(j + 1) * P], mixed[W_RANK:P, 6, :],
                                   start=True, stop=True)
                mm.then_inc(a_ready, 1)
                pe.wait_ge(low_ready, 1)
                for j in range(2):
                    mm = pe.matmul(m.ps[:, j, :], wa[0:W_RANK, j * P:(j + 1) * P], th[:], start=True, stop=True)
                mm.then_inc(u_ready, 1)
                pe.wait_ge(low_ready, 3)
                for j in range(2):
                    pe.matmul(m.ps[:, 4 + j, :], g2[:, 0, j * P:(j + 1) * P], mixed[:, 7, :], start=True, stop=False)
                    mm = pe.matmul(m.ps[:, 4 + j, :], g2[0:32, 1, j * P:(j + 1) * P], mixed[0:32, 8, :],
                                   start=False, stop=True)
                mm.then_inc(g_ready, 1)
                if l:
                    for j in range(2):
                        mm = pe.matmul(m.ps[0:V_RANK, 6, :], v1[:, j, :], v[:, j, :], start=(j == 0), stop=(j == 1))
                    mm.then_inc(v1_ready, 1)
                    pe.wait_ge(t1_ready, 1)
                    for j in range(2):
                        mm = pe.matmul(m.ps[:, 6 + j, :], v2[:, j * P:(j + 1) * P], t1[:], start=True, stop=True)
                    mm.then_inc(v2_ready, 1)
                pe.wait_ge(sq_ready, 1)
                pe.wait_ge(ld_ready, 1)
                for j in range(2):
                    mm = pe.matmul(m.ps[:, j, :], halves[:], sq[:, j, :], start=True, stop=True)
                mm.then_inc(ss_ready, 1)
                pe.wait_ge(rk_ready, 1)
                pe.wait_ge(a_kept, 1)
                for j in range(2):
                    mm = pe.matmul(m.ps[:, 2 + j, :], halves[:], sq[:, j, :], start=True, stop=True)
                mm.then_inc(rk_summed, 1)

            @block.scalar
            def _(act):
                act.activation(th[:], mixed[0:W_RANK, 6, :], ACT.Tanh).then_inc(low_ready, 1)
                act.activation(mixed[:, 7, :], mixed[:, 7, :], ACT.Sigmoid).then_inc(low_ready, 1)
                act.activation(mixed[0:32, 8, :], mixed[0:32, 8, :], ACT.Sigmoid).then_inc(low_ready, 1)
                act.wait_ge(a_ready, 1)
                for j in range(2):
                    ins = act.activation(a[:, j, :], m.ps[:, 2 + j, :], ACT.Sigmoid, bias=col(C_A0, j))
                ins.then_inc(a_kept, 1)
                act.wait_ge(u_ready, 1)
                for j in range(2):
                    ins = act.activation(ld[:, j, :], m.ps[:, j, :], ACT.Sigmoid, bias=col(C_W0, j))
                ins.then_inc(ld_ready, 1)
                if l:
                    act.wait_ge(v1_ready, 1)
                    act.copy(t1[:], m.ps[0:V_RANK, 6, :]).then_inc(t1_ready, 1)
                    act.wait_ge(v2_ready, 1)
                    for j in range(2):
                        ins = act.activation(nrm[:, j, :], m.ps[:, 6 + j, :], ACT.Sigmoid, bias=col(C_V0, j))
                    ins.then_inc(vs_ready, 1)
                act.wait_ge(g_ready, 1)
                act.copy(gate[:], m.ps[:, 4:6, :])
                act.wait_ge(floor_ready, 1)
                act.activation(nrm[:], nrm[:], ACT.Sqrt).then_inc(sqrt_ready, 1)
                act.wait_ge(cum_ready, 1)
                act.activation(rho[:], cum[:], ACT.Exp)
                act.activation(bet[:], cum[:], ACT.Exp, scale=-1.0)
                act.activation(khat[:], cum[:], ACT.Exp, scale=-1.0)
                act.activation(pend[:], cum[:].rearrange("p j (c t) -> p j c t", t=CH)[:, :, :, CH - 1], ACT.Exp)
                act.activation(kap[:], kap[:], ACT.Exp).then_inc(ex_ready, 1)

            @block.vector
            def _(dve):
                do = Step(dve, step)
                for j in range(2):
                    do(dve.tensor_scalar(kk[:, j, :], k[:, j, :], col(C_KK, j), None, ALU.mult))
                dve.tensor_tensor(sq[:], kk[:], kk[:], ALU.mult).then_inc(sq_ready, 1)
                dve.wait_ge(ld_ready, 1)
                do(dve.tensor_scalar(ld[:], ld[:], -float(np.exp(-0.5)), None, ALU.mult))
                dve.wait_ge(w_loaded, 16 * n_loads)
                for j in range(2):
                    do(dve.tensor_tensor_scan(cum[:, j, :], keep[:], ld[:, j, :], 0.0, ALU.mult, ALU.add))
                dve.tensor_tensor(kap[:], cum[:], ld[:], ALU.subtract).then_inc(cum_ready, 1)
                if l:
                    dve.wait_ge(vs_ready, 1)
                    dve.wait_ge(cum_ready, 1)
                    do(dve.tensor_tensor(ld[:], m.v_first[:], v, ALU.subtract))
                    do(dve.tensor_tensor(ld[:], ld[:], nrm[:], ALU.mult))
                    do(dve.tensor_tensor(v, v, ld[:], ALU.add))
                else:
                    do(dve.tensor_copy(m.v_first[:], v))
                dve.wait_ge(ss_ready, 1)
                dve.tensor_scalar(nrm[:], m.ps[:, 0:2, :], 1e-24, None, ALU.max).then_inc(floor_ready, 1)
                dve.wait_ge(sqrt_ready, 1)
                do(dve.reciprocal(nrm[:], nrm[:]))
                do(dve.tensor_tensor(kk[:], kk[:], nrm[:], ALU.mult))
                dve.wait_ge(a_kept, 1)
                for j in range(2):
                    do(dve.tensor_scalar(nrm[:, j, :], a[:, j, :], -1.0, col(C_KA, j), ALU.add, ALU.mult))
                do(dve.scalar_tensor_tensor(k, nrm[:], 1.0, k, ALU.add, ALU.mult))
                do(dve.tensor_tensor(a[:], a[:], kk[:], ALU.mult))
                do(dve.tensor_tensor(sq[:], r, k, ALU.mult))
                for j in range(2):
                    ins = dve.tensor_scalar(sq[:, j, :], sq[:, j, :], col(C_RK, j), None, ALU.mult)
                ins.then_inc(rk_ready, 1)
                dve.wait_ge(ex_ready, 1)
                do(dve.tensor_tensor(rho[:], rho[:], r, ALU.mult))
                do(dve.tensor_tensor(kap[:], kap[:], kk[:], ALU.mult))
                do(dve.tensor_tensor(bet[:], bet[:], a[:], ALU.mult))
                do(dve.tensor_tensor(khat[:], khat[:], k, ALU.mult))
                dve.wait_ge(rk_summed, 1)
                do(dve.tensor_tensor(bonus[:], m.ps[:, 2:4, :], v, ALU.mult))


def turn_stage(m, pairs):
    nc = m.nc
    turned, *_ = m.stage()
    with nc.Block() as block:
        @block.sync
        def _(sp):
            m.clear_previous(sp)
            m.feed(sp, 0)

        @block.tensor
        def _(pe):
            for i, (src, _dst) in enumerate(pairs):
                for n in range(2):
                    for t in range(2):
                        for j in range(2):
                            tt = 2 * n + t
                            mm = pe.transpose(m.ps[:, 2 * i + n, (2 * t + j) * P:(2 * t + j + 1) * P],
                                              src[:, j, tt * P:(tt + 1) * P], m.ident[:])
                    mm.then_inc(turned, 1)

        def copies(eng, copy, odd):
            for i, (_src, dst) in enumerate(pairs):
                for n in range(2):
                    if n == odd:
                        eng.wait_ge(turned, 2 * i + n + 1)
                        copy(dst[:, 2 * n:2 * n + 2, :].rearrange("p t f -> p (t f)"), m.ps[:, 2 * i + n, :])

        @block.scalar
        def _(act):
            copies(act, act.copy, 0)

        @block.vector
        def _(dve):
            copies(dve, dve.tensor_copy, 1)


def rwkv_inverse(m, kap, bet, khat, kap_tok, v_tok, uT, w):
    nc = m.nc
    (loaded, l_ready, l_kept, init, as_ready, b_ready, b_kept, xy_ready, x_kept, y_kept, u_ready, vp_ready, vp_kept,
     w_ready, step, *_) = m.stage()
    with ExitStack() as ctx:
        LbT, LkT, X, Y, B, As = (m.sbuf(ctx, n, [P, 4, TT, P]) for n in ("LbT", "LkT", "X", "Y", "B", "As"))
        before = m.sbuf(ctx, "before", [P, P])
        masks = m.sbuf(ctx, "masks", [P, LEVELS, P])
        vp = LkT[:, 0:2]
        wide = lambda t: t.rearrange("p t i -> p (t i)")
        with nc.Block() as block:
            @block.sync
            def _(sp):
                m.clear_previous(sp)
                sp.dma_start(before[:], m.table("before")).then_inc(loaded, 16)
                sp.dma_start(masks[:].rearrange("p s t -> p (s t)"), m.table("levels")).then_inc(loaded, 16)
                m.feed(sp, 0)

            @block.tensor
            def _(pe):
                for i, lhs in enumerate((bet, khat)):
                    for h in range(4):
                        j, at = h // 2, h % 2 * HD
                        for tt in range(TT):
                            mm = pe.matmul(m.ps[:, 4 * i + h, tt * P:(tt + 1) * P],
                                           lhs[at:at + HD, j, tt * P:(tt + 1) * P],
                                           kap[at:at + HD, j, tt * P:(tt + 1) * P], start=True, stop=True)
                        mm.then_inc(l_ready, 1)
                pe.wait_ge(init, 1)
                for lv in range(LEVELS):
                    for h in range(4):
                        n = 4 * lv + h
                        pe.wait_ge(as_ready, n + 1)
                        if lv == 0:
                            pe.wait_ge(l_kept, h + 1)
                        else:
                            pe.wait_ge(x_kept, n - 3)
                        for tt in range(TT):
                            mm = pe.matmul(m.ps[:, h, tt * P:(tt + 1) * P], As[:, h, tt, :], X[:, h, tt, :],
                                           start=True, stop=True)
                        mm.then_inc(b_ready, 1)
                    for h in range(4):
                        n = 4 * lv + h
                        bank = 4 + 2 * (h % 2)
                        pe.wait_ge(b_kept, n + 1)
                        if lv:
                            pe.wait_ge(y_kept, n - 3)
                        if n >= 2:
                            pe.wait_ge(y_kept, n - 1)
                        elif n == 0:
                            pe.wait_ge(l_kept, 8)
                        for tt in range(TT):
                            pe.matmul(m.ps[:, bank, tt * P:(tt + 1) * P], Y[:, h, tt, :], B[:, h, tt, :],
                                      start=True, stop=True)
                            mm = pe.matmul(m.ps[:, bank + 1, tt * P:(tt + 1) * P], B[:, h, tt, :], Y[:, h, tt, :],
                                           start=True, stop=True)
                        mm.then_inc(xy_ready, 1)
                pe.wait_ge(y_kept, 4 * LEVELS)
                for h in range(4):
                    o = h % 2 * HD
                    for tt in range(TT):
                        mm = pe.matmul(m.ps[o:o + HD, h // 2, tt * P:(tt + 1) * P],
                                       kap_tok[:, tt, h * HD:(h + 1) * HD], Y[:, h, tt, :], start=True, stop=True)
                mm.then_inc(u_ready, 1)
                for tt in range(TT):
                    for h in range(4):
                        at = tt % 2 * GROUP + h * HD
                        mm = pe.matmul(m.ps[:, 2 + tt // 2, at:at + HD], LkT[:, h, tt, :],
                                       v_tok[:, tt, h * HD:(h + 1) * HD], start=True, stop=True)
                mm.then_inc(vp_ready, 1)
                pe.wait_ge(vp_kept, 2)
                for tt in range(TT):
                    for h in range(4):
                        at = tt % 2 * GROUP + h * HD
                        mm = pe.matmul(m.ps[:, 4 + tt // 2, at:at + HD], Y[:, h, tt, :],
                                       wide(vp[:, tt // 2])[:, at:at + HD], start=True, stop=True)
                mm.then_inc(w_ready, 1)

            @block.gpsimd
            def _(pool):
                for lv in range(LEVELS):
                    for h in range(4):
                        n = 4 * lv + h
                        if lv == 0:
                            pool.wait_ge(l_kept, h + 1)
                        else:
                            pool.wait_ge(b_ready, n - 3)
                        nc.gpsimd.tensor_tensor(As[:, h], LbT[:, h],
                                                masks[:, lv, :].unsqueeze(1).to_broadcast([P, TT, P]),
                                                ALU.mult).then_inc(as_ready, 1)

            @block.scalar
            def _(act):
                for n in range(4 * LEVELS):
                    h = n % 4
                    act.wait_ge(b_ready, n + 1)
                    if n >= 4:
                        act.wait_ge(xy_ready, n - 3)
                    act.copy(wide(B[:, h]), m.ps[:, h, :]).then_inc(b_kept, 1)
                act.wait_ge(u_ready, 1)
                act.copy(uT[:], m.ps[:, 0:2, :])

            @block.vector
            def _(dve):
                ident = m.ident[:].unsqueeze(1).to_broadcast([P, TT, P])
                for h in range(4):
                    dve.tensor_copy(X[:, h], ident)
                    ins = dve.tensor_copy(Y[:, h], ident)
                ins.then_inc(init, 1)
                dve.wait_ge(init, 1)
                dve.wait_ge(loaded, 32)
                for n in range(8):
                    dve.wait_ge(l_ready, n + 1)
                    dst = (LbT, LkT)[n // 4]
                    dve.tensor_tensor(dst[:, n % 4], m.ps[:, n, :].rearrange("p (t i) -> p t i", t=TT),
                                      before[:].unsqueeze(1).to_broadcast([P, TT, P]), ALU.mult).then_inc(l_kept, 1)
                for n in range(4 * LEVELS):
                    h = n % 4
                    bank = 4 + 2 * (h % 2)
                    dve.wait_ge(xy_ready, n + 1)
                    if n >= 4:
                        dve.wait_ge(y_kept, n - 3)
                    dve.tensor_tensor(wide(X[:, h]), wide(X[:, h]), m.ps[:, bank, :], ALU.subtract).then_inc(x_kept, 1)
                    dve.tensor_tensor(wide(Y[:, h]), wide(Y[:, h]), m.ps[:, bank + 1, :],
                                      ALU.subtract).then_inc(y_kept, 1)
                dve.wait_ge(vp_ready, 1)
                for i in range(2):
                    dve.tensor_copy(wide(vp[:, i]), m.ps[:, 2 + i, :]).then_inc(vp_kept, 1)
                dve.wait_ge(w_ready, 1)
                for i in range(2):
                    dve.tensor_copy(w[:, 2 * i:2 * i + 2, :].rearrange("p t f -> p (t f)"), m.ps[:, 4 + i, :])


def rwkv_scan(m, cols, rho, bet, khat, bet_tok, kh_tok, v_tok, uT, w, pend, gate, bonus):
    nc = m.nc
    (loaded, m_ready, m_kept, pm_ready, sa_ready, sa_kept, d_ready, s_ready, o_ready, var_ready, rs_ready, y_ready,
     y_turned, half_ready, step, *_) = m.stage()
    with ExitStack() as ctx:
        MbT, MkT = (m.sbuf(ctx, n, [P, 4, TT, P]) for n in ("MbT", "MkT"))
        upto = m.sbuf(ctx, "upto", [P, P])
        halves = m.sbuf(ctx, "halves", [P, P])
        pm = m.sbuf(ctx, "pm", [P, NC, 2, P])
        state = m.sbuf(ctx, "state", [P, NC, 2, P])
        sa = m.sbuf(ctx, "sa", [P, TT, GROUP])
        t = m.sbuf(ctx, "t", [P, 2, P])
        y = m.sbuf(ctx, "y", [P, TT, GROUP])
        yl = m.sbuf(ctx, "yl", [P, 2, SEQ])
        stats = m.sbuf(ctx, "stats", [P, TT, 4, 6])
        mv = m.sbuf(ctx, "mv", [P, TT, 4, 2])
        rs = m.sbuf(ctx, "rs", [P, TT, 4])
        half = m.sbuf(ctx, "half", [P, TT, 4])
        with nc.Block() as block:
            @block.sync
            def _(sp):
                m.clear_previous(sp)
                sp.dma_start(upto[:], m.table("upto")).then_inc(loaded, 16)
                sp.dma_start(halves[:], m.table("halves")).then_inc(loaded, 16)
                m.feed(sp, 0)

            @block.gpsimd
            def _(pool):
                nc.gpsimd.memset(half[:], -0.5).then_inc(half_ready, 1)
                pool.wait_ge(loaded, 32)
                for c in range(NC - 1):
                    nc.gpsimd.tensor_tensor(pm[:, c], halves[:].unsqueeze(1).to_broadcast([P, 2, P]),
                                            pend[:, :, c:c + 1].to_broadcast([P, 2, P]), ALU.mult).then_inc(pm_ready, 1)
                pool.wait_ge(half_ready, 1)
                pool.wait_ge(var_ready, 1)
                nc.gpsimd.tensor_tensor(rs[:], mv[:, :, :, 1], half[:], ALU.pow).then_inc(rs_ready, 1)

            @block.tensor
            def _(pe):
                for i, lhs in enumerate((bet, khat)):
                    for h in range(4):
                        j, at = h // 2, h % 2 * HD
                        if i:
                            pe.wait_ge(m_kept, h + 1)
                        for tt in range(TT):
                            mm = pe.matmul(m.ps[:, 4 + h, tt * P:(tt + 1) * P],
                                           lhs[at:at + HD, j, tt * P:(tt + 1) * P],
                                           rho[at:at + HD, j, tt * P:(tt + 1) * P], start=True, stop=True)
                        mm.then_inc(m_ready, 1)
                for c in range(NC):
                    o, tt = c % 2 * CH, c // 2
                    pe.wait_ge(s_ready, c + 1)
                    if c >= 2:
                        pe.wait_ge(sa_kept, c - 1)
                    for j in range(2):
                        mm = pe.matmul(m.ps[o:o + CH, c % 2, j * P:(j + 1) * P], uT[:, j, c * CH:(c + 1) * CH],
                                       state[:, c, j, :], start=True, stop=True)
                    mm.then_inc(sa_ready, 1)
                    if c < NC - 1:
                        pe.wait_ge(sa_kept, c + 1)
                        for j in range(2):
                            f = slice(j * P, (j + 1) * P)
                            pe.matmul(m.ps[:, 2 + c % 2, f], kh_tok[o:o + CH, tt, f], v_tok[o:o + CH, tt, f],
                                      start=True, stop=False)
                            mm = pe.matmul(m.ps[:, 2 + c % 2, f], bet_tok[o:o + CH, tt, f], sa[o:o + CH, tt, f],
                                           start=False, stop=True)
                        mm.then_inc(d_ready, 1)
                pe.wait_ge(sa_kept, NC)
                pe.wait_ge(m_kept, 8)
                for tt in range(TT):
                    for h in range(4):
                        f = slice(h * HD, (h + 1) * HD)
                        pe.matmul(m.ps[:, 4 + tt, f], MbT[:, h, tt, :], sa[:, tt, f], start=(h == 0), stop=False,
                                  skip_group_check=True)
                        pe.matmul(m.ps[:, 4 + tt, f], MkT[:, h, tt, :], v_tok[:, tt, f], start=False, stop=False,
                                  skip_group_check=True)
                    for c in (2 * tt, 2 * tt + 1):
                        o = c % 2 * CH
                        for j in range(2):
                            mm = pe.matmul(m.ps[o:o + CH, 4 + tt, j * P:(j + 1) * P], rho[:, j, c * CH:(c + 1) * CH],
                                           state[:, c, j, :], start=False, stop=(j == 1), skip_group_check=True)
                    mm.then_inc(o_ready, 1)
                for tt in range(TT):
                    pe.wait_ge(y_ready, tt + 1)
                    for j in range(2):
                        mm = pe.transpose(m.ps[:, j, tt * P:(tt + 1) * P], y[:, tt, j * P:(j + 1) * P], m.ident[:])
                    mm.then_inc(y_turned, 1)

            @block.vector
            def _(dve):
                do = Step(dve, step)
                dve.memset(state[:, 0], 0.0).then_inc(s_ready, 1)
                dve.wait_ge(s_ready, 1)
                dve.wait_ge(loaded, 32)
                for n in range(8):
                    dve.wait_ge(m_ready, n + 1)
                    dst = (MbT, MkT)[n // 4]
                    dve.tensor_tensor(dst[:, n % 4], m.ps[:, 4 + n % 4, :].rearrange("p (t i) -> p t i", t=TT),
                                      upto[:].unsqueeze(1).to_broadcast([P, TT, P]), ALU.mult).then_inc(m_kept, 1)
                for c in range(NC):
                    o, tt = c % 2 * CH, c // 2
                    dve.wait_ge(sa_ready, c + 1)
                    dve.scalar_tensor_tensor(sa[o:o + CH, tt, :], m.ps[o:o + CH, c % 2, 0:GROUP], -1.0,
                                             w[o:o + CH, tt, :], ALU.mult, ALU.subtract).then_inc(sa_kept, 1)
                    if c < NC - 1:
                        dve.wait_ge(d_ready, c + 1)
                        do(dve.tensor_tensor(t[:].rearrange("p j v -> p (j v)"), m.ps[:, 2 + c % 2, 0:GROUP],
                                             state[:, c].rearrange("p j v -> p (j v)"), ALU.add))
                        dve.wait_ge(pm_ready, c + 1)
                        dve.tensor_tensor(state[:, c + 1], t[:], pm[:, c], ALU.mult).then_inc(s_ready, 1)
                        dve.wait_ge(s_ready, c + 2)
                group_norm_rows(m, dve, do, 4, o_ready, y, stats, mv, LNX_EPS, var_ready, rs_ready, rs, y_ready)
                dve.wait_ge(y_turned, TT)
                for j in range(2):
                    do(dve.tensor_scalar(yl[:, j, :], m.ps[:, j, :], cols[:, C_LG + j:C_LG + j + 1],
                                         cols[:, C_LB + j:C_LB + j + 1], ALU.mult, ALU.add))
                do(dve.tensor_tensor(yl[:], yl[:], bonus[:], ALU.add))
                dve.tensor_tensor(m.mixT[:, 4:6, :], yl[:], gate[:], ALU.mult)


def group_norm_rows(m, dve, do, bank, o_ready, y, stats, mv, eps, var_ready, rs_ready, rs, y_ready):
    for tt in range(TT):
        dve.wait_ge(o_ready, tt + 1)
        do(dve.tensor_copy(y[:, tt, :], m.ps[:, bank + tt, 0:GROUP]))
        for h in range(4):
            do(dve.bn_stats(stats[:, tt, h, :], y[:, tt, h * HD:(h + 1) * HD]))
            do(dve.bn_aggr(mv[:, tt, h, :], stats[:, tt, h, :]))
    dve.tensor_scalar(mv[:, :, :, 1], mv[:, :, :, 1], eps, None, ALU.add).then_inc(var_ready, 1)
    dve.wait_ge(rs_ready, 1)
    for tt in range(TT):
        y3 = y[:, tt, :].rearrange("p (h d) -> p h d", h=4)
        do(dve.tensor_tensor(y3, y3, mv[:, tt, :, 0:1].to_broadcast([P, 4, HD]), ALU.subtract))
        dve.tensor_tensor(y3, y3, rs[:, tt, :].unsqueeze(2).to_broadcast([P, 4, HD]), ALU.mult).then_inc(y_ready, 1)


def rwkv_mixer(m, l, A, cols):
    with ExitStack() as ctx:
        rho, kap, bet, khat, gate, bonus = (m.sbuf(ctx, "rw_" + n, [P, 2, SEQ])
                                            for n in ("rho", "kap", "bet", "khat", "gate", "bonus"))
        kap_tok, bet_tok, kh_tok, v_tok = (m.sbuf(ctx, "rw_" + n, [P, TT, GROUP])
                                           for n in ("kap_tok", "bet_tok", "kh_tok", "v_tok"))
        pend = m.sbuf(ctx, "rw_pend", [P, 2, NC])
        with ExitStack() as c2:
            mixed = m.sbuf(c2, "rw_mixed", [P, 9, SEQ])
            rwkv_project(m, mixed, cols)
            rwkv_prepare(m, l, A, cols, mixed, rho, kap, bet, khat, gate, bonus, pend)
            turn_stage(m, [(kap, kap_tok), (bet, bet_tok), (khat, kh_tok), (mixed[:, 4:6], v_tok)])
        uT = m.sbuf(ctx, "rw_uT", [P, 2, SEQ])
        w = m.sbuf(ctx, "rw_w", [P, TT, GROUP])
        rwkv_inverse(m, kap, bet, khat, kap_tok, v_tok, uT, w)
        rwkv_scan(m, cols, rho, bet, khat, bet_tok, kh_tok, v_tok, uT, w, pend, gate, bonus)


def angles_stage(m, A, cos, sin):
    nc = m.nc
    loaded, step, ready, *_ = m.stage()
    MAGIC = 1.5 * 2.0 ** 23
    C1 = 6.28125
    C2 = float(np.float32(TWO_PI - C1))
    C3 = float(TWO_PI - C1 - C2)
    PI = 3.1415925
    with ExitStack() as ctx:
        pos_i = m.sbuf(ctx, "pos_i", [P, TT], I32)
        pos = m.sbuf(ctx, "pos", [P, TT])
        freq = m.sbuf(ctx, "freq", [P, 32])
        x, n, c = (m.sbuf(ctx, s, [P, TT, 32]) for s in ("x", "n", "c"))
        with nc.Block() as block:
            @block.sync
            def _(sp):
                m.clear_previous(sp)
                with nc.allow_non_contiguous_dma(reason="512 numbers, one for each token's partition"):
                    sp.dma_start(pos_i[:], A["positions_2"][0].rearrange("(t p) -> p t", p=P)).then_inc(loaded, 16)
                sp.dma_start(freq[:], m.table("inv_freq")).then_inc(loaded, 16)
                m.feed(sp, 0)

            @block.vector
            def _(dve):
                do = Step(dve, step)
                dve.wait_ge(loaded, 32)
                do(dve.tensor_copy(pos[:], pos_i[:]))
                for tt in range(TT):
                    do(dve.tensor_scalar(x[:, tt, :], freq[:], pos[:, tt:tt + 1], None, ALU.mult))
                do(dve.tensor_scalar(n[:], x[:], 1.0 / TWO_PI, None, ALU.mult))
                do(dve.tensor_scalar(n[:], n[:], MAGIC, None, ALU.add))
                do(dve.tensor_scalar(n[:], n[:], MAGIC, None, ALU.subtract))
                for k in (C1, C2, C3):
                    do(dve.scalar_tensor_tensor(x[:], n[:], -k, x[:], ALU.mult, ALU.add))
                do(dve.tensor_scalar(c[:], x[:], float(np.pi / 2), None, ALU.add))
                do(dve.tensor_scalar(n[:], c[:], float(np.pi), None, ALU.is_gt))
                do(dve.scalar_tensor_tensor(c[:], n[:], -TWO_PI, c[:], ALU.mult, ALU.add))
                do(dve.tensor_scalar(c[:], c[:], PI, -PI, ALU.min, ALU.max))
                dve.tensor_scalar(x[:], x[:], PI, -PI, ALU.min, ALU.max).then_inc(ready, 1)

            @block.scalar
            def _(act):
                act.wait_ge(ready, 1)
                act.activation(sin[:], x[:], ACT.Sin)
                act.activation(cos[:], c[:], ACT.Sin)


def ret_mixer(m, A):
    nc = m.nc
    with ExitStack() as ctx:
        qk = m.sbuf(ctx, "re_qk", [P, TT, 512])
        rot = m.sbuf(ctx, "re_rot", [P, TT, 512])
        qkT = m.sbuf(ctx, "re_qkT", [P, 4, SEQ])
        gate = m.sbuf(ctx, "re_gate", [P, 2, SEQ])
        v = m.sbuf(ctx, "re_v", [P, TT, GROUP])
        cos, sin = (m.sbuf(ctx, n, [P, TT, 32]) for n in ("cos", "sin"))
        decay = m.sbuf(ctx, "decay", [P, 4, SEQ])
        tmp = m.sbuf(ctx, "re_tmp", [P, 8, 32])
        scores = m.sbuf(ctx, "re_scores", [P, 2, TT, SEQ])
        y = m.sbuf(ctx, "re_y", [P, TT, GROUP])
        stats = m.sbuf(ctx, "stats", [P, TT, 4, 6])
        mv = m.sbuf(ctx, "mv", [P, TT, 4, 2])
        rs = m.sbuf(ctx, "rs", [P, TT, 4])
        half = m.sbuf(ctx, "half", [P, TT, 4])
        angles_stage(m, A, cos, sin)
        (loaded, tok_ready, tok_kept, tile_ready, tile_kept, rot_ready, turned, turn_kept, half_ready, *_) = m.stage()
        with nc.Block() as block:
            @block.sync
            def _(sp):
                m.clear_previous(sp)
                m.feed(sp, 2)

            @block.tensor
            def _(pe):
                project_tok(m, pe, m.take(pe, KT), m.hT, (0, 512), (4, 5, 6, 7), 0, tok_ready, tok_kept)
                released(m, pe, tok_ready, 4)
                w = m.take(pe, KT)
                project_tok(m, pe, w, m.hT, (0, GROUP), (4, 5, 6, 7), 4, tok_ready, tok_kept)
                project_cols(m, pe, w, [(GROUP, GROUP + P), (GROUP + P, 512)], (0, 1), 0, tile_ready, tile_kept)
                released(m, pe, tile_ready, 2)
                for tt in range(TT):
                    pe.wait_ge(rot_ready, tt + 1)
                    if tt >= 2:
                        pe.wait_ge(turn_kept, tt - 1)
                    for j in range(4):
                        mm = pe.transpose(m.ps[:, 2 + tt % 2, j * P:(j + 1) * P], rot[:, tt, j * P:(j + 1) * P],
                                          m.ident[:])
                    mm.then_inc(turned, 1)

            @block.scalar
            def _(act):
                for n in range(2):
                    act.wait_ge(tile_ready, n + 1)
                    act.activation(gate[:, n, :], m.ps[:, n, :], ACT.Silu).then_inc(tile_kept, 1)
                for tt in range(TT):
                    act.wait_ge(turned, tt + 1)
                    act.copy(qkT[:, :, tt * P:(tt + 1) * P],
                             m.ps[:, 2 + tt % 2, :].rearrange("p (j t) -> p j t", j=4)).then_inc(turn_kept, 1)

            @block.vector
            def _(dve):
                do = Step(dve, half_ready)
                for tt in range(TT):
                    dve.wait_ge(tok_ready, tt + 1)
                    dve.tensor_copy(qk[:, tt, :], m.ps[:, 4 + tt, :]).then_inc(tok_kept, 1)
                dve.wait_ge(tok_kept, 4)
                for tt in range(TT):
                    s = qk[:, tt, :].rearrange("p (h o e) -> p h o e", o=2, e=32)
                    d = rot[:, tt, :].rearrange("p (h o e) -> p h o e", o=2, e=32)
                    c = cos[:, tt].unsqueeze(1).to_broadcast([P, 8, 32])
                    n_ = sin[:, tt].unsqueeze(1).to_broadcast([P, 8, 32])
                    do(dve.tensor_tensor(d[:, :, 0], s[:, :, 0], c, ALU.mult))
                    do(dve.tensor_tensor(tmp[:], s[:, :, 1], n_, ALU.mult))
                    do(dve.tensor_tensor(d[:, :, 0], d[:, :, 0], tmp[:], ALU.subtract))
                    do(dve.tensor_tensor(d[:, :, 1], s[:, :, 0], n_, ALU.mult))
                    do(dve.tensor_tensor(tmp[:], s[:, :, 1], c, ALU.mult))
                    ins = dve.tensor_tensor(d[:, :, 1], d[:, :, 1], tmp[:], ALU.add)
                    ins.then_inc(rot_ready, 1)
                    dve.wait_ge(rot_ready, tt + 1)
                for tt in range(TT):
                    dve.wait_ge(tok_ready, 5 + tt)
                    dve.tensor_copy(v[:, tt, :], m.ps[:, 4 + tt, 0:GROUP]).then_inc(tok_kept, 1)

        (loaded, s_ready, s_kept, o_ready, var_ready, rs_ready, y_ready, y_turned, half_ready, step, *_) = m.stage()
        with nc.Block() as block:
            @block.sync
            def _(sp):
                m.clear_previous(sp)
                sp.dma_start(decay[:], m.decay).then_inc(loaded, 16)
                m.feed(sp, 0)

            @block.gpsimd
            def _(pool):
                nc.gpsimd.memset(half[:], -0.5).then_inc(half_ready, 1)
                pool.wait_ge(half_ready, 1)
                pool.wait_ge(var_ready, 1)
                nc.gpsimd.tensor_tensor(rs[:], mv[:, :, :, 1], half[:], ALU.pow).then_inc(rs_ready, 1)

            @block.tensor
            def _(pe):
                for h in range(5):
                    if h < 4:
                        j, at = h // 2, h % 2 * HD
                        for J in range(TT):
                            n = 4 * h + J
                            if h:
                                pe.wait_ge(s_kept, n - 3)
                            pe.matmul(m.ps[:, J, J * P:], qkT[at:at + HD, 2 + j, J * P:(J + 1) * P],
                                      qkT[at:at + HD, j, J * P:], start=True, stop=True).then_inc(s_ready, 1)
                    if h:
                        g = h - 1
                        for tt in range(TT):
                            pe.wait_ge(s_kept, 4 * g + tt + 1)
                            for J in range(tt + 1):
                                mm = pe.matmul(m.ps[:, 4 + tt, g * HD:(g + 1) * HD],
                                               scores[:, g % 2, J, tt * P:(tt + 1) * P],
                                               v[:, J, g * HD:(g + 1) * HD], start=(J == 0), stop=(J == tt))
                            mm.then_inc(o_ready, 1)
                for tt in range(TT):
                    pe.wait_ge(y_ready, tt + 1)
                    for j in range(2):
                        mm = pe.transpose(m.ps[:, j, tt * P:(tt + 1) * P], y[:, tt, j * P:(j + 1) * P], m.ident[:])
                    mm.then_inc(y_turned, 1)

            @block.vector
            def _(dve):
                do = Step(dve, step)
                dve.wait_ge(loaded, 16)
                for h in range(4):
                    for J in range(TT):
                        dve.wait_ge(s_ready, 4 * h + J + 1)
                        if h >= 2:
                            dve.wait_ge(o_ready, 4 * (h - 1))
                        dve.scalar_tensor_tensor(scores[:, h % 2, J, J * P:], m.ps[:, J, J * P:], HD ** -0.5,
                                                 decay[:, h, 0:SEQ - J * P], ALU.mult, ALU.mult).then_inc(s_kept, 1)
                dve.wait_ge(o_ready, 12)
                for tt in range(TT):
                    dve.wait_ge(o_ready, 13 + tt)
                    do(dve.tensor_copy(y[:, tt, :], m.ps[:, 4 + tt, 0:GROUP]))
                    for h in range(4):
                        do(dve.bn_stats(stats[:, tt, h, :], y[:, tt, h * HD:(h + 1) * HD]))
                        do(dve.bn_aggr(mv[:, tt, h, :], stats[:, tt, h, :]))
                dve.tensor_scalar(mv[:, :, :, 1], mv[:, :, :, 1], LN_EPS, None, ALU.add).then_inc(var_ready, 1)
                dve.wait_ge(rs_ready, 1)
                for tt in range(TT):
                    y3 = y[:, tt, :].rearrange("p (h d) -> p h d", h=4)
                    do(dve.tensor_tensor(y3, y3, mv[:, tt, :, 0:1].to_broadcast([P, 4, HD]), ALU.subtract))
                    dve.tensor_tensor(y3, y3, rs[:, tt, :].unsqueeze(2).to_broadcast([P, 4, HD]),
                                      ALU.mult).then_inc(y_ready, 1)
                dve.wait_ge(y_turned, TT)
                for j in range(2):
                    dve.tensor_tensor(m.mixT[:, 6 + j, :], m.ps[:, j, :], gate[:, j, :], ALU.mult)


def swiglu_stage(m, sizes, weight=None):
    nc = m.nc
    (gu_ready, g_kept, hid_ready, d_ready, d_kept, loaded, *_) = m.stage()
    with ExitStack() as ctx:
        silu = m.sbuf(ctx, "silu", [P, 2, SEQ])
        hid = m.sbuf(ctx, "hid", [P, 2, 4, SEQ])
        with nc.Block() as block:
            @block.sync
            def _(sp):
                m.clear_previous(sp)
                m.feed(sp, 3 * len(sizes))

            @block.tensor
            def _(pe):
                n = 0
                for gi, size in enumerate(sizes):
                    wg, wu = m.take(pe, KT), m.take(pe, KT)
                    for i in range(size):
                        if n >= 2:
                            pe.wait_ge(hid_ready, n - 1)
                        for bank, w in ((n % 2, wg), (2 + n % 2, wu)):
                            for j in range(KT):
                                mm = pe.matmul(m.ps[:, bank, :], w[:, j, i * P:(i + 1) * P], m.hT[:, j, :],
                                               start=(j == 0), stop=(j == KT - 1))
                        mm.then_inc(gu_ready, 1)
                        n += 1
                    released(m, pe, gu_ready, n)
                    pe.sem_inc(m.slots_used, 1)
                    wd = m.take(pe, size)
                    pe.wait_ge(hid_ready, n)
                    for q in range(2 * TT):
                        tt, nh = divmod(q, 2)
                        dn = 8 * gi + q
                        if dn >= 4:
                            pe.wait_ge(d_kept, dn - 3)
                        for i in range(size):
                            mm = pe.matmul(m.ps[:, 4 + dn % 4, :], hid[:, gi % 2, i, tt * P:(tt + 1) * P],
                                           wd[:, i, nh * 512:(nh + 1) * 512], start=(i == 0), stop=(i == size - 1))
                        mm.then_inc(d_ready, 1)
                    released(m, pe, d_ready, 8 * (gi + 1))

            @block.scalar
            def _(act):
                for n in range(sum(sizes)):
                    act.wait_ge(gu_ready, n + 1)
                    if n >= 2:
                        act.wait_ge(hid_ready, n - 1)
                    act.activation(silu[:, n % 2, :], m.ps[:, n % 2, :], ACT.Silu).then_inc(g_kept, 1)

            @block.vector
            def _(dve):
                n = 0
                for gi, size in enumerate(sizes):
                    for i in range(size):
                        dve.wait_ge(g_kept, n + 1)
                        if i == 0 and gi >= 2:
                            dve.wait_ge(d_ready, 8 * (gi - 1))
                        dve.tensor_tensor(hid[:, gi % 2, i, :], m.ps[:, 2 + n % 2, :], silu[:, n % 2, :],
                                          ALU.mult).then_inc(hid_ready, 1)
                        n += 1
                    for q in range(2 * TT):
                        tt, nh = divmod(q, 2)
                        dn = 8 * gi + q
                        dve.wait_ge(d_ready, dn + 1)
                        if gi:
                            dve.wait_ge(d_kept, dn - 7)
                        h = m.h[:, tt, nh * 512:(nh + 1) * 512]
                        if weight is None:
                            dve.tensor_tensor(h, h, m.ps[:, 4 + dn % 4, :], ALU.add).then_inc(d_kept, 1)
                        else:
                            dve.scalar_tensor_tensor(h, m.ps[:, 4 + dn % 4, :], weight(tt), h, ALU.mult,
                                                     ALU.add).then_inc(d_kept, 1)


def swiglu_plan(wg, wu, wd, tiles):
    plan, sizes, t = [], [], 0
    while t < tiles:
        n = min(4, tiles - t)
        lo, hi = t * P, (t + n) * P
        plan += [rows_chunk(wg, (lo, hi)), rows_chunk(wu, (lo, hi)), rows_chunk(wd[lo:hi], (0, D), n)]
        sizes.append(n)
        t += n
    return plan, sizes


def dense_ffn(m, A):
    plan, sizes = swiglu_plan(A["ffn_w_gate_2"][0], A["ffn_w_up_2"][0], A["ffn_w_down_2"][0], FFN // P)
    m.plan = plan
    h = m.h[:].rearrange("p t d -> p (t d)")
    scale_stage(m, h, h, ALPHA)
    swiglu_stage(m, sizes)
    end_ring_stage(m)


def router_stage(m, A, gates):
    nc = m.nc
    loaded, ready, shifted, ex_ready, step, *_ = m.stage()
    E = EXPERTS
    with ExitStack() as ctx:
        w = m.sbuf(ctx, "router", [P, KT, E])
        lg, p, pick, t, iota = (m.sbuf(ctx, n, [P, TT, E]) for n in ("lg", "p", "pick", "t", "iota"))
        first = m.sbuf(ctx, "first", [P, TT, E])
        mx, s = (m.sbuf(ctx, n, [P, TT]) for n in ("mx", "s"))
        wide = lambda c: c[:].unsqueeze(2).to_broadcast([P, TT, E])
        with nc.Block() as block:
            @block.sync
            def _(sp):
                m.clear_previous(sp)
                sp.dma_start(w[:], A["moe_router_2"][0].rearrange("(k p) e -> p k e", p=P)).then_inc(loaded, 16)

            @block.tensor
            def _(pe):
                pe.wait_ge(loaded, 16)
                for tt in range(TT):
                    for j in range(KT):
                        mm = pe.matmul(m.ps[:, 0, tt * E:(tt + 1) * E], m.hT[:, j, tt * P:(tt + 1) * P], w[:, j, :],
                                       start=(j == 0), stop=(j == KT - 1))
                mm.then_inc(ready, 1)

            @block.scalar
            def _(act):
                act.wait_ge(shifted, 1)
                act.activation(p[:], lg[:], ACT.Exp).then_inc(ex_ready, 1)

            @block.vector
            def _(dve):
                do = Step(dve, step)
                h = m.h[:].rearrange("p t d -> p (t d)")
                do(dve.tensor_scalar(h, h, ALPHA, None, ALU.mult))
                for e in range(E):
                    do(dve.memset(iota[:, :, e:e + 1], float(e)))
                dve.wait_ge(ready, 1)
                do(dve.tensor_copy(lg[:].rearrange("p t e -> p (t e)"), m.ps[:, 0, 0:TT * E]))
                do(dve.reduce_max(mx[:], lg[:], AX.X))
                dve.tensor_tensor(lg[:], lg[:], wide(mx), ALU.subtract).then_inc(shifted, 1)
                dve.wait_ge(ex_ready, 1)
                do(dve.reduce_sum(s[:], p[:], AX.X))
                do(dve.reciprocal(s[:], s[:]))
                do(dve.tensor_tensor(p[:], p[:], wide(s), ALU.mult))
                do(dve.tensor_copy(lg[:], p[:]))
                for k in range(2):
                    do(dve.reduce_max(mx[:], lg[:], AX.X))
                    do(dve.tensor_tensor(t[:], lg[:], wide(mx), ALU.is_equal))
                    do(dve.tensor_scalar(pick[:], t[:], -float(E), float(E), ALU.mult, ALU.add))
                    do(dve.tensor_tensor(pick[:], pick[:], iota[:], ALU.add))
                    do(dve.tensor_reduce(s[:], pick[:], AX.X, ALU.min))
                    do(dve.tensor_tensor(t[:], iota[:], wide(s), ALU.is_equal))
                    if k == 0:
                        do(dve.tensor_copy(first[:], t[:]))
                        do(dve.scalar_tensor_tensor(lg[:], t[:], -2.0, lg[:], ALU.mult, ALU.add))
                do(dve.tensor_tensor(t[:], t[:], first[:], ALU.add))
                do(dve.tensor_tensor(p[:], p[:], t[:], ALU.mult))
                do(dve.reduce_sum(s[:], p[:], AX.X))
                do(dve.reciprocal(s[:], s[:]))
                dve.tensor_tensor(gates[:], p[:], wide(s), ALU.mult)


def pick_gate_stage(m, gate, gates, e):
    nc = m.nc
    m.stage()
    with nc.Block() as block:
        @block.sync
        def _(sp):
            m.clear_previous(sp)
            m.feed(sp, 0)

        @block.vector
        def _(dve):
            dve.tensor_copy(gate[:], gates[:, :, bass.ds(e, 1)])


def moe_ffn(m, A):
    nc = m.nc
    with ExitStack() as ctx:
        gates = m.sbuf(ctx, "gates", [P, TT, EXPERTS])
        gate = m.sbuf(ctx, "gate", [P, TT, 1])
        router_stage(m, A, gates)
        turn = m.turn
        with nc.Fori(0, EXPERTS) as e:
            one = lambda w: w[0, bass.ds(e, 1)].rearrange("a r c -> (a r) c")
            m.plan, sizes = swiglu_plan(one(A["moe_w_gate_2"]), one(A["moe_w_up_2"]), one(A["moe_w_down_2"]),
                                        FFN_E // P)
            pick_gate_stage(m, gate, gates, e)
            swiglu_stage(m, sizes, lambda tt: gate[:, tt, :])
            end_ring_stage(m)
            idle_stage(m)
            assert m.turn == turn


def second_block_layer(m, l, A, out):
    w_in = A["w_in_2"][l]
    c = lambda lo, n=512: rows_chunk(w_in, (lo, lo + n))
    m.plan = [c(HGRN), c(HGRN + 512), c(GLA), c(GLA + 512, 272), c(RWKV), c(RWKV + 512), c(RWKV + D, 32),
              c(RET), c(RET + 512), rows_chunk(A["w_out_2"][l], (0, 512)), rows_chunk(A["w_out_2"][l], (512, D))]
    with ExitStack() as ctx:
        cols = m.sbuf(ctx, "cols", [P, C_N])
        lb = m.sbuf(ctx, "lb", [P, 4])
        params_stage(m, l, A, cols, lb)
        hgrn_mixer(m, cols, lb)
        gla_mixer(m, l, A, cols)
        rwkv_mixer(m, l, A, cols)
        ret_mixer(m, A)
    out_stage(m, None)
    end_ring_stage(m)
    norm_stage(m, A["ln1_g_2"][l], A["ln1_b_2"][l])
    if l % 2 == 0:
        dense_ffn(m, A)
    else:
        moe_ffn(m, A)
    norm_stage(m, A["ln2_g_2"][l], A["ln2_b_2"][l], store=out)


def build_program(nc, A, out, tables, decay):
    A = dict(A)
    A["rpb_pad"] = nc.dram_tensor("rpb_pad", [HEADS, 15, 2 * GRID_W - 1], F32, kind="Internal").ap()
    with ExitStack() as ctx:
        m = Machine(nc, ctx, tables)
        m.decay = decay
        first_load_stage(m, A["x"][0])
        norm_stage(m, A["ln_in_g"], A["ln_in_b"])
        turn = m.turn
        with nc.Fori(0, DEPTH) as l:
            first_block_layer(m, l, A)
            if m.turn != turn:
                idle_stage(m)
        persist2(m, ctx)
        for l in range(DEPTH):
            second_block_layer(m, l, A, out[0] if l == DEPTH - 1 else None)


_INS = ["x", "ln_in_g", "ln_in_b", "w_in", "b_in", "na_rpb", "q_norm_g", "k_norm_g", "sg_ln_g", "sg_ln_b", "sg_w",
        "sg_b", "w_br_a", "w_br_b", "w_br_c", "w_out", "b_out", "ln_post_g", "ln_post_b", "positions_2", "w_in_2",
        "w_out_2", "ln1_g_2", "ln1_b_2", "ln2_g_2", "ln2_b_2", "hgrn_lb_logits_2", "hgrn_norm_g_2", "gla_gate_w2_2",
        "gla_gate_b_2", "gla_norm_g_2", "rwkv_mu_2", "rwkv_w0_2", "rwkv_w2_2", "rwkv_a0_2", "rwkv_a2_2",
        "rwkv_g2_2", "rwkv_k_k_2", "rwkv_k_a_2", "rwkv_r_k_2", "rwkv_lnx_g_2", "rwkv_lnx_b_2", "rwkv_v0_2",
        "rwkv_v1_2", "rwkv_v2_2", "ffn_w_gate_2", "ffn_w_up_2", "ffn_w_down_2", "moe_router_2", "moe_w_gate_2",
        "moe_w_up_2", "moe_w_down_2"]


def kernel(**inputs):
    import concourse.bacc as _bacc
    from concourse import mybir as _mybir
    from concourse.bass_utils import run_bass_kernel_spmd as _run

    nc = _bacc.Bacc("TRN2", target_bir_lowering=False, num_devices=1)
    arrays, args = {}, {}

    def given(name, a):
        a = np.ascontiguousarray(a)
        arrays[f"in_{name}"] = a
        return nc.dram_tensor(f"in_{name}", a.shape, _mybir.dt.from_np(a.dtype), kind="ExternalInput").ap()

    for name in _INS:
        args[name] = given(name, inputs[name])
    tables, decay = given("tables", make_tables()), given("decay", make_decay_table())
    out = nc.dram_tensor("out_0", (1, SEQ, D), F32, kind="ExternalOutput").ap()
    build_program(nc, args, out, tables, decay)
    r = _run(nc, [arrays], core_ids=[0])
    return r.results[0]["out_0"]
```

```python
from contextlib import ExitStack

import numpy as np

import concourse.bass as bass
from concourse import mybir

P = 128
F32 = mybir.dt.float32
F32R = mybir.dt.float32r
I32 = mybir.dt.int32
ALU = mybir.AluOpType
ACT = mybir.ActivationFunctionType
AX = mybir.AxisListType

SEQ, D = 512, 1024
TT = SEQ // P
KT = D // P
DEPTH = 2
HD = 64
ALPHA = (2.0 * DEPTH) ** 0.25
LN_EPS = 1e-5
RMS_EPS = 1e-6
PARTS_SLOT = 2 * D
RING = 3
SLOT = 4 * D
WARM_UP = 4
RAW = 3
SPLIT = 2

NA_Q, NA_K, NA_V, NA_Z, GQ_Q, GQ_KV, GQ_Z = 0, 512, 1024, 1536, 2048, 2560, 2816
SG_U, SG_V, SG_Z, GATES, IN_WIDTH = 3328, 3840, 4352, 4864, 7936
GRID_W, NA_KW, HEADS = 64, 16, 8

TABLES = {}


def make_tables():
    parts, at = [], 0

    def put(name, a):
        nonlocal at
        a = np.asarray(a, np.float32).reshape(P, -1)
        TABLES[name] = (at, a.shape[1])
        parts.append(a)
        at += a.shape[1]

    i = np.arange(P)
    put("ident", np.eye(P))
    tok = np.arange(SEQ)
    freqs = (np.float32(10000.0) ** (-np.arange(0, 32, 2, dtype=np.float32) / np.float32(32))).astype(np.float32)
    ang = np.concatenate([(tok // GRID_W).astype(np.float32)[:, None] * freqs,
                          (tok % GRID_W).astype(np.float32)[:, None] * freqs], -1).astype(np.float32)
    for name, f in (("rope_cos", np.cos), ("rope_sin", np.sin)):
        put(name, f(ang).astype(np.float32).reshape(TT, P, 32).transpose(1, 0, 2))
    c = np.arange(GRID_W)
    start = np.clip(c - NA_KW // 2, 0, GRID_W - NA_KW)
    ok = (c[None] >= start[:, None]) & (c[None] < start[:, None] + NA_KW)
    put("window", np.tile(np.where(ok, 0.0, -1e30), (2, 1)))
    put("halves", (i[:, None] // HD == i[None] // HD))
    put("quarters", i[:, None] // 32 == np.arange(256)[None] // HD)
    same = i[:, None] // HD == i[None] // HD
    put("before", same & (i[:, None] < i[None]))
    put("upto", same & (i[:, None] <= i[None]))
    lv = [(i[:, None] // (2 * s) == i[None] // (2 * s)) & (i[:, None] // s % 2 == 0) & (i[None] // s % 2 == 1)
          for s in (1, 2, 4, 8, 16, 32)]
    put("levels", np.stack(lv, 1))
    put("keep", np.tile((tok % HD != 0)[None], (P, 1)))
    inv = (np.float32(10000.0) ** (-np.arange(32, dtype=np.float32) / np.float32(32))).astype(np.float32)
    put("inv_freq", np.tile(inv[None], (P, 1)))
    return np.concatenate(parts, 1)


def make_decay_table():
    gamma = np.log(1.0 - 2.0 ** (-5.0 - np.arange(4, dtype=np.float64)))
    rel = np.arange(SEQ)[None] - np.arange(P)[:, None]
    d = np.where(rel[:, None, :] >= 0, np.exp(np.maximum(rel, 0)[:, None, :] * gamma[None, :, None]), 0.0)
    return d.astype(np.float32)


class Step:

    def __init__(self, eng, sem):
        self.eng, self.sem, self.n = eng, sem, 0

    def __call__(self, ins):
        self.n += 1
        ins.then_inc(self.sem, 1)
        self.eng.wait_ge(self.sem, self.n)


class Machine:

    def __init__(self, nc, ctx, tables):
        self.nc, self.ctx, self.tables = nc, ctx, tables
        self.sets = [[ctx.enter_context(nc.semaphore(f"set{k}_{i}")) for i in range(28)] for k in range(2)]
        self.turn = 0
        self.raw_landed = [ctx.enter_context(nc.semaphore(f"raw_landed{i}")) for i in range(RAW)]
        self.hi_ready = ctx.enter_context(nc.semaphore("hi_ready"))
        self.lo_ready = ctx.enter_context(nc.semaphore("lo_ready"))
        self.parts_used = ctx.enter_context(nc.semaphore("parts_used"))
        self.out_stored = ctx.enter_context(nc.semaphore("out_stored"))
        self.slot_landed = [ctx.enter_context(nc.semaphore(f"slot_landed{i}")) for i in range(RING)]
        self.slots_used = ctx.enter_context(nc.semaphore("slots_used"))
        self.ps = ctx.enter_context(nc.psum_tensor("ps", [P, 8, 512], F32))
        self.ident = self.sbuf(ctx, "ident", [P, P])
        self.h = self.sbuf(ctx, "h", [P, TT, D])
        self.start_plan([])

    def first_block_buffers(self, ctx):
        self.xT = self.sbuf(ctx, "xT", [P, 2, KT, SEQ], F32R)
        self.mixT = self.sbuf(ctx, "mixT", [P, KT, SEQ])
        self.raw = self.sbuf(ctx, "raw", [P, RAW, PARTS_SLOT])
        self.split = self.sbuf(ctx, "split", [P, SPLIT, 2, PARTS_SLOT], F32R)

    def second_block_buffers(self, ctx):
        self.hT = self.sbuf(ctx, "hT", [P, KT, SEQ])
        self.v_first = self.sbuf(ctx, "v_first", [P, 2, SEQ])

    def mixer_buffers(self, ctx):
        self.mixT = self.sbuf(ctx, "mixT", [P, KT, SEQ])
        self.ring = self.sbuf(ctx, "ring", [P, RING, SLOT])

    def sbuf(self, ctx, name, shape, dt=F32):
        return ctx.enter_context(self.nc.sbuf_tensor(f"{name}_{self.nc.next_id()}", shape, dt))

    def stage(self):
        self.turn ^= 1
        return self.sets[self.turn]

    def clear_previous(self, sp):
        nums = [s.num for s in self.sets[self.turn ^ 1]]
        sp.sem_clear(range(min(nums), max(nums) + 1))

    def table(self, name):
        at, n = TABLES[name]
        return self.tables[:, at:at + n]

    def start_plan(self, plan):
        self.plan, self.fed, self.hid, self.lod, self.taken, self.released_to = plan, 0, 0, 0, 0, 0

    def feed_parts(self, sp, n, splitting=True):
        self.began, self.released_to = self.released_to, self.released_to + n
        self.parts_room = self.released_to + SPLIT - (1 if n else 0) if splitting else 0
        end = min(len(self.plan), self.parts_room + RAW)
        for c in range(self.fed, end):
            if c >= RAW:
                sp.wait_ge(self.lo_ready, c - RAW + 1)
            src, size, k = self.plan[c]
            sp.dma_start(self.raw[:, c % RAW, 0:size].rearrange("p (k c) -> p k c", k=k), src
                         ).then_inc(self.raw_landed[c % RAW], 16)
        self.fed = max(self.fed, end)

    def hi(self, act, n=None):
        end = min(len(self.plan), self.parts_room, len(self.plan) if n is None else self.began + n)
        for c in range(self.hid, end):
            act.wait_ge(self.raw_landed[c % RAW], 16 * (c // RAW + 1))
            if c >= SPLIT:
                act.wait_ge(self.parts_used, c - SPLIT + 1)
            size = self.plan[c][1]
            act.copy(self.split[:, c % SPLIT, 0, 0:size], self.raw[:, c % RAW, 0:size]).then_inc(self.hi_ready, 1)
        self.hid = max(self.hid, end)

    def lo(self, pool, n=None):
        end = min(len(self.plan), self.parts_room, len(self.plan) if n is None else self.began + n)
        for c in range(self.lod, end):
            size = self.plan[c][1]
            pool.wait_ge(self.hi_ready, c + 1)
            pool.tensor_tensor(self.split[:, c % SPLIT, 1, 0:size], self.raw[:, c % RAW, 0:size],
                               self.split[:, c % SPLIT, 0, 0:size].bitcast(F32), ALU.subtract
                               ).then_inc(self.lo_ready, 1)
        self.lod = max(self.lod, end)

    def take_parts(self, pe):
        c = self.taken
        self.taken += 1
        pe.wait_ge(self.lo_ready, c + 1)
        _, size, k = self.plan[c]
        return [self.split[:, c % SPLIT, part, 0:size].rearrange("p (k c) -> p k c", k=k) for part in range(2)]

    def end_parts_plan(self):
        assert self.fed == self.hid == self.lod == self.taken == len(self.plan) == self.released_to
        self.start_plan([])

    def warm_up(self, pe, bank, n=WARM_UP, x=None):
        x = self.hT[:, 0, :] if x is None else x
        for _ in range(n):
            pe.matmul(self.ps[:, bank, :], x[:, 0:P], x, start=True, stop=True)

    def feed(self, sp, n_taken):
        self.released_to += n_taken
        end = min(len(self.plan), self.released_to + RING)
        while self.fed < end:
            n = self.fed
            if n >= RING:
                sp.wait_ge(self.slots_used, n - RING + 1)
            for src, lo, size, shape in self.plan[n]:
                dst = self.ring[:, n % RING, lo:lo + size].rearrange("p (k c) -> p k c", k=shape)
                sp.dma_start(dst, src).then_inc(self.slot_landed[n % RING], 16)
            self.fed += 1

    def take(self, pe, k):
        n = self.taken
        self.taken += 1
        landed = sum(len(self.plan[m]) for m in range(n % RING, n + 1, RING))
        pe.wait_ge(self.slot_landed[n % RING], 16 * landed)
        size = sum(c[2] for c in self.plan[n])
        return self.ring[:, n % RING, 0:size].rearrange("p (k c) -> p k c", k=k)

    def end_plan(self):
        assert self.fed == self.taken == len(self.plan) == self.released_to
        self.plan, self.fed, self.taken, self.released_to = [], 0, 0, 0


def parts_product(pe, out, lhs, rhs, first, last):
    pe.matmul(out, lhs[0], rhs[0], start=first, stop=False)
    pe.matmul(out, lhs[0], rhs[1], start=False, stop=False)
    return pe.matmul(out, lhs[1], rhs[0], start=False, stop=last)


def parts_chunk(w, cols, k=KT):
    lo, hi = cols
    assert k * (hi - lo) <= PARTS_SLOT
    return (w.rearrange("(k p) c -> p k c", p=P)[:, :, lo:hi], k * (hi - lo), k)


def parts_tok_chunks(w, lo):
    return [parts_chunk(w[0:512], (lo, lo + 512), 4), parts_chunk(w[512:D], (lo, lo + 512), 4)]


def parts_T_chunks(w, lo, n):
    return [parts_chunk(w, (c, min(c + 256, lo + n))) for c in range(lo, lo + n, 256)]


def parts_T(m, pe, w, cols, banks, first, ready, kept):
    for i, lo in enumerate(cols):
        n = first + i
        if n >= len(banks):
            pe.wait_ge(kept, n - len(banks) + 1)
        for j in range(KT):
            mm = parts_product(pe, m.ps[:, banks[n % len(banks)], :], [p[:, j, lo:lo + P] for p in w],
                         [m.xT[:, p, j, :] for p in range(2)], j == 0, j == KT - 1)
        mm.then_inc(ready, 1)
    parts_released(m, pe, ready, first + len(cols))


def parts_tok(m, pe, x, parts, banks, first, ready, kept):
    for part in range(parts):
        w = m.take_parts(pe)
        k = KT // parts
        for tt in range(TT):
            n = first + tt
            if part == 0 and n >= len(banks):
                pe.wait_ge(kept, n - len(banks) + 1)
            for j in range(k):
                kt = part * k + j
                mm = parts_product(pe, m.ps[:, banks[n % len(banks)], 0:w[0].shape[2]],
                             [x[:, p, kt, tt * P:(tt + 1) * P] for p in range(2)], [p[:, j, :] for p in w],
                             kt == 0, kt == KT - 1)
            if part == parts - 1:
                mm.then_inc(ready, 1)
            elif tt == TT - 1:
                mm.then_inc(m.parts_used, 1)
    parts_released(m, pe, ready, first + TT)


def rows_chunk(w, cols, k=KT):
    lo, hi = cols
    return [(w.rearrange("(k p) c -> p k c", p=P)[:, :, lo:hi], 0, k * (hi - lo), k)]


def project_T(m, pe, w, rhs, k, ntiles, banks, first, ready, kept, last_cols=P):
    for i in range(ntiles):
        n = first + i
        if n >= len(banks):
            pe.wait_ge(kept, n - len(banks) + 1)
        cols = P if i < ntiles - 1 else last_cols
        for j in range(k):
            mm = pe.matmul(m.ps[0:cols, banks[n % len(banks)], :], w[:, j, i * P:i * P + cols], rhs[:, j, :],
                           start=(j == 0), stop=(j == k - 1))
        mm.then_inc(ready, 1)
    return mm


def project_tok(m, pe, w, lhs, cols, banks, first, ready, kept):
    lo, hi = cols
    for tt in range(TT):
        n = first + tt
        if n >= len(banks):
            pe.wait_ge(kept, n - len(banks) + 1)
        for j in range(KT):
            mm = pe.matmul(m.ps[:, banks[n % len(banks)], 0:hi - lo], lhs[:, j, tt * P:(tt + 1) * P], w[:, j, lo:hi],
                           start=(j == 0), stop=(j == KT - 1))
        mm.then_inc(ready, 1)
    return mm


def spread(ap, n=P):
    return ap.partition_broadcast(n)


def backwards(ap):
    *outer, (step, n) = [list(x) for x in ap.ap]
    return bass.AP(ap.tensor, ap.offset + step * (n - 1), outer + [[-step, n]])


def layer(ap, l):
    if isinstance(l, int):
        return ap[l]
    names = "bcdef"[:len(ap.shape) - 1]
    return ap[bass.ds(l, 1)].rearrange(f"a {' '.join(names)} -> (a {names[0]}) {' '.join(names[1:])}")


def columns_stage(m, rows_ap, n, out, q8):
    nc = m.nc
    loaded, turned, *_ = m.stage()
    with ExitStack() as ctx:
        rows = m.sbuf(ctx, "rows", [n, P])
        with nc.Block() as block:
            @block.sync
            def _(sp):
                m.clear_previous(sp)
                for (r0, r1, src) in rows_ap:
                    sp.dma_start(rows[r0:r1, :], src).then_inc(loaded, 16)
                m.feed_parts(sp, 0, splitting=False)

            @block.tensor
            def _(pe):
                pe.wait_ge(loaded, 16 * len(rows_ap))
                pe.transpose(m.ps[:, 0, 0:n], rows[:, :], m.ident[0:n, 0:n]).then_inc(turned, 1)

            @block.vector
            def _(dve):
                dve.wait_ge(turned, 1)
                dve.tensor_copy(out, m.ps[:, 0, 0:n])
                dve.tensor_scalar(q8, m.ps[:, 0, 0:4], HD ** -0.5, None, ALU.mult)


def norm_stage(m, gain, shift, store=None, parts=False, start_loads=None):
    nc = m.nc
    (loaded, step, var_ready, rstd_ready, mean_ready, centred, normed, turned, half_ready, hi_ready,
     *_) = m.stage()
    with ExitStack() as ctx:
        g = m.sbuf(ctx, "g", [P, D])
        b = m.sbuf(ctx, "b", [P, D])
        stats = m.sbuf(ctx, "stats", [P, TT, 2, 6])
        mv = m.sbuf(ctx, "mv", [P, TT, 2])
        rstd = m.sbuf(ctx, "rstd", [P, TT])
        half = m.sbuf(ctx, "half", [P, TT])
        with nc.Block() as block:
            @block.sync
            def _(sp):
                m.clear_previous(sp)
                sp.dma_start(g[:], spread(gain)).then_inc(loaded, 16)
                sp.dma_start(b[:], spread(shift)).then_inc(loaded, 16)
                if start_loads is not None:
                    start_loads(sp)
                if store is not None:
                    for tt in range(TT):
                        sp.wait_ge(normed, tt + 1)
                        sp.dma_start(store[tt * P:(tt + 1) * P, :], m.h[:, tt, :]).then_inc(m.out_stored, 16)
                    sp.wait_ge(m.out_stored, 16 * TT)

            @block.gpsimd
            def _(pool):
                nc.gpsimd.memset(half[:], -0.5).then_inc(half_ready, 1)
                pool.wait_ge(half_ready, 1)
                pool.wait_ge(var_ready, 1)
                nc.gpsimd.tensor_tensor(rstd[:], mv[:, :, 1], half[:], ALU.pow).then_inc(rstd_ready, 1)

            @block.vector
            def _(dve):
                do = Step(dve, step)
                for tt in range(TT):
                    for q in range(2):
                        do(dve.bn_stats(stats[:, tt, q, :], m.h[:, tt, q * 512:(q + 1) * 512]))
                    do(dve.bn_aggr(mv[:, tt, :], stats[:, tt, :, :]))
                dve.tensor_scalar(mv[:, :, 1], mv[:, :, 1], LN_EPS, None, ALU.add).then_inc(var_ready, 1)
                dve.tensor_scalar(mv[:, :, 0], mv[:, :, 0], -1.0, None, ALU.mult).then_inc(mean_ready, 1)
                dve.wait_ge(rstd_ready, 1)
                dve.wait_ge(loaded, 32)
                for tt in range(TT):
                    dve.wait_ge(centred, tt + 1)
                    do(dve.scalar_tensor_tensor(m.h[:, tt, :], m.h[:, tt, :], rstd[:, tt:tt + 1], g[:], ALU.mult,
                                                ALU.mult))
                    dve.tensor_tensor(m.h[:, tt, :], m.h[:, tt, :], b[:], ALU.add).then_inc(normed, 1)
                if parts:
                    for n in range(2 * TT):
                        tt, q = n // 2, n % 2
                        at = (slice(4 * q, 4 * q + 4), slice(tt * P, (tt + 1) * P))
                        dve.wait_ge(hi_ready, n + 1)
                        dve.tensor_tensor(m.xT[:, 1, at[0], at[1]], m.ps[:, n, :].rearrange("p (j t) -> p j t", j=4),
                                          m.xT[:, 0, at[0], at[1]].bitcast(F32), ALU.subtract)

            @block.scalar
            def _(act):
                act.wait_ge(mean_ready, 1)
                for tt in range(TT):
                    act.activation(m.h[:, tt, :], m.h[:, tt, :], ACT.Identity, bias=mv[:, tt, 0:1]
                                   ).then_inc(centred, 1)
                if store is None:
                    for n in range(2 * TT):
                        tt, q = n // 2, n % 2
                        act.wait_ge(turned, n + 1)
                        dst = m.xT[:, 0] if parts else m.hT
                        act.copy(dst[:, 4 * q:4 * q + 4, tt * P:(tt + 1) * P],
                                 m.ps[:, n, :].rearrange("p (j t) -> p j t", j=4)).then_inc(hi_ready, 1)

            if store is None:
                @block.tensor
                def _(pe):
                    for tt in range(TT):
                        pe.wait_ge(normed, tt + 1)
                        for q in range(2):
                            for j in range(4):
                                mm = pe.transpose(m.ps[:, 2 * tt + q, j * P:(j + 1) * P],
                                                  m.h[:, tt, (4 * q + j) * P:(4 * q + j + 1) * P], m.ident[:])
                            mm.then_inc(turned, 1)


def turn_h_stage(m):
    turned, *_ = m.stage()
    with m.nc.Block() as block:
        @block.sync
        def _(sp):
            m.clear_previous(sp)

        @block.tensor
        def _(pe):
            for n in range(2 * TT):
                tt, q = divmod(n, 2)
                for j in range(4):
                    mm = pe.transpose(m.ps[:, n, j * P:(j + 1) * P],
                                      m.h[:, tt, (4 * q + j) * P:(4 * q + j + 1) * P], m.ident[:])
                mm.then_inc(turned, 1)

        @block.scalar
        def _(act):
            for n in range(2 * TT):
                tt, q = divmod(n, 2)
                act.wait_ge(turned, n + 1)
                act.copy(m.hT[:, 4 * q:4 * q + 4, tt * P:(tt + 1) * P],
                         m.ps[:, n, :].rearrange("p (j t) -> p j t", j=4))


def attention_stage(m, qT, kT, place, v, v_col, zT, yT, bias, scale):
    nc = m.nc
    (scores_ready, scores_read, max_ready, probs_ready, probs_turned, probs_kept, pv_ready, y_ready,
     y_turned, y_kept, step, *_) = m.stage()
    NH = HEADS * TT
    with ExitStack() as ctx:
        s_sum = m.sbuf(ctx, "s_sum", [P, 2, SEQ])
        probs = m.sbuf(ctx, "probs", [P, 2, SEQ])
        probsT = m.sbuf(ctx, "probsT", [P, 2, SEQ])
        y = m.sbuf(ctx, "y", [P, SEQ])
        rowmax = m.sbuf(ctx, "rowmax", [P, 2])
        negmax = m.sbuf(ctx, "negmax", [P, 2])
        total = m.sbuf(ctx, "total", [P, 2, HEADS])
        inv = m.sbuf(ctx, "inv", [P, HEADS])

        S = lambda n: m.ps[:, n % 2, :]
        PT = lambda n: m.ps[:, 2 + n % 2, :]
        Y = lambda qt: m.ps[:, 4 + qt % 2, :]
        YT = m.ps[:, 6, :]
        with nc.Block() as block:
            @block.sync
            def _(sp):
                m.clear_previous(sp)
                m.feed_parts(sp, 0)

            @block.gpsimd
            def _(pool):
                m.lo(pool)

            @block.tensor
            def _(pe):
                m.warm_up(pe, 0, x=kT[:, 0, :])
                for i in range(NH + 3):
                    if i < NH:
                        qt, hd = divmod(i, HEADS)
                        tq, tk, at = place(hd)
                        if i >= 2:
                            pe.wait_ge(scores_read, i - 1)
                        pe.matmul(S(i), qT[at:at + HD, tq, qt * P:(qt + 1) * P], kT[at:at + HD, tk, :],
                                  start=True, stop=True).then_inc(scores_ready, 1)
                    if 1 <= i <= NH:
                        n = i - 1
                        pe.wait_ge(probs_ready, n + 1)
                        if n >= 2:
                            pe.wait_ge(probs_kept, n - 1)
                        for j in range(TT):
                            mm = pe.transpose(PT(n)[:, j * P:(j + 1) * P], probs[:, n % 2, j * P:(j + 1) * P],
                                              m.ident[:])
                        mm.then_inc(probs_turned, 1)
                    if 2 <= i <= NH + 1:
                        n = i - 2
                        qt, hd = divmod(n, HEADS)
                        pe.wait_ge(probs_kept, n + 1)
                        if hd == 0 and qt >= 2:
                            pe.wait_ge(y_ready, qt - 1)
                        for j in range(TT):
                            mm = pe.matmul(Y(qt)[:, hd * HD:(hd + 1) * HD], probsT[:, n % 2, j * P:(j + 1) * P],
                                           v[:, j, v_col(hd):v_col(hd) + HD], start=(j == 0), stop=(j == TT - 1))
                        mm.then_inc(pv_ready, 1)
                    if i >= 3 and (i - 3) % HEADS == HEADS - 1:
                        qt = (i - 3) // HEADS
                        pe.wait_ge(y_ready, qt + 1)
                        if qt >= 1:
                            pe.wait_ge(y_kept, qt)
                        for j in range(4):
                            mm = pe.transpose(YT[:, j * P:(j + 1) * P], y[:, j * P:(j + 1) * P], m.ident[:])
                        mm.then_inc(y_turned, 1)

            @block.scalar
            def _(act):
                m.hi(act)
                for n in range(NH):
                    qt, hd = divmod(n, HEADS)
                    act.wait_ge(max_ready, n + 1)
                    if n >= 2:
                        act.wait_ge(probs_turned, n - 1)
                    if hd == 0 and qt >= 2:
                        act.wait_ge(y_ready, qt - 1)
                    src = S(n) if bias is None else s_sum[:, n % 2, :]
                    act.activation(probs[:, n % 2, :], src, ACT.Exp, bias=negmax[:, n % 2:n % 2 + 1],
                                   scale=scale, accum_out=total[:, qt % 2, hd:hd + 1]).then_inc(probs_ready, 1)
                    if bias is None:
                        act.wait_ge(probs_ready, n + 1)
                        act.sem_inc(scores_read, 1)

            @block.vector
            def _(dve):
                do = Step(dve, step)
                for i in range(NH + 3):
                    if i < NH:
                        n = i
                        qt, hd = divmod(n, HEADS)
                        dve.wait_ge(scores_ready, n + 1)
                        if n >= 2:
                            dve.wait_ge(probs_ready, n - 1)
                        if bias is None:
                            do(dve.reduce_max(rowmax[:, n % 2:n % 2 + 1], S(n), AX.X))
                        else:
                            dve.tensor_tensor_reduce(
                                out=s_sum[:, n % 2, :], in0=S(n), in1=bias(qt, hd), scale=1.0, scalar=-3e38,
                                op0=ALU.add, op1=ALU.max, accum_out=rowmax[:, n % 2:n % 2 + 1]
                            ).then_inc(scores_read, 1)
                            dve.wait_ge(scores_read, n + 1)
                        dve.tensor_scalar(negmax[:, n % 2:n % 2 + 1], rowmax[:, n % 2:n % 2 + 1], -scale, None,
                                          ALU.mult).then_inc(max_ready, 1)
                    if 1 <= i <= NH:
                        n = i - 1
                        dve.wait_ge(probs_turned, n + 1)
                        if n >= 2:
                            dve.wait_ge(pv_ready, n - 1)
                        dve.tensor_copy(probsT[:, n % 2, :], PT(n)).then_inc(probs_kept, 1)
                    if i >= 2 and (i - 2) % HEADS == HEADS - 1:
                        qt = (i - 2) // HEADS
                        dve.wait_ge(probs_ready, (qt + 1) * HEADS)
                        do(dve.reciprocal(inv[:], total[:, qt % 2, :]))
                        dve.wait_ge(pv_ready, (qt + 1) * HEADS)
                        if qt >= 1:
                            dve.wait_ge(y_turned, qt)
                        dve.tensor_tensor(y[:].rearrange("p (h d) -> p h d", h=HEADS),
                                          Y(qt).rearrange("p (h d) -> p h d", h=HEADS),
                                          inv[:].unsqueeze(2).to_broadcast([P, HEADS, HD]),
                                          ALU.mult).then_inc(y_ready, 1)
                    if i >= 3 and (i - 3) % HEADS == HEADS - 1:
                        qt = (i - 3) // HEADS
                        dve.wait_ge(y_turned, qt + 1)
                        dve.tensor_tensor(yT[:, :, qt * P:(qt + 1) * P], YT.rearrange("p (j t) -> p j t", j=4),
                                          zT[:, :, qt * P:(qt + 1) * P], ALU.mult).then_inc(y_kept, 1)


def merge_stage(m, branch, b_col, yT):
    nc = m.nc
    gate_ready, gate_kept, p_ready, summed, step, y_hi, y_lo, *_ = m.stage()
    with ExitStack() as ctx:
        gate = m.sbuf(ctx, "gate", [P, 2, SEQ])
        part = m.sbuf(ctx, "part", [P, 2, SEQ])
        ys = m.sbuf(ctx, "ys", [P, 2, 4, SEQ], F32R)
        with nc.Block() as block:
            @block.sync
            def _(sp):
                m.clear_previous(sp)
                m.feed_parts(sp, 6)

            @block.tensor
            def _(pe):
                gates = lambda dt: parts_T(m, pe, m.take_parts(pe), (0, P), (0, 1, 2, 3), dt, gate_ready, gate_kept)
                for half in range(2):
                    gates(4 * half)
                    wb = m.take_parts(pe)
                    if half == 0:
                        pe.wait_ge(y_lo, 1)
                    for i in range(4):
                        dt = 4 * half + i
                        if half:
                            pe.wait_ge(summed, dt - 3)
                        for j in range(4):
                            mm = parts_product(pe, m.ps[:, 4 + i, :], [p[:, j, i * P:(i + 1) * P] for p in wb],
                                         [ys[:, p, j, :] for p in range(2)], j == 0, j == 3)
                        mm.then_inc(p_ready, 1)
                    parts_released(m, pe, p_ready, 4 * half + 4)
                    gates(4 * half + 2)

            @block.scalar
            def _(act):
                act.copy(ys[:, 0], yT[:]).then_inc(y_hi, 1)
                for dt in range(KT):
                    if dt % 2 == 0:
                        m.hi(act, (2, 4, 5, 7)[dt // 2])
                    act.wait_ge(gate_ready, dt + 1)
                    if dt >= 2:
                        act.wait_ge(summed, dt - 1)
                    act.activation(gate[:, dt % 2, :], m.ps[:, dt % 4, :], ACT.Sigmoid,
                                   bias=b_col[:, branch * KT + dt:branch * KT + dt + 1]).then_inc(gate_kept, 1)
                m.hi(act)

            @block.gpsimd
            def _(pool):
                m.lo(pool)

            @block.vector
            def _(dve):
                do = Step(dve, step)
                dve.wait_ge(y_hi, 1)
                dve.tensor_tensor(ys[:, 1], yT[:], ys[:, 0].bitcast(F32), ALU.subtract).then_inc(y_lo, 1)
                for dt in range(KT):
                    dve.wait_ge(gate_kept, dt + 1)
                    dve.wait_ge(p_ready, dt + 1)
                    if branch == 0:
                        dve.tensor_tensor(m.mixT[:, dt, :], m.ps[:, 4 + dt % 4, :], gate[:, dt % 2, :],
                                          ALU.mult).then_inc(summed, 1)
                    else:
                        do(dve.tensor_tensor(part[:, dt % 2, :], m.ps[:, 4 + dt % 4, :], gate[:, dt % 2, :],
                                             ALU.mult))
                        dve.tensor_tensor(m.mixT[:, dt, :], m.mixT[:, dt, :], part[:, dt % 2, :],
                                          ALU.add).then_inc(summed, 1)


def first_out_stage(m, b_out):
    nc = m.nc
    loaded, scaled, ready, step, hi_ready, lo_ready, *_ = m.stage()
    with ExitStack() as ctx:
        bias = m.sbuf(ctx, "b_out", [P, D])
        with nc.Block() as block:
            @block.sync
            def _(sp):
                m.clear_previous(sp)
                if b_out is not None:
                    sp.dma_start(bias[:], spread(b_out)).then_inc(loaded, 16)
                m.feed_parts(sp, 4)

            @block.tensor
            def _(pe):
                pe.wait_ge(lo_ready, KT)
                for nh in range(2):
                    parts_tok(m, pe, m.xT, 2, tuple(range(8)), nh * TT, ready, None)

            @block.scalar
            def _(act):
                for j in range(KT):
                    act.copy(m.xT[:, 0, j, :], m.mixT[:, j, :]).then_inc(hi_ready, 1)
                m.hi(act)

            @block.gpsimd
            def _(pool):
                m.lo(pool)

            @block.vector
            def _(dve):
                do = Step(dve, step)
                for j in range(KT):
                    dve.wait_ge(hi_ready, j + 1)
                    dve.tensor_tensor(m.xT[:, 1, j, :], m.mixT[:, j, :], m.xT[:, 0, j, :].bitcast(F32),
                                      ALU.subtract).then_inc(lo_ready, 1)
                if b_out is not None:
                    dve.wait_ge(loaded, 16)
                for tt in range(TT):
                    if b_out is not None:
                        do(dve.scalar_tensor_tensor(m.h[:, tt, :], m.h[:, tt, :], ALPHA, bias[:], ALU.mult, ALU.add))
                    else:
                        do(dve.tensor_scalar(m.h[:, tt, :], m.h[:, tt, :], ALPHA, None, ALU.mult))
                for n in range(2 * TT):
                    nh, tt = divmod(n, TT)
                    dve.wait_ge(ready, n + 1)
                    dve.tensor_tensor(m.h[:, tt, nh * 512:(nh + 1) * 512], m.h[:, tt, nh * 512:(nh + 1) * 512],
                                      m.ps[:, n, :], ALU.add)


def out_stage(m):
    nc = m.nc
    ready, step, *_ = m.stage()
    with nc.Block() as block:
        @block.sync
        def _(sp):
            m.clear_previous(sp)
            m.feed(sp, 2)

        @block.tensor
        def _(pe):
            for nh in range(2):
                w = m.take(pe, KT)
                project_out(m, pe, w, nh, ready)

        @block.vector
        def _(dve):
            do = Step(dve, step)
            for tt in range(TT):
                do(dve.tensor_scalar(m.h[:, tt, :], m.h[:, tt, :], ALPHA, None, ALU.mult))
            for n in range(2 * TT):
                nh, tt = divmod(n, TT)
                dve.wait_ge(ready, n + 1)
                dve.tensor_tensor(m.h[:, tt, nh * 512:(nh + 1) * 512], m.h[:, tt, nh * 512:(nh + 1) * 512],
                                  m.ps[:, n, :], ALU.add)


def project_out(m, pe, w, nh, ready):
    for tt in range(TT):
        for j in range(KT):
            mm = pe.matmul(m.ps[:, nh * TT + tt, :], m.mixT[:, j, tt * P:(tt + 1) * P], w[:, j, :],
                           start=(j == 0), stop=(j == KT - 1))
        mm.then_inc(ready, 1)
    pe.wait_ge(ready, (nh + 1) * TT)
    pe.sem_inc(m.slots_used, 1)


def parts_released(m, pe, sem, n):
    pe.wait_ge(sem, n)
    pe.sem_inc(m.parts_used, 1)


def released(m, pe, sem, n):
    pe.wait_ge(sem, n)
    pe.sem_inc(m.slots_used, 1)


def first_load_stage(m, x):
    nc = m.nc
    loaded, *_ = m.stage()
    with nc.Block() as block:
        @block.sync
        def _(sp):
            m.clear_previous(sp)
            sp.dma_start(m.ident[:], m.table("ident")).then_inc(loaded, 16)
            sp.dma_start(m.h[:], x.rearrange("(t p) d -> p t d", p=P)).then_inc(loaded, 16)
            sp.wait_ge(loaded, 32)


def na_branch(m, l, A, b_cols):
    nc = m.nc
    rpb_pad = A["rpb_pad"]
    RO = 2 * HEADS - 1
    CO = 2 * NA_KW - 1
    PADDED = 2 * GRID_W - 1
    NS = RO - 1
    with ExitStack() as outer, ExitStack() as ctx:
        yT = m.sbuf(outer, "na_yT", [P, 4, SEQ])
        qT = m.sbuf(ctx, "na_qT", [P, 4, SEQ])
        kT = m.sbuf(ctx, "na_kT", [P, 4, SEQ])
        zT = m.sbuf(ctx, "na_zT", [P, 4, SEQ])
        v = m.sbuf(ctx, "na_v", [P, TT, 512])
        table = m.sbuf(ctx, "na_table", [P, HEADS, NS, GRID_W])

        (loaded, rpb_loaded, padded, pad_stored, even_loaded, odd_loaded, table_kept, zeroed, tile_ready, tile_kept,
         tok_ready, tok_kept, *_) = m.stage()
        table_loaded = (even_loaded, odd_loaded)
        with ExitStack() as c2:
            rpb = m.sbuf(c2, "rpb", [HEADS * RO, CO])
            pad = m.sbuf(c2, "pad", [HEADS * RO, PADDED])
            skewed = m.sbuf(c2, "skewed", [P, 2, NS, GRID_W])
            v_bias = m.sbuf(c2, "v_bias", [P, 512])
            window = m.sbuf(c2, "window", [P, GRID_W])
            with nc.Block() as block:
                @block.sync
                def _(sp):
                    m.clear_previous(sp)
                    sp.dma_start(rpb[:], layer(A["na_rpb"], l).rearrange("h r c -> (h r) c")).then_inc(rpb_loaded, 16)
                    sp.dma_start(v_bias[:], spread(layer(A["b_in"], l)[NA_V:NA_V + 512])).then_inc(loaded, 16)
                    sp.dma_start(window[:], m.table("window")).then_inc(loaded, 16)
                    sp.wait_ge(padded, 1)
                    sp.dma_start(rpb_pad.rearrange("h r c -> (h r) c"), pad[:]).then_inc(pad_stored, 16)
                    m.feed_parts(sp, 8)

                @block.gpsimd
                def _(pool):
                    nc.gpsimd.memset(pad[:], 0.0).then_inc(zeroed, 1)
                    m.lo(pool, 1)
                    pool.wait_ge(zeroed, 1)
                    pool.wait_ge(rpb_loaded, 16)
                    lo = GRID_W - NA_KW
                    nc.gpsimd.tensor_copy(pad[:, lo:lo + CO], backwards(rpb[:])).then_inc(padded, 1)
                    m.lo(pool, 8)
                    m.lo(pool)

                @block.tensor
                def _(pe):
                    for n in range(4):
                        parts_T(m, pe, m.take_parts(pe), (0, P), (0, 1, 2, 3), 2 * n, tile_ready, tile_kept)
                    parts_tok(m, pe, m.xT, 2, (4, 5, 6, 7), 0, tok_ready, tok_kept)
                    for n in range(4, 6):
                        parts_T(m, pe, m.take_parts(pe), (0, P), (0, 1, 2, 3), 2 * n, tile_ready, tile_kept)

                @block.scalar
                def _(act):
                    def load_skewed(h):
                        if h >= 2:
                            act.wait_ge(table_kept, h - 1)
                        for b in range(2):
                            src = bass.AP(rpb_pad.tensor, (h * RO + 1 - b) * PADDED,
                                          [[1, GRID_W], [PADDED, NS], [1, GRID_W]])
                            act.dma_start(skewed[GRID_W * b:GRID_W * (b + 1), h % 2], src
                                          ).then_inc(table_loaded[h % 2], 16)

                    m.hi(act, 2)
                    act.wait_ge(pad_stored, 16)
                    load_skewed(0)
                    load_skewed(1)
                    for n in range(12):
                        if n % 2 == 0:
                            m.hi(act, (2, 3, 4, 5, 8, 9)[n // 2])
                        act.wait_ge(tile_ready, n + 1)
                        src = m.ps[:, n % 4, :]
                        if n < 4:
                            act.activation(qT[:, n, :], src, ACT.Identity, bias=b_cols["q8"][:, n:n + 1],
                                           scale=HD ** -0.5).then_inc(tile_kept, 1)
                        elif n < 8:
                            act.activation(kT[:, n - 4, :], src, ACT.Identity,
                                           bias=b_cols["all"][:, n:n + 1]).then_inc(tile_kept, 1)
                        else:
                            c = NA_Z // P + n - 8
                            act.activation(zT[:, n - 8, :], src, ACT.Silu,
                                           bias=b_cols["all"][:, c:c + 1]).then_inc(tile_kept, 1)
                        if n + 2 < HEADS:
                            load_skewed(n + 2)
                    m.hi(act)

                @block.vector
                def _(dve):
                    dve.wait_ge(loaded, 32)
                    for h in range(HEADS):
                        dve.wait_ge(table_loaded[h % 2], 16 * 2 * (h // 2 + 1))
                        dve.tensor_tensor(table[:, h], backwards(skewed[:, h % 2]),
                                          window[:].unsqueeze(1).to_broadcast([P, NS, GRID_W]),
                                          ALU.add).then_inc(table_kept, 1)
                    for tt in range(TT):
                        dve.wait_ge(tok_ready, tt + 1)
                        dve.tensor_tensor(v[:, tt, :], m.ps[:, 4 + tt, :], v_bias[:], ALU.add).then_inc(tok_kept, 1)

        def bias(qt, hd):
            s0 = NS // 2 - 1 - 2 * qt
            return table[:, hd, s0:s0 + HEADS, :].rearrange("p s c -> p (s c)")

        attention_stage(m, qT, kT, lambda hd: (hd // 2, hd // 2, hd % 2 * HD), v, lambda hd: hd * HD, zT, yT,
                        bias, 1.0)
        ctx.close()
        merge_stage(m, 0, b_cols["gates"], yT)


def gqa_branch(m, l, A, b_cols):
    nc = m.nc
    NQK = 10
    with ExitStack() as outer, ExitStack() as ctx:
        yT = m.sbuf(outer, "gq_yT", [P, 4, SEQ])
        zT = m.sbuf(ctx, "gq_zT", [P, 4, SEQ])
        qT = m.sbuf(ctx, "gq_qT", [P, 4, SEQ])
        kT = m.sbuf(ctx, "gq_kT", [P, 1, SEQ])
        v = m.sbuf(ctx, "gq_v", [P, TT, P])
        (loaded, tile_ready, tile_kept, tok_ready, tok_kept, ms_ready, rs_ready, turn_ready, turned, turn_kept,
         half_ready, step, *_) = m.stage()
        with ExitStack() as c2:
            qk = m.sbuf(c2, "qk", [P, TT, NQK * HD])
            rot = m.sbuf(c2, "rot", [P, 2, NQK * HD])
            tmp = m.sbuf(c2, "tmp", [P, NQK * HD])
            bias = m.sbuf(c2, "bias", [P, 768])
            gain = m.sbuf(c2, "gain", [P, 2 * HD])
            cos = m.sbuf(c2, "cos", [P, TT, 32])
            sin = m.sbuf(c2, "sin", [P, TT, 32])
            ms = m.sbuf(c2, "ms", [P, TT, NQK])
            rs = m.sbuf(c2, "rs", [P, TT, NQK])
            half = m.sbuf(c2, "half", [P, TT, NQK])
            with nc.Block() as block:
                @block.sync
                def _(sp):
                    m.clear_previous(sp)
                    sp.dma_start(bias[:], spread(layer(A["b_in"], l)[GQ_Q:GQ_Q + 768])).then_inc(loaded, 16)
                    sp.dma_start(gain[:, 0:HD], spread(layer(A["q_norm_g"], l))).then_inc(loaded, 16)
                    sp.dma_start(gain[:, HD:2 * HD], spread(layer(A["k_norm_g"], l))).then_inc(loaded, 16)
                    sp.dma_start(cos[:].rearrange("p t f -> p (t f)"), m.table("rope_cos")).then_inc(loaded, 16)
                    sp.dma_start(sin[:].rearrange("p t f -> p (t f)"), m.table("rope_sin")).then_inc(loaded, 16)
                    m.feed_parts(sp, 5)

                @block.gpsimd
                def _(pool):
                    m.lo(pool, 5)
                    nc.gpsimd.memset(half[:], -0.5).then_inc(half_ready, 1)
                    pool.wait_ge(half_ready, 1)
                    pool.wait_ge(ms_ready, 1)
                    nc.gpsimd.tensor_tensor(rs[:], ms[:], half[:], ALU.pow).then_inc(rs_ready, 1)
                    m.lo(pool)

                @block.tensor
                def _(pe):
                    parts_tok(m, pe, m.xT, 2, (4, 5, 6, 7), 0, tok_ready, tok_kept)
                    parts_tok(m, pe, m.xT, 1, (4, 5, 6, 7), 4, tok_ready, tok_kept)
                    for n in range(2):
                        parts_T(m, pe, m.take_parts(pe), (0, P), (0, 1), 2 * n, tile_ready, tile_kept)
                    pe.wait_ge(tok_kept, 8)
                    for tt in range(TT):
                        pe.wait_ge(turn_ready, tt + 1)
                        if tt >= 2:
                            pe.wait_ge(turn_kept, tt - 1)
                        for j in range(5):
                            bank, at = 4 + 2 * (tt % 2) + j // 4, j % 4 * P
                            mm = pe.transpose(m.ps[:, bank, at:at + P], rot[:, tt % 2, j * P:(j + 1) * P], m.ident[:])
                        mm.then_inc(turned, 1)

                @block.scalar
                def _(act):
                    m.hi(act, 5)
                    for n in range(4):
                        if n == 2:
                            m.hi(act)
                        act.wait_ge(tile_ready, n + 1)
                        c = GQ_Z // P + n
                        act.activation(zT[:, n, :], m.ps[:, n % 2, :], ACT.Silu,
                                       bias=b_cols["all"][:, c:c + 1]).then_inc(tile_kept, 1)
                    for tt in range(TT):
                        act.wait_ge(turned, tt + 1)
                        b = 4 + 2 * (tt % 2)
                        act.copy(qT[:, :, tt * P:(tt + 1) * P], m.ps[:, b, :].rearrange("p (j t) -> p j t", j=4))
                        act.copy(kT[:, 0, tt * P:(tt + 1) * P], m.ps[:, b + 1, 0:P]).then_inc(turn_kept, 1)

                @block.vector
                def _(dve):
                    do = Step(dve, step)
                    dve.wait_ge(loaded, 80)
                    for n in range(8):
                        tt = n % 4
                        dve.wait_ge(tok_ready, n + 1)
                        if n < 4:
                            dve.tensor_tensor(qk[:, tt, 0:512], m.ps[:, 4 + tt, :], bias[:, 0:512],
                                              ALU.add).then_inc(tok_kept, 1)
                        else:
                            do(dve.tensor_tensor(qk[:, tt, 512:640], m.ps[:, 4 + tt, 0:P], bias[:, 512:640], ALU.add))
                            dve.tensor_tensor(v[:, tt, :], m.ps[:, 4 + tt, P:2 * P], bias[:, 640:768],
                                              ALU.add).then_inc(tok_kept, 1)
                    dve.wait_ge(tok_kept, 8)
                    for tt in range(TT):
                        do(dve.tensor_tensor(tmp[:], qk[:, tt, :], qk[:, tt, :], ALU.mult))
                        do(dve.reduce_sum(ms[:, tt, :], tmp[:].rearrange("p (h d) -> p h d", h=NQK), AX.X))
                    dve.tensor_scalar(ms[:], ms[:], 1.0 / HD, RMS_EPS, ALU.mult, ALU.add).then_inc(ms_ready, 1)
                    dve.wait_ge(rs_ready, 1)
                    for tt in range(TT):
                        x3 = qk[:, tt, :].rearrange("p (h d) -> p h d", h=NQK)
                        do(dve.tensor_tensor(x3, x3, rs[:, tt, :].unsqueeze(2).to_broadcast([P, NQK, HD]), ALU.mult))
                        do(dve.tensor_tensor(x3[:, 0:8], x3[:, 0:8],
                                             gain[:, 0:HD].unsqueeze(1).to_broadcast([P, 8, HD]), ALU.mult))
                        do(dve.tensor_tensor(x3[:, 8:10], x3[:, 8:10],
                                             gain[:, HD:].unsqueeze(1).to_broadcast([P, 2, HD]), ALU.mult))
                        if tt >= 2:
                            dve.wait_ge(turned, tt - 1)
                        src = qk[:, tt, 0:512].rearrange("p (g j e o) -> p g j e o", g=2, j=4, o=2)
                        dst = rot[:, tt % 2, 0:512].rearrange("p (j g e o) -> p g j e o", g=2, j=4, o=2)
                        t4 = tmp[:, 0:512].rearrange("p (g j e o) -> p g j e o", g=2, j=4, o=2)
                        ks = qk[:, tt, 512:640].rearrange("p (g e o) -> p g e o", g=2, o=2)
                        kd = rot[:, tt % 2, 512:640].rearrange("p (g e o) -> p g e o", g=2, o=2)
                        kt = tmp[:, 512:640].rearrange("p (g e o) -> p g e o", g=2, o=2)
                        for g in range(3):
                            s, d, t = (src[:, g], dst[:, g], t4[:, g]) if g < 2 else (ks, kd, kt)
                            nh = 4 if g < 2 else 2
                            c = cos[:, tt].unsqueeze(1).to_broadcast([P, nh, 32])
                            n_ = sin[:, tt].unsqueeze(1).to_broadcast([P, nh, 32])
                            do(dve.tensor_tensor(d[..., 0], s[..., 0], c, ALU.mult))
                            do(dve.tensor_tensor(t[..., 0], s[..., 1], n_, ALU.mult))
                            do(dve.tensor_tensor(d[..., 0], d[..., 0], t[..., 0], ALU.subtract))
                            do(dve.tensor_tensor(d[..., 1], s[..., 0], n_, ALU.mult))
                            do(dve.tensor_tensor(t[..., 1], s[..., 1], c, ALU.mult))
                            ins = dve.tensor_tensor(d[..., 1], d[..., 1], t[..., 1], ALU.add)
                            if g < 2:
                                do(ins)
                            else:
                                ins.then_inc(turn_ready, 1)

        attention_stage(m, qT, kT, lambda hd: (hd % 4, 0, hd // 4 * HD), v, lambda hd: hd // 4 * HD, zT, yT,
                        None, HD ** -0.5)
        ctx.close()
        merge_stage(m, 1, b_cols["gates"], yT)


def gating_branch(m, l, A, b_cols):
    nc = m.nc
    G = 8
    with ExitStack() as outer, ExitStack() as ctx:
        yT = m.sbuf(outer, "sg_yT", [P, 4, SEQ])
        uT = m.sbuf(ctx, "sg_uT", [P, 4, SEQ])
        zT = m.sbuf(ctx, "sg_zT", [P, 4, SEQ])
        v = m.sbuf(ctx, "sg_v", [P, TT, 512])
        w = m.sbuf(ctx, "sg_w", [P, G, P])
        wT = m.sbuf(ctx, "sg_wT", [P, G, P])
        mix_b = m.sbuf(ctx, "sg_b", [P, 4, P])
        tmp = m.sbuf(ctx, "sg_tmp", [P, SEQ])
        bias = m.sbuf(ctx, "sg_bias", [P, 512])
        g = m.sbuf(ctx, "sg_g", [P, 512])
        b = m.sbuf(ctx, "sg_lb", [P, 512])
        stats = m.sbuf(ctx, "sg_stats", [P, TT, 6])
        mv = m.sbuf(ctx, "sg_mv", [P, TT, 2])
        rstd = m.sbuf(ctx, "sg_rstd", [P, TT])
        half = m.sbuf(ctx, "sg_half", [P, TT])
        (loaded, w_loaded, tile_ready, tile_kept, tok_ready, tok_kept, var_ready, rs_ready, half_ready, w_turned,
         wT_ready, v_ready, mixed, mix_read, step, *_) = m.stage()
        with nc.Block() as block:
            @block.sync
            def _(sp):
                m.clear_previous(sp)
                sp.dma_start(w[:], layer(A["sg_w"], l).rearrange("g m n -> m g n")).then_inc(w_loaded, 16)
                sp.dma_start(bias[:], spread(layer(A["b_in"], l)[SG_V:SG_V + 512])).then_inc(loaded, 16)
                sp.dma_start(g[:], spread(layer(A["sg_ln_g"], l))).then_inc(loaded, 16)
                sp.dma_start(b[:], spread(layer(A["sg_ln_b"], l))).then_inc(loaded, 16)
                pairs = layer(A["sg_b"], l).rearrange("(j o) m -> o j m", o=2)
                for o in range(2):
                    sp.dma_start(mix_b[o * HD:(o + 1) * HD], spread(pairs[o], HD)).then_inc(loaded, 16)
                m.feed_parts(sp, 6)

            @block.gpsimd
            def _(pool):
                m.lo(pool, 4)
                nc.gpsimd.memset(half[:], -0.5).then_inc(half_ready, 1)
                pool.wait_ge(half_ready, 1)
                pool.wait_ge(var_ready, 1)
                nc.gpsimd.tensor_tensor(rstd[:], mv[:, :, 1], half[:], ALU.pow).then_inc(rs_ready, 1)
                m.lo(pool)

            @block.tensor
            def _(pe):
                parts_tok(m, pe, m.xT, 2, (4, 5, 6, 7), 0, tok_ready, tok_kept)
                pe.wait_ge(w_loaded, 16)
                for gr in range(G):
                    mm = pe.transpose(m.ps[:, 2 + gr // 4, gr % 4 * P:(gr % 4 + 1) * P], w[:, gr, :], m.ident[:])
                mm.then_inc(w_turned, 1)
                for n in range(4):
                    parts_T(m, pe, m.take_parts(pe), (0, P), (0, 1), 2 * n, tile_ready, tile_kept)
                pe.wait_ge(wT_ready, 1)
                pe.wait_ge(v_ready, 1)
                pe.wait_ge(tok_kept, 4)
                for j in range(4):
                    for c in range(TT):
                        for o in range(2):
                            gr = 2 * j + o
                            mm = pe.matmul(m.ps[o * HD:(o + 1) * HD, 4 + j, c * P:(c + 1) * P],
                                           v[:, c, gr * HD:(gr + 1) * HD], wT[:, gr, :], start=True, stop=True)
                    mm.then_inc(mixed, 1)

            @block.scalar
            def _(act):
                m.hi(act, 3)
                act.wait_ge(w_turned, 1)
                act.copy(wT[:, 0:4, :], m.ps[:, 2, :].rearrange("p (g m) -> p g m", g=4))
                act.copy(wT[:, 4:8, :], m.ps[:, 3, :].rearrange("p (g m) -> p g m", g=4)).then_inc(wT_ready, 1)
                for n in range(8):
                    m.hi(act, 4 + n // 2)
                    act.wait_ge(tile_ready, n + 1)
                    if n < 4:
                        c = SG_U // P + n
                        act.activation(uT[:, n, :], m.ps[:, n % 2, :], ACT.Identity,
                                       bias=b_cols["all"][:, c:c + 1]).then_inc(tile_kept, 1)
                    else:
                        c = SG_Z // P + n - 4
                        act.activation(zT[:, n - 4, :], m.ps[:, n % 2, :], ACT.Silu,
                                       bias=b_cols["all"][:, c:c + 1]).then_inc(tile_kept, 1)
                m.hi(act)

            @block.vector
            def _(dve):
                do = Step(dve, step)
                dve.wait_ge(loaded, 80)
                for tt in range(TT):
                    dve.wait_ge(tok_ready, tt + 1)
                    dve.tensor_tensor(v[:, tt, :], m.ps[:, 4 + tt, :], bias[:], ALU.add).then_inc(tok_kept, 1)
                    dve.wait_ge(tok_kept, tt + 1)
                    do(dve.bn_stats(stats[:, tt, :], v[:, tt, :]))
                    do(dve.bn_aggr(mv[:, tt, :], stats[:, tt, :]))
                dve.tensor_scalar(mv[:, :, 1], mv[:, :, 1], LN_EPS, None, ALU.add).then_inc(var_ready, 1)
                dve.wait_ge(rs_ready, 1)
                for tt in range(TT):
                    do(dve.tensor_scalar(v[:, tt, :], v[:, tt, :], mv[:, tt, 0:1], rstd[:, tt:tt + 1],
                                         ALU.subtract, ALU.mult))
                    do(dve.tensor_tensor(v[:, tt, :], v[:, tt, :], g[:], ALU.mult))
                    ins = dve.tensor_tensor(v[:, tt, :], v[:, tt, :], b[:], ALU.add)
                    if tt < TT - 1:
                        do(ins)
                ins.then_inc(v_ready, 1)
                dve.wait_ge(tile_kept, 8)
                for j in range(4):
                    dve.wait_ge(mixed, j + 1)
                    do(dve.tensor_tensor(tmp[:].rearrange("p (c m) -> p c m", c=TT),
                                         m.ps[:, 4 + j, :].rearrange("p (c m) -> p c m", c=TT),
                                         mix_b[:, j, :].unsqueeze(1).to_broadcast([P, TT, P]), ALU.add))
                    do(dve.tensor_tensor(tmp[:], tmp[:], uT[:, j, :], ALU.mult))
                    do(dve.tensor_tensor(yT[:, j, :], tmp[:], zT[:, j, :], ALU.mult))
        ctx.close()
        merge_stage(m, 2, b_cols["gates"], yT)


def first_block_plan(w_in, w_br, w_out):
    def branch(i):
        plan = []
        for half in range(2):
            first, last = parts_T_chunks(w_in, GATES + i * D + half * 512, 512)
            plan += [first, parts_chunk(w_br[i], (half * 512, half * 512 + 512), 4), last]
        return plan

    plan = parts_T_chunks(w_in, NA_Q, 512) + parts_T_chunks(w_in, NA_K, 512) + parts_tok_chunks(w_in, NA_V)
    plan += parts_T_chunks(w_in, NA_Z, 512) + branch(0)
    plan += parts_tok_chunks(w_in, GQ_Q) + parts_T_chunks(w_in, GQ_KV, 256) + parts_T_chunks(w_in, GQ_Z, 512) + branch(1)
    plan += parts_tok_chunks(w_in, SG_V) + parts_T_chunks(w_in, SG_U, 512) + parts_T_chunks(w_in, SG_Z, 512) + branch(2)
    return plan + parts_tok_chunks(w_out, 0) + parts_tok_chunks(w_out, 512)


def first_block_layer(m, l, A):
    with ExitStack() as ctx:
        n = IN_WIDTH // P
        b_all = m.sbuf(ctx, "b_all", [P, n])
        b_q8 = m.sbuf(ctx, "b_q8", [P, 4])
        m.start_plan(first_block_plan(layer(A["w_in"], l), [layer(A[k], l) for k in ("w_br_a", "w_br_b", "w_br_c")],
                                      layer(A["w_out"], l)))
        columns_stage(m, [(0, n, layer(A["b_in"], l).rearrange("(r c) -> r c", c=P))], n, b_all[:], b_q8[:])
        b_cols = {"all": b_all, "q8": b_q8, "gates": b_all[:, GATES // P:]}
        na_branch(m, l, A, b_cols)
        gqa_branch(m, l, A, b_cols)
        gating_branch(m, l, A, b_cols)
    first_out_stage(m, layer(A["b_out"], l))
    norm_stage(m, layer(A["ln_post_g"], l), layer(A["ln_post_b"], l), parts=True)
    end_parts_stage(m)


def end_parts_stage(m):
    nc = m.nc
    m.stage()
    m.end_parts_plan()
    with nc.Block() as block:
        @block.sync
        def _(sp):
            m.clear_previous(sp)
            nums = [s.num for s in m.raw_landed + [m.hi_ready, m.lo_ready, m.parts_used]]
            sp.sem_clear(range(min(nums), max(nums) + 1))


def end_ring_stage(m):
    nc = m.nc
    m.stage()
    m.end_plan()
    with nc.Block() as block:
        @block.sync
        def _(sp):
            m.clear_previous(sp)
            nums = [s.num for s in m.slot_landed + [m.slots_used]]
            sp.sem_clear(range(min(nums), max(nums) + 1))


def idle_stage(m):
    m.stage()
    with m.nc.Block() as block:
        @block.sync
        def _(sp):
            m.clear_previous(sp)



GROUP = 256
HGRN, GLA, RWKV, RET, IN2 = 0, 1024, 1808, 2864, 3888
GLA_RANK, GLA_KEY = 16, 32
W_RANK, G_RANK, V_RANK = 64, 160, 32
CH = 64
NC = SEQ // CH
LEVELS = 6
EXPERTS = 8
(C_MU, C_W0, C_A0, C_KK, C_KA, C_RK, C_LG, C_LB, C_V0, C_GLAB, C_HN, C_GN, C_L0, C_L1, C_N) = (
    0, 9, 11, 13, 15, 17, 19, 21, 23, 25, 26, 27, 28, 30, 32)


def project_cols(m, pe, w, cols, banks, first, ready, kept):
    for i, (lo, hi) in enumerate(cols):
        n = first + i
        if n >= len(banks):
            pe.wait_ge(kept, n - len(banks) + 1)
        for j in range(KT):
            mm = pe.matmul(m.ps[0:hi - lo, banks[n % len(banks)], :], w[:, j, lo:hi], m.hT[:, j, :],
                           start=(j == 0), stop=(j == KT - 1))
        mm.then_inc(ready, 1)


def params_stage(m, l, A, cols, lb):
    nc = m.nc
    row = lambda ap: ap.rearrange("(r c) -> r c", c=P)
    one = lambda ap: ap.rearrange("(r c) -> r c", r=1)
    full = 8 * P
    src = [(C_MU, 8, P, row(A["rwkv_mu_2"][l, 0:full])),
           (C_MU + 8, 1, 32, one(A["rwkv_mu_2"][l, full:full + 32])),
           (C_W0, 2, P, row(A["rwkv_w0_2"][l])), (C_A0, 2, P, row(A["rwkv_a0_2"][l])),
           (C_KK, 2, P, row(A["rwkv_k_k_2"][l])), (C_KA, 2, P, row(A["rwkv_k_a_2"][l])),
           (C_RK, 2, P, row(A["rwkv_r_k_2"][l].rearrange("h d -> (h d)"))),
           (C_LG, 2, P, row(A["rwkv_lnx_g_2"][l])), (C_LB, 2, P, row(A["rwkv_lnx_b_2"][l])),
           (C_GLAB, 1, P, one(A["gla_gate_b_2"][l])),
           (C_L0, 2, P, row(A["hgrn_lb_logits_2"][0])), (C_L1, 2, P, row(A["hgrn_lb_logits_2"][1]))]
    if l > 0:
        src.append((C_V0, 2, P, row(A["rwkv_v0_2"][l - 1])))
    twice = [(C_HN, A["hgrn_norm_g_2"][l]), (C_GN, A["gla_norm_g_2"][l])]
    loaded, zeroed, turned, kept, diffed, lb_ready, *_ = m.stage()
    with ExitStack() as ctx:
        rows = m.sbuf(ctx, "prow", [C_N, P])
        diff = m.sbuf(ctx, "lb_diff", [P, 2])
        with nc.Block() as block:
            @block.sync
            def _(sp):
                m.clear_previous(sp)
                sp.wait_ge(zeroed, 1)
                for r, n, c, ap in src:
                    sp.dma_start(rows[r:r + n, 0:c], ap).then_inc(loaded, 16)
                for r, ap in twice:
                    for o in range(2):
                        sp.dma_start(rows[r:r + 1, o * HD:(o + 1) * HD], one(ap)).then_inc(loaded, 16)
                m.feed(sp, 0)

            @block.gpsimd
            def _(pool):
                nc.gpsimd.memset(rows[:], 0.0).then_inc(zeroed, 1)

            @block.tensor
            def _(pe):
                pe.wait_ge(loaded, 16 * (len(src) + 4))
                pe.transpose(m.ps[:, 0, 0:C_N], rows[:], m.ident[0:C_N, 0:C_N]).then_inc(turned, 1)

            @block.vector
            def _(dve):
                dve.wait_ge(turned, 1)
                dve.tensor_copy(cols[:], m.ps[:, 0, 0:C_N]).then_inc(kept, 1)
                dve.wait_ge(kept, 1)
                if l == 0:
                    dve.memset(lb[:, 0:2], 0.0)
                    dve.memset(lb[:, 2:4], 1.0)
                else:
                    dve.tensor_tensor(diff[:], cols[:, C_L1:C_L1 + 2], cols[:, C_L0:C_L0 + 2],
                                      ALU.subtract).then_inc(diffed, 1)
                    dve.wait_ge(lb_ready, 1)
                    dve.tensor_scalar(lb[:, 2:4], lb[:, 0:2], -1.0, 1.0, ALU.mult, ALU.add)

            if l > 0:
                @block.scalar
                def _(act):
                    act.wait_ge(diffed, 1)
                    act.activation(lb[:, 0:2], diff[:], ACT.Sigmoid).then_inc(lb_ready, 1)


def hgrn_project(m, qT, kT, gT, v, gate, lb):
    nc = m.nc
    ready, kept, tok_ready, tok_kept, f_ready, step, *_ = m.stage()
    with nc.Block() as block:
        @block.sync
        def _(sp):
            m.clear_previous(sp)
            m.feed(sp, 2)

        @block.tensor
        def _(pe):
            tile = [(i * P, (i + 1) * P) for i in range(4)]
            project_cols(m, pe, m.take(pe, KT), tile, (0, 1, 2, 3), 0, ready, kept)
            released(m, pe, ready, 4)
            w = m.take(pe, KT)
            project_tok(m, pe, w, m.hT, (0, GROUP), (4, 5, 6, 7), 0, tok_ready, tok_kept)
            project_cols(m, pe, w, tile[2:], (0, 1, 2, 3), 4, ready, kept)
            released(m, pe, ready, 6)

        @block.scalar
        def _(act):
            for n in range(6):
                act.wait_ge(ready, n + 1)
                dst, f = ((qT, ACT.Silu), (gT, ACT.Sigmoid), (gate, ACT.Silu))[n // 2]
                act.activation(dst[:, n % 2, :], m.ps[:, n % 4, :], f).then_inc(kept, 1)
            for j in range(2):
                act.wait_ge(f_ready, j + 1)
                act.activation(gT[:, j, :], gT[:, j, :], ACT.Ln)

        @block.vector
        def _(dve):
            do = Step(dve, step)
            for j in range(2):
                dve.wait_ge(kept, 3 + j)
                do(dve.tensor_scalar(gT[:, j, :], gT[:, j, :], lb[:, 2 + j:3 + j], lb[:, j:j + 1], ALU.mult, ALU.add))
                do(dve.tensor_scalar(kT[:, j, :], gT[:, j, :], -1.0, 1.0, ALU.mult, ALU.add))
                dve.tensor_scalar(gT[:, j, :], gT[:, j, :], 1e-19, None, ALU.max).then_inc(f_ready, 1)
            for tt in range(TT):
                dve.wait_ge(tok_ready, tt + 1)
                dve.tensor_copy(v[:, tt, :], m.ps[:, 4 + tt, 0:GROUP]).then_inc(tok_kept, 1)


def gla_project(m, qT, kT, gT, v, gate, w2, b_col):
    nc = m.nc
    (ready, kept, tok_ready, tok_kept, w_loaded, g_ready, x_ready, abs_ready, ln_ready, step, *_) = m.stage()
    with ExitStack() as ctx:
        lr = m.sbuf(ctx, "g_lr", [GLA_RANK, SEQ])
        w = m.sbuf(ctx, "gla_w2", [GLA_RANK, P])
        x = m.sbuf(ctx, "gla_x", [P, SEQ])
        e = m.sbuf(ctx, "gla_e", [P, SEQ])
        with nc.Block() as block:
            @block.sync
            def _(sp):
                m.clear_previous(sp)
                sp.dma_start(w[:], w2).then_inc(w_loaded, 16)
                m.feed(sp, 2)

            @block.tensor
            def _(pe):
                wa = m.take(pe, KT)
                project_cols(m, pe, wa, [(0, P), (P, 2 * P)], (0, 1, 2, 3), 0, ready, kept)
                project_tok(m, pe, wa, m.hT, (GROUP, 2 * GROUP), (4, 5, 6, 7), 0, tok_ready, tok_kept)
                released(m, pe, tok_ready, 4)
                r = GLA_RANK
                project_cols(m, pe, m.take(pe, KT), [(0, r), (r, r + P), (r + P, r + 2 * P)], (0, 1, 2, 3), 2,
                             ready, kept)
                released(m, pe, ready, 5)
                pe.wait_ge(w_loaded, 16)
                pe.wait_ge(kept, 3)
                pe.matmul(m.ps[:, 1, :], w[:], lr[:], start=True, stop=True).then_inc(g_ready, 1)

            @block.scalar
            def _(act):
                for n in range(5):
                    act.wait_ge(ready, n + 1)
                    src = m.ps[:, n % 4, :]
                    if n == 0:
                        act.mul(qT[:, 0, :], src, GLA_KEY ** -0.5).then_inc(kept, 1)
                    elif n == 1:
                        act.copy(kT[:, 0, :], src).then_inc(kept, 1)
                    elif n == 2:
                        act.copy(lr[:], m.ps[0:GLA_RANK, n, :]).then_inc(kept, 1)
                    else:
                        act.activation(gate[:, n - 3, :], src, ACT.Silu).then_inc(kept, 1)
                act.wait_ge(x_ready, 1)
                act.activation(e[:], x[:], ACT.Abs).then_inc(abs_ready, 1)
                act.wait_ge(abs_ready, 1)
                act.activation(e[:], e[:], ACT.Exp, scale=-1.0).then_inc(abs_ready, 1)
                act.wait_ge(abs_ready, 2)
                act.activation(e[:], e[:], ACT.Ln, bias=1.0).then_inc(ln_ready, 1)

            @block.vector
            def _(dve):
                for tt in range(TT):
                    dve.wait_ge(tok_ready, tt + 1)
                    dve.tensor_copy(v[:, tt, :], m.ps[:, 4 + tt, 0:GROUP]).then_inc(tok_kept, 1)
                do = Step(dve, step)
                dve.wait_ge(g_ready, 1)
                dve.tensor_scalar(x[:], m.ps[:, 1, :], b_col, None, ALU.add).then_inc(x_ready, 1)
                dve.wait_ge(ln_ready, 1)
                do(dve.tensor_scalar(x[:], x[:], 0.0, None, ALU.min))
                do(dve.tensor_tensor(x[:], x[:], e[:], ALU.subtract))
                do(dve.tensor_scalar(gT[:, 0, :], x[:], 1.0 / 16, None, ALU.mult))


def gated_linear_stage(m, nt, width, qT, kT, gT, v, gate, norm_col, out_tile):
    nc = m.nc
    (loaded, cum_ready, diff_ready, exp_ready, ql_ready, kl_ready, level_ready, level_kept, dec_ready, kdec_turned,
     kdec_kept, delta_ready, state_ready, o_ready, ms_ready, rs_ready, y_ready, y_turned, step, half_ready,
     edec_ready, *_) = m.stage()
    NV = GROUP // nt
    delta = lambda c, j: m.ps[:, 2 + 2 * (c % 2) + c // 4, (c // 2 % 2 * nt + j) * NV:(c // 2 % 2 * nt + j + 1) * NV]
    place = (lambda h: (h // 2, h % 2 * HD)) if width == HD else (lambda h: (0, h * width))
    with ExitStack() as ctx:
        keep = m.sbuf(ctx, "keep", [P, SEQ])
        masks = m.sbuf(ctx, "masks", [P, LEVELS, P])
        cum = m.sbuf(ctx, "cum", [P, nt, SEQ])
        diff = m.sbuf(ctx, "diff", [P, nt, SEQ])
        ex = m.sbuf(ctx, "ex", [P, nt, SEQ])
        ql = m.sbuf(ctx, "ql", [P, 2, nt, SEQ])
        kl = m.sbuf(ctx, "kl", [P, 2, nt, SEQ])
        scores = m.sbuf(ctx, "scores", [P, 4, TT, P])
        qd = m.sbuf(ctx, "qd", [P, nt, SEQ])
        kd_tok = m.sbuf(ctx, "kd_tok", [P, TT, nt * P])
        pend = m.sbuf(ctx, "pend", [P, nt, NC])
        state = m.sbuf(ctx, "state", [P, NC, nt, NV])
        own = m.sbuf(ctx, "own", [P, NV])
        y = m.sbuf(ctx, "y", [P, TT, GROUP])
        sq = m.sbuf(ctx, "sq", [P, GROUP])
        ms = m.sbuf(ctx, "ms", [P, TT, 4])
        rs = m.sbuf(ctx, "rs", [P, TT, 4])
        half = m.sbuf(ctx, "half", [P, TT, 4])
        kd = kl[:, 1]
        by_chunk = lambda t, j: t[:, j, :].rearrange("p (c t) -> p c t", c=NC)
        with nc.Block() as block:
            @block.sync
            def _(sp):
                m.clear_previous(sp)
                sp.dma_start(keep[:], m.table("keep")).then_inc(loaded, 16)
                sp.dma_start(masks[:].rearrange("p s t -> p (s t)"), m.table("levels")).then_inc(loaded, 16)
                sp.dma_start(own[:], m.table("halves" if nt == 2 else "quarters")).then_inc(loaded, 16)
                m.feed(sp, 0)

            @block.tensor
            def _(pe):
                m.warm_up(pe, 7)
                for lv in range(-1, LEVELS):
                    if lv == 0:
                        pe.wait_ge(dec_ready, 1)
                        pe.wait_ge(level_kept, 4)
                        for tt in range(TT):
                            for j in range(nt):
                                n = tt * nt + j
                                mm = pe.transpose(m.ps[:, n // 4, n % 4 * P:(n % 4 + 1) * P],
                                                  kd[:, j, tt * P:(tt + 1) * P], m.ident[:])
                        mm.then_inc(kdec_turned, 1)
                        pe.wait_ge(kdec_kept, 1)
                        for c in range(NC):
                            o, tt = c % 2 * CH, c // 2
                            for j in range(nt):
                                mm = pe.matmul(delta(c, j), kd_tok[o:o + CH, tt, j * P:(j + 1) * P],
                                               v[o:o + CH, tt, j * NV:(j + 1) * NV], start=True, stop=True)
                        mm.then_inc(delta_ready, 1)
                        m.warm_up(pe, 7, 8)
                        pe.wait_ge(state_ready, 1)
                    if lv >= 1:
                        pe.wait_ge(level_kept, 4 * (lv + 1) - 7)
                        m.warm_up(pe, 4 * ((lv + 1) % 2), 2)
                    if lv >= 0:
                        pe.wait_ge(ql_ready, lv + 1)
                        pe.wait_ge(kl_ready, lv + 1)
                    for h in range(4):
                        j, at = place(h)
                        bank = 4 * ((lv + 1) % 2) + h
                        n = 4 * (lv + 1) + h
                        if n >= 8:
                            pe.wait_ge(level_kept, n - 7)
                        q_, k_ = (qT, kT) if lv < 0 else (ql[:, lv % 2], kl[:, lv % 2])
                        for tt in range(TT):
                            mm = pe.matmul(m.ps[:, bank, tt * P:(tt + 1) * P],
                                           k_[at:at + width, j, tt * P:(tt + 1) * P],
                                           q_[at:at + width, j, tt * P:(tt + 1) * P], start=True, stop=True)
                        mm.then_inc(level_ready, 1)
                pe.wait_ge(level_kept, 4 * (LEVELS + 1))
                for tt in range(TT):
                    for h in range(4):
                        pe.matmul(m.ps[:, tt, h * HD:(h + 1) * HD], scores[:, h, tt, :],
                                  v[:, tt, h * HD:(h + 1) * HD], start=(h == 0), stop=False,
                                  skip_group_check=True)
                    for c in (2 * tt, 2 * tt + 1):
                        o = c % 2 * CH
                        for j in range(nt):
                            mm = pe.matmul(m.ps[o:o + CH, tt, j * NV:(j + 1) * NV], qd[:, j, c * CH:(c + 1) * CH],
                                           state[:, c, j, :], start=False, stop=(j == nt - 1),
                                           skip_group_check=True)
                    mm.then_inc(o_ready, 1)
                for tt in range(TT):
                    pe.wait_ge(y_ready, tt + 1)
                    for j in range(2):
                        mm = pe.transpose(m.ps[:, 4 + j, tt * P:(tt + 1) * P], y[:, tt, j * P:(j + 1) * P], m.ident[:])
                    mm.then_inc(y_turned, 1)

            @block.scalar
            def _(act):
                act.wait_ge(cum_ready, 1)
                act.activation(ex[:], cum[:], ACT.Exp).then_inc(edec_ready, 1)
                act.activation(pend[:], cum[:].rearrange("p j (c t) -> p j c t", t=CH)[:, :, :, CH - 1],
                               ACT.Exp).then_inc(edec_ready, 1)
                act.wait_ge(diff_ready, 1)
                act.wait_ge(dec_ready, 1)
                act.activation(ex[:], diff[:], ACT.Exp).then_inc(edec_ready, 1)
                for lv in range(LEVELS):
                    act.wait_ge(diff_ready, lv + 2)
                    if lv == 0:
                        act.wait_ge(dec_ready, 2)
                    else:
                        act.wait_ge(ql_ready, lv)
                        act.wait_ge(kl_ready, lv)
                    act.activation(ex[:], diff[:], ACT.Exp).then_inc(exp_ready, 1)
                act.wait_ge(kdec_turned, 1)

            @block.gpsimd
            def _(pool):
                nc.gpsimd.memset(half[:], -0.5).then_inc(half_ready, 1)
                for lv in range(LEVELS):
                    pool.wait_ge(exp_ready, lv + 1)
                    if lv >= 1:
                        pool.wait_ge(level_ready, 4 * lv)
                    if lv == 1:
                        pool.wait_ge(kdec_turned, 1)
                    nc.gpsimd.tensor_tensor(kl[:, lv % 2], kT[:, 0:nt], ex[:], ALU.mult).then_inc(kl_ready, 1)
                pool.wait_ge(half_ready, 1)
                pool.wait_ge(ms_ready, 1)
                nc.gpsimd.tensor_tensor(rs[:], ms[:], half[:], ALU.pow).then_inc(rs_ready, 1)

            @block.vector
            def _(dve):
                do = Step(dve, step)

                def middle(lv):
                    s = 1 << lv
                    if lv == 0:
                        dve.wait_ge(edec_ready, 3)
                    else:
                        dve.wait_ge(exp_ready, lv)
                    for j in range(nt):
                        cb = cum[:, j, :].rearrange("p (b t) -> p b t", t=2 * s)
                        db = diff[:, j, :].rearrange("p (b t) -> p b t", t=2 * s)
                        mid = cb[:, :, s - 1:s].to_broadcast([P, SEQ // (2 * s), s])
                        dve.tensor_tensor(db[:, :, 0:s], mid, cb[:, :, 0:s], ALU.subtract)
                        ins = dve.tensor_tensor(db[:, :, s:2 * s], cb[:, :, s:2 * s], mid, ALU.subtract)
                    ins.then_inc(diff_ready, 1)

                def take(lv):
                    for h in range(4):
                        dve.wait_ge(level_ready, 4 * (lv + 1) + h + 1)
                        mask = m.ident[:] if lv < 0 else masks[:, lv, :]
                        dve.copy_predicated(scores[:, h], mask.bitcast(I32).unsqueeze(1).to_broadcast([P, TT, P]),
                                            m.ps[:, 4 * ((lv + 1) % 2) + h, :].rearrange("p (t i) -> p t i", t=TT)
                                            ).then_inc(level_kept, 1)

                do(dve.memset(scores[:], 0.0))
                do(dve.memset(state[:, 0], 0.0))
                dve.wait_ge(loaded, 48)
                for j in range(nt):
                    ins = dve.tensor_tensor_scan(cum[:, j, :], keep[:], gT[:, j, :], 0.0, ALU.mult, ALU.add)
                    if j < nt - 1:
                        do(ins)
                ins.then_inc(cum_ready, 1)
                dve.wait_ge(cum_ready, 1)
                for j in range(nt):
                    cb = by_chunk(cum, j)
                    ins = dve.tensor_tensor(by_chunk(diff, j), cb[:, :, CH - 1:CH].to_broadcast([P, NC, CH]), cb,
                                            ALU.subtract)
                ins.then_inc(diff_ready, 1)
                dve.wait_ge(edec_ready, 2)
                dve.tensor_tensor(qd[:], qT[:, 0:nt], ex[:], ALU.mult).then_inc(dec_ready, 1)
                dve.wait_ge(edec_ready, 3)
                dve.tensor_tensor(kd[:], kT[:, 0:nt], ex[:], ALU.mult).then_inc(dec_ready, 1)
                take(-1)
                middle(0)
                dve.wait_ge(kdec_turned, 1)
                for n in range((nt * TT + 3) // 4):
                    ins = dve.tensor_copy(kd_tok[:].rearrange("p t f -> p (t f)")[:, n * 512:(n + 1) * 512],
                                          m.ps[:, n, :])
                ins.then_inc(kdec_kept, 1)
                dve.wait_ge(delta_ready, 1)
                for c in range(NC - 1):
                    for j in range(nt):
                        do(dve.scalar_tensor_tensor(state[:, c + 1, j, :], state[:, c, j, :], pend[:, j, c:c + 1],
                                                    delta(c, j), ALU.mult, ALU.add))
                st = state[:].rearrange("p c j v -> p (c j) v")
                dve.tensor_tensor(st, st, own[:].unsqueeze(1).to_broadcast([P, NC * nt, NV]),
                                  ALU.mult).then_inc(state_ready, 1)
                for lv in range(LEVELS):
                    dve.wait_ge(exp_ready, lv + 1)
                    if lv >= 2:
                        dve.wait_ge(level_ready, 4 * lv)
                    dve.tensor_tensor(ql[:, lv % 2], qT[:, 0:nt], ex[:], ALU.mult).then_inc(ql_ready, 1)
                    if lv + 1 < LEVELS:
                        middle(lv + 1)
                    take(lv)
                for tt in range(TT):
                    dve.wait_ge(o_ready, tt + 1)
                    do(dve.tensor_copy(y[:, tt, :], m.ps[:, tt, 0:GROUP]))
                    do(dve.tensor_tensor(sq[:], y[:, tt, :], y[:, tt, :], ALU.mult))
                    do(dve.reduce_sum(ms[:, tt, :], sq[:].rearrange("p (h d) -> p h d", h=4), AX.X))
                dve.tensor_scalar(ms[:], ms[:], 1.0 / HD, RMS_EPS, ALU.mult, ALU.add).then_inc(ms_ready, 1)
                dve.wait_ge(rs_ready, 1)
                for tt in range(TT):
                    y3 = y[:, tt, :].rearrange("p (h d) -> p h d", h=4)
                    dve.tensor_tensor(y3, y3, rs[:, tt, :].unsqueeze(2).to_broadcast([P, 4, HD]),
                                      ALU.mult).then_inc(y_ready, 1)
                dve.wait_ge(y_turned, TT)
                for j in range(2):
                    dve.scalar_tensor_tensor(m.mixT[:, out_tile + j, :], m.ps[:, 4 + j, :], norm_col, gate[:, j, :],
                                             ALU.mult, ALU.mult)


def hgrn_mixer(m, cols, lb):
    with ExitStack() as ctx:
        qT, kT, gT, gate = (m.sbuf(ctx, n, [P, 2, SEQ]) for n in ("hg_qT", "hg_kT", "hg_gT", "hg_gate"))
        v = m.sbuf(ctx, "hg_v", [P, TT, GROUP])
        hgrn_project(m, qT, kT, gT, v, gate, lb)
        gated_linear_stage(m, 2, HD, qT, kT, gT, v, gate, cols[:, C_HN:C_HN + 1], 0)


def gla_mixer(m, l, A, cols):
    with ExitStack() as ctx:
        qT, kT, gT = (m.sbuf(ctx, n, [P, 1, SEQ]) for n in ("gl_qT", "gl_kT", "gl_gT"))
        gate = m.sbuf(ctx, "gl_gate", [P, 2, SEQ])
        v = m.sbuf(ctx, "gl_v", [P, TT, GROUP])
        gla_project(m, qT, kT, gT, v, gate, A["gla_gate_w2_2"][l], cols[:, C_GLAB:C_GLAB + 1])
        gated_linear_stage(m, 1, GLA_KEY, qT, kT, gT, v, gate, cols[:, C_GN:C_GN + 1], 2)


LNX_EPS = 64e-5
TWO_PI = 2 * np.pi


def rwkv_project(m, mixed, cols):
    nc = m.nc
    ready, kept, raw_ready, raw_used, step, zeroed, *_ = m.stage()
    with ExitStack() as ctx:
        raw = m.sbuf(ctx, "rw_raw", [P, 2, SEQ + 1])
        d = m.sbuf(ctx, "rw_d", [P, SEQ])
        with nc.Block() as block:
            @block.sync
            def _(sp):
                m.clear_previous(sp)
                m.feed(sp, 3)

            @block.gpsimd
            def _(pool):
                nc.gpsimd.memset(raw[:, :, 0:1], 0.0).then_inc(zeroed, 1)

            @block.tensor
            def _(pe):
                tile = [(i * P, (i + 1) * P) for i in range(4)]
                for first, cs in ((0, tile), (4, tile), (8, [(0, 32)])):
                    project_cols(m, pe, m.take(pe, KT), cs, (0, 1, 2, 3), first, ready, kept)
                    released(m, pe, ready, first + len(cs))

            @block.scalar
            def _(act):
                for n in range(9):
                    p = P if n < 8 else 32
                    act.wait_ge(ready, n + 1)
                    if n >= 2:
                        act.wait_ge(raw_used, n - 1)
                    act.copy(raw[0:p, n % 2, 1:], m.ps[0:p, n % 4, :]).then_inc(kept, 1)

            @block.vector
            def _(dve):
                do = Step(dve, step)
                dve.wait_ge(zeroed, 1)
                for n in range(9):
                    p = P if n < 8 else 32
                    dve.wait_ge(kept, n + 1)
                    do(dve.tensor_tensor(d[0:p], raw[0:p, n % 2, 0:SEQ], raw[0:p, n % 2, 1:], ALU.subtract))
                    dve.scalar_tensor_tensor(mixed[0:p, n, :], d[0:p], cols[0:p, C_MU + n:C_MU + n + 1],
                                             raw[0:p, n % 2, 1:], ALU.mult, ALU.add).then_inc(raw_used, 1)
                    dve.wait_ge(raw_used, n + 1)


def rwkv_prepare(m, l, A, cols, mixed, rho, kap, bet, khat, gate, bonus, pend):
    nc = m.nc
    (w_loaded, low_ready, u_ready, a_ready, g_ready, v1_ready, t1_ready, v2_ready, vs_ready, sq_ready, ss_ready,
     floor_ready, sqrt_ready, ld_ready, a_kept, cum_ready, ex_ready, rk_ready, rk_summed, step, *_) = m.stage()
    with ExitStack() as ctx:
        wa = m.sbuf(ctx, "w2a2", [P, GROUP])
        g2 = m.sbuf(ctx, "g2", [P, 2, GROUP])
        v1 = m.sbuf(ctx, "v1", [P, 2, V_RANK])
        v2 = m.sbuf(ctx, "v2", [V_RANK, GROUP])
        halves = m.sbuf(ctx, "halves", [P, P])
        keep = m.sbuf(ctx, "keep", [P, SEQ])
        th = m.sbuf(ctx, "th", [W_RANK, SEQ])
        t1 = m.sbuf(ctx, "t1", [V_RANK, SEQ])
        kk, sq, ld, cum, a, nrm = (m.sbuf(ctx, n, [P, 2, SEQ]) for n in ("kk", "sq", "ld", "cum", "a", "nrm"))
        r, k, v = mixed[:, 0:2], mixed[:, 2:4], mixed[:, 4:6]
        n_loads = 6 + (2 if l else 0)
        col = lambda c, j: cols[:, c + j:c + j + 1]
        with nc.Block() as block:
            @block.sync
            def _(sp):
                m.clear_previous(sp)
                sp.dma_start(wa[0:W_RANK], A["rwkv_w2_2"][l]).then_inc(w_loaded, 16)
                sp.dma_start(wa[W_RANK:P], A["rwkv_a2_2"][l]).then_inc(w_loaded, 16)
                sp.dma_start(g2[:, 0], A["rwkv_g2_2"][l, 0:P]).then_inc(w_loaded, 16)
                sp.dma_start(g2[0:32, 1], A["rwkv_g2_2"][l, P:G_RANK]).then_inc(w_loaded, 16)
                sp.dma_start(halves[:], m.table("halves")).then_inc(w_loaded, 16)
                sp.dma_start(keep[:], m.table("keep")).then_inc(w_loaded, 16)
                if l:
                    sp.dma_start(v1[:], A["rwkv_v1_2"][l - 1].rearrange("(j p) c -> p j c", p=P)).then_inc(w_loaded, 16)
                    sp.dma_start(v2[:], A["rwkv_v2_2"][l - 1]).then_inc(w_loaded, 16)
                m.feed(sp, 0)

            @block.tensor
            def _(pe):
                m.warm_up(pe, 7)
                pe.wait_ge(w_loaded, 16 * n_loads)
                for j in range(2):
                    mm = pe.matmul(m.ps[:, 2 + j, :], wa[W_RANK:P, j * P:(j + 1) * P], mixed[W_RANK:P, 6, :],
                                   start=True, stop=True)
                mm.then_inc(a_ready, 1)
                pe.wait_ge(low_ready, 1)
                for j in range(2):
                    mm = pe.matmul(m.ps[:, j, :], wa[0:W_RANK, j * P:(j + 1) * P], th[:], start=True, stop=True)
                mm.then_inc(u_ready, 1)
                pe.wait_ge(low_ready, 3)
                for j in range(2):
                    pe.matmul(m.ps[:, 4 + j, :], g2[:, 0, j * P:(j + 1) * P], mixed[:, 7, :], start=True, stop=False)
                    mm = pe.matmul(m.ps[:, 4 + j, :], g2[0:32, 1, j * P:(j + 1) * P], mixed[0:32, 8, :],
                                   start=False, stop=True)
                mm.then_inc(g_ready, 1)
                if l:
                    for j in range(2):
                        mm = pe.matmul(m.ps[0:V_RANK, 6, :], v1[:, j, :], v[:, j, :], start=(j == 0), stop=(j == 1))
                    mm.then_inc(v1_ready, 1)
                    pe.wait_ge(t1_ready, 1)
                    for j in range(2):
                        mm = pe.matmul(m.ps[:, 6 + j, :], v2[:, j * P:(j + 1) * P], t1[:], start=True, stop=True)
                    mm.then_inc(v2_ready, 1)
                pe.wait_ge(sq_ready, 1)
                pe.wait_ge(ld_ready, 1)
                for j in range(2):
                    mm = pe.matmul(m.ps[:, j, :], halves[:], sq[:, j, :], start=True, stop=True)
                mm.then_inc(ss_ready, 1)
                pe.wait_ge(rk_ready, 1)
                pe.wait_ge(a_kept, 1)
                for j in range(2):
                    mm = pe.matmul(m.ps[:, 2 + j, :], halves[:], sq[:, j, :], start=True, stop=True)
                mm.then_inc(rk_summed, 1)

            @block.scalar
            def _(act):
                act.activation(th[:], mixed[0:W_RANK, 6, :], ACT.Tanh).then_inc(low_ready, 1)
                act.activation(mixed[:, 7, :], mixed[:, 7, :], ACT.Sigmoid).then_inc(low_ready, 1)
                act.activation(mixed[0:32, 8, :], mixed[0:32, 8, :], ACT.Sigmoid).then_inc(low_ready, 1)
                act.wait_ge(a_ready, 1)
                for j in range(2):
                    ins = act.activation(a[:, j, :], m.ps[:, 2 + j, :], ACT.Sigmoid, bias=col(C_A0, j))
                ins.then_inc(a_kept, 1)
                act.wait_ge(u_ready, 1)
                for j in range(2):
                    ins = act.activation(ld[:, j, :], m.ps[:, j, :], ACT.Sigmoid, bias=col(C_W0, j))
                ins.then_inc(ld_ready, 1)
                if l:
                    act.wait_ge(v1_ready, 1)
                    act.copy(t1[:], m.ps[0:V_RANK, 6, :]).then_inc(t1_ready, 1)
                    act.wait_ge(v2_ready, 1)
                    for j in range(2):
                        ins = act.activation(nrm[:, j, :], m.ps[:, 6 + j, :], ACT.Sigmoid, bias=col(C_V0, j))
                    ins.then_inc(vs_ready, 1)
                act.wait_ge(g_ready, 1)
                act.copy(gate[:], m.ps[:, 4:6, :])
                act.wait_ge(floor_ready, 1)
                act.activation(nrm[:], nrm[:], ACT.Sqrt).then_inc(sqrt_ready, 1)
                act.wait_ge(cum_ready, 1)
                act.activation(rho[:], cum[:], ACT.Exp)
                act.activation(bet[:], cum[:], ACT.Exp, scale=-1.0)
                act.activation(khat[:], cum[:], ACT.Exp, scale=-1.0)
                act.activation(pend[:], cum[:].rearrange("p j (c t) -> p j c t", t=CH)[:, :, :, CH - 1], ACT.Exp)
                act.activation(kap[:], kap[:], ACT.Exp).then_inc(ex_ready, 1)

            @block.vector
            def _(dve):
                do = Step(dve, step)
                for j in range(2):
                    do(dve.tensor_scalar(kk[:, j, :], k[:, j, :], col(C_KK, j), None, ALU.mult))
                dve.tensor_tensor(sq[:], kk[:], kk[:], ALU.mult).then_inc(sq_ready, 1)
                dve.wait_ge(ld_ready, 1)
                do(dve.tensor_scalar(ld[:], ld[:], -float(np.exp(-0.5)), None, ALU.mult))
                dve.wait_ge(w_loaded, 16 * n_loads)
                for j in range(2):
                    do(dve.tensor_tensor_scan(cum[:, j, :], keep[:], ld[:, j, :], 0.0, ALU.mult, ALU.add))
                dve.tensor_tensor(kap[:], cum[:], ld[:], ALU.subtract).then_inc(cum_ready, 1)
                if l:
                    dve.wait_ge(vs_ready, 1)
                    dve.wait_ge(cum_ready, 1)
                    do(dve.tensor_tensor(ld[:], m.v_first[:], v, ALU.subtract))
                    do(dve.tensor_tensor(ld[:], ld[:], nrm[:], ALU.mult))
                    do(dve.tensor_tensor(v, v, ld[:], ALU.add))
                else:
                    do(dve.tensor_copy(m.v_first[:], v))
                dve.wait_ge(ss_ready, 1)
                dve.tensor_scalar(nrm[:], m.ps[:, 0:2, :], 1e-24, None, ALU.max).then_inc(floor_ready, 1)
                dve.wait_ge(sqrt_ready, 1)
                do(dve.reciprocal(nrm[:], nrm[:]))
                do(dve.tensor_tensor(kk[:], kk[:], nrm[:], ALU.mult))
                dve.wait_ge(a_kept, 1)
                for j in range(2):
                    do(dve.tensor_scalar(nrm[:, j, :], a[:, j, :], -1.0, col(C_KA, j), ALU.add, ALU.mult))
                do(dve.scalar_tensor_tensor(k, nrm[:], 1.0, k, ALU.add, ALU.mult))
                do(dve.tensor_tensor(a[:], a[:], kk[:], ALU.mult))
                do(dve.tensor_tensor(sq[:], r, k, ALU.mult))
                for j in range(2):
                    ins = dve.tensor_scalar(sq[:, j, :], sq[:, j, :], col(C_RK, j), None, ALU.mult)
                ins.then_inc(rk_ready, 1)
                dve.wait_ge(ex_ready, 1)
                do(dve.tensor_tensor(rho[:], rho[:], r, ALU.mult))
                do(dve.tensor_tensor(kap[:], kap[:], kk[:], ALU.mult))
                do(dve.tensor_tensor(bet[:], bet[:], a[:], ALU.mult))
                do(dve.tensor_tensor(khat[:], khat[:], k, ALU.mult))
                dve.wait_ge(rk_summed, 1)
                do(dve.tensor_tensor(bonus[:], m.ps[:, 2:4, :], v, ALU.mult))


def turn_stage(m, pairs):
    nc = m.nc
    turned, *_ = m.stage()
    with nc.Block() as block:
        @block.sync
        def _(sp):
            m.clear_previous(sp)
            m.feed(sp, 0)

        @block.tensor
        def _(pe):
            for i, (src, _dst) in enumerate(pairs):
                for n in range(2):
                    for t in range(2):
                        for j in range(2):
                            tt = 2 * n + t
                            mm = pe.transpose(m.ps[:, 2 * i + n, (2 * t + j) * P:(2 * t + j + 1) * P],
                                              src[:, j, tt * P:(tt + 1) * P], m.ident[:])
                    mm.then_inc(turned, 1)

        def copies(eng, copy, odd):
            for i, (_src, dst) in enumerate(pairs):
                for n in range(2):
                    if n == odd:
                        eng.wait_ge(turned, 2 * i + n + 1)
                        copy(dst[:, 2 * n:2 * n + 2, :].rearrange("p t f -> p (t f)"), m.ps[:, 2 * i + n, :])

        @block.scalar
        def _(act):
            copies(act, act.copy, 0)

        @block.vector
        def _(dve):
            copies(dve, dve.tensor_copy, 1)


def rwkv_inverse(m, kap, bet, khat, kap_tok, v_tok, uT, w):
    nc = m.nc
    (loaded, l_ready, l_kept, init, as_ready, b_ready, b_kept, xy_ready, x_kept, y_kept, u_ready, vp_ready, vp_kept,
     w_ready, step, *_) = m.stage()
    with ExitStack() as ctx:
        LbT, LkT, X, Y, B, As = (m.sbuf(ctx, n, [P, 4, TT, P]) for n in ("LbT", "LkT", "X", "Y", "B", "As"))
        before = m.sbuf(ctx, "before", [P, P])
        masks = m.sbuf(ctx, "masks", [P, LEVELS, P])
        vp = LkT[:, 0:2]
        wide = lambda t: t.rearrange("p t i -> p (t i)")
        with nc.Block() as block:
            @block.sync
            def _(sp):
                m.clear_previous(sp)
                sp.dma_start(before[:], m.table("before")).then_inc(loaded, 16)
                sp.dma_start(masks[:].rearrange("p s t -> p (s t)"), m.table("levels")).then_inc(loaded, 16)
                m.feed(sp, 0)

            @block.tensor
            def _(pe):
                for i, lhs in enumerate((bet, khat)):
                    for h in range(4):
                        j, at = h // 2, h % 2 * HD
                        for tt in range(TT):
                            mm = pe.matmul(m.ps[:, 4 * i + h, tt * P:(tt + 1) * P],
                                           lhs[at:at + HD, j, tt * P:(tt + 1) * P],
                                           kap[at:at + HD, j, tt * P:(tt + 1) * P], start=True, stop=True)
                        mm.then_inc(l_ready, 1)
                pe.wait_ge(init, 1)
                for lv in range(LEVELS):
                    for h in range(4):
                        n = 4 * lv + h
                        pe.wait_ge(as_ready, n + 1)
                        if lv == 0:
                            pe.wait_ge(l_kept, h + 1)
                        else:
                            pe.wait_ge(x_kept, n - 3)
                        for tt in range(TT):
                            mm = pe.matmul(m.ps[:, h, tt * P:(tt + 1) * P], As[:, h, tt, :], X[:, h, tt, :],
                                           start=True, stop=True)
                        mm.then_inc(b_ready, 1)
                    for h in range(4):
                        n = 4 * lv + h
                        bank = 4 + 2 * (h % 2)
                        pe.wait_ge(b_kept, n + 1)
                        if lv:
                            pe.wait_ge(y_kept, n - 3)
                        if n >= 2:
                            pe.wait_ge(y_kept, n - 1)
                        elif n == 0:
                            pe.wait_ge(l_kept, 8)
                        for tt in range(TT):
                            pe.matmul(m.ps[:, bank, tt * P:(tt + 1) * P], Y[:, h, tt, :], B[:, h, tt, :],
                                      start=True, stop=True)
                            mm = pe.matmul(m.ps[:, bank + 1, tt * P:(tt + 1) * P], B[:, h, tt, :], Y[:, h, tt, :],
                                           start=True, stop=True)
                        mm.then_inc(xy_ready, 1)
                pe.wait_ge(y_kept, 4 * LEVELS)
                for h in range(4):
                    o = h % 2 * HD
                    for tt in range(TT):
                        mm = pe.matmul(m.ps[o:o + HD, h // 2, tt * P:(tt + 1) * P],
                                       kap_tok[:, tt, h * HD:(h + 1) * HD], Y[:, h, tt, :], start=True, stop=True)
                mm.then_inc(u_ready, 1)
                for tt in range(TT):
                    for h in range(4):
                        at = tt % 2 * GROUP + h * HD
                        mm = pe.matmul(m.ps[:, 2 + tt // 2, at:at + HD], LkT[:, h, tt, :],
                                       v_tok[:, tt, h * HD:(h + 1) * HD], start=True, stop=True)
                mm.then_inc(vp_ready, 1)
                pe.wait_ge(vp_kept, 2)
                for tt in range(TT):
                    for h in range(4):
                        at = tt % 2 * GROUP + h * HD
                        mm = pe.matmul(m.ps[:, 4 + tt // 2, at:at + HD], Y[:, h, tt, :],
                                       wide(vp[:, tt // 2])[:, at:at + HD], start=True, stop=True)
                mm.then_inc(w_ready, 1)

            @block.gpsimd
            def _(pool):
                for lv in range(LEVELS):
                    for h in range(4):
                        n = 4 * lv + h
                        if lv == 0:
                            pool.wait_ge(l_kept, h + 1)
                        else:
                            pool.wait_ge(b_ready, n - 3)
                        nc.gpsimd.tensor_tensor(As[:, h], LbT[:, h],
                                                masks[:, lv, :].unsqueeze(1).to_broadcast([P, TT, P]),
                                                ALU.mult).then_inc(as_ready, 1)

            @block.scalar
            def _(act):
                for n in range(4 * LEVELS):
                    h = n % 4
                    act.wait_ge(b_ready, n + 1)
                    if n >= 4:
                        act.wait_ge(xy_ready, n - 3)
                    act.copy(wide(B[:, h]), m.ps[:, h, :]).then_inc(b_kept, 1)
                act.wait_ge(u_ready, 1)
                act.copy(uT[:], m.ps[:, 0:2, :])

            @block.vector
            def _(dve):
                ident = m.ident[:].unsqueeze(1).to_broadcast([P, TT, P])
                for h in range(4):
                    dve.tensor_copy(X[:, h], ident)
                    ins = dve.tensor_copy(Y[:, h], ident)
                ins.then_inc(init, 1)
                dve.wait_ge(init, 1)
                dve.wait_ge(loaded, 32)
                for n in range(8):
                    dve.wait_ge(l_ready, n + 1)
                    dst = (LbT, LkT)[n // 4]
                    dve.tensor_tensor(dst[:, n % 4], m.ps[:, n, :].rearrange("p (t i) -> p t i", t=TT),
                                      before[:].unsqueeze(1).to_broadcast([P, TT, P]), ALU.mult).then_inc(l_kept, 1)
                for n in range(4 * LEVELS):
                    h = n % 4
                    bank = 4 + 2 * (h % 2)
                    dve.wait_ge(xy_ready, n + 1)
                    if n >= 4:
                        dve.wait_ge(y_kept, n - 3)
                    dve.tensor_tensor(wide(X[:, h]), wide(X[:, h]), m.ps[:, bank, :], ALU.subtract).then_inc(x_kept, 1)
                    dve.tensor_tensor(wide(Y[:, h]), wide(Y[:, h]), m.ps[:, bank + 1, :],
                                      ALU.subtract).then_inc(y_kept, 1)
                dve.wait_ge(vp_ready, 1)
                for i in range(2):
                    dve.tensor_copy(wide(vp[:, i]), m.ps[:, 2 + i, :]).then_inc(vp_kept, 1)
                dve.wait_ge(w_ready, 1)
                for i in range(2):
                    dve.tensor_copy(w[:, 2 * i:2 * i + 2, :].rearrange("p t f -> p (t f)"), m.ps[:, 4 + i, :])


def rwkv_scan(m, cols, rho, bet, khat, bet_tok, kh_tok, v_tok, uT, w, pend, gate, bonus):
    nc = m.nc
    (loaded, m_ready, m_kept, pm_ready, sa_ready, sa_kept, d_ready, s_ready, o_ready, var_ready, rs_ready, y_ready,
     y_turned, half_ready, step, *_) = m.stage()
    with ExitStack() as ctx:
        MbT, MkT = (m.sbuf(ctx, n, [P, 4, TT, P]) for n in ("MbT", "MkT"))
        upto = m.sbuf(ctx, "upto", [P, P])
        halves = m.sbuf(ctx, "halves", [P, P])
        pm = m.sbuf(ctx, "pm", [P, NC, 2, P])
        state = m.sbuf(ctx, "state", [P, NC, 2, P])
        sa = m.sbuf(ctx, "sa", [P, TT, GROUP])
        t = m.sbuf(ctx, "t", [P, 2, P])
        y = m.sbuf(ctx, "y", [P, TT, GROUP])
        yl = m.sbuf(ctx, "yl", [P, 2, SEQ])
        stats = m.sbuf(ctx, "stats", [P, TT, 4, 6])
        mv = m.sbuf(ctx, "mv", [P, TT, 4, 2])
        rs = m.sbuf(ctx, "rs", [P, TT, 4])
        half = m.sbuf(ctx, "half", [P, TT, 4])
        with nc.Block() as block:
            @block.sync
            def _(sp):
                m.clear_previous(sp)
                sp.dma_start(upto[:], m.table("upto")).then_inc(loaded, 16)
                sp.dma_start(halves[:], m.table("halves")).then_inc(loaded, 16)
                m.feed(sp, 0)

            @block.gpsimd
            def _(pool):
                nc.gpsimd.memset(half[:], -0.5).then_inc(half_ready, 1)
                pool.wait_ge(loaded, 32)
                for c in range(NC - 1):
                    nc.gpsimd.tensor_tensor(pm[:, c], halves[:].unsqueeze(1).to_broadcast([P, 2, P]),
                                            pend[:, :, c:c + 1].to_broadcast([P, 2, P]), ALU.mult).then_inc(pm_ready, 1)
                pool.wait_ge(half_ready, 1)
                pool.wait_ge(var_ready, 1)
                nc.gpsimd.tensor_tensor(rs[:], mv[:, :, :, 1], half[:], ALU.pow).then_inc(rs_ready, 1)

            @block.tensor
            def _(pe):
                m.warm_up(pe, 7)
                for i, lhs in enumerate((bet, khat)):
                    for h in range(4):
                        j, at = h // 2, h % 2 * HD
                        if i:
                            pe.wait_ge(m_kept, h + 1)
                        for tt in range(TT):
                            mm = pe.matmul(m.ps[:, 4 + h, tt * P:(tt + 1) * P],
                                           lhs[at:at + HD, j, tt * P:(tt + 1) * P],
                                           rho[at:at + HD, j, tt * P:(tt + 1) * P], start=True, stop=True)
                        mm.then_inc(m_ready, 1)
                for c in range(NC):
                    o, tt = c % 2 * CH, c // 2
                    pe.wait_ge(s_ready, c + 1)
                    if c >= 2:
                        pe.wait_ge(sa_kept, c - 1)
                    for j in range(2):
                        mm = pe.matmul(m.ps[o:o + CH, c % 2, j * P:(j + 1) * P], uT[:, j, c * CH:(c + 1) * CH],
                                       state[:, c, j, :], start=True, stop=True)
                    mm.then_inc(sa_ready, 1)
                    if c < NC - 1:
                        pe.wait_ge(sa_kept, c + 1)
                        for j in range(2):
                            f = slice(j * P, (j + 1) * P)
                            pe.matmul(m.ps[:, 2 + c % 2, f], kh_tok[o:o + CH, tt, f], v_tok[o:o + CH, tt, f],
                                      start=True, stop=False)
                            mm = pe.matmul(m.ps[:, 2 + c % 2, f], bet_tok[o:o + CH, tt, f], sa[o:o + CH, tt, f],
                                           start=False, stop=True)
                        mm.then_inc(d_ready, 1)
                pe.wait_ge(sa_kept, NC)
                pe.wait_ge(m_kept, 8)
                for tt in range(TT):
                    for h in range(4):
                        f = slice(h * HD, (h + 1) * HD)
                        pe.matmul(m.ps[:, 4 + tt, f], MbT[:, h, tt, :], sa[:, tt, f], start=(h == 0), stop=False,
                                  skip_group_check=True)
                        pe.matmul(m.ps[:, 4 + tt, f], MkT[:, h, tt, :], v_tok[:, tt, f], start=False, stop=False,
                                  skip_group_check=True)
                    for c in (2 * tt, 2 * tt + 1):
                        o = c % 2 * CH
                        for j in range(2):
                            mm = pe.matmul(m.ps[o:o + CH, 4 + tt, j * P:(j + 1) * P], rho[:, j, c * CH:(c + 1) * CH],
                                           state[:, c, j, :], start=False, stop=(j == 1), skip_group_check=True)
                    mm.then_inc(o_ready, 1)
                for tt in range(TT):
                    pe.wait_ge(y_ready, tt + 1)
                    for j in range(2):
                        mm = pe.transpose(m.ps[:, j, tt * P:(tt + 1) * P], y[:, tt, j * P:(j + 1) * P], m.ident[:])
                    mm.then_inc(y_turned, 1)

            @block.vector
            def _(dve):
                do = Step(dve, step)
                dve.memset(state[:, 0], 0.0).then_inc(s_ready, 1)
                dve.wait_ge(s_ready, 1)
                dve.wait_ge(loaded, 32)
                for n in range(8):
                    dve.wait_ge(m_ready, n + 1)
                    dst = (MbT, MkT)[n // 4]
                    dve.tensor_tensor(dst[:, n % 4], m.ps[:, 4 + n % 4, :].rearrange("p (t i) -> p t i", t=TT),
                                      upto[:].unsqueeze(1).to_broadcast([P, TT, P]), ALU.mult).then_inc(m_kept, 1)
                for c in range(NC):
                    o, tt = c % 2 * CH, c // 2
                    dve.wait_ge(sa_ready, c + 1)
                    dve.scalar_tensor_tensor(sa[o:o + CH, tt, :], m.ps[o:o + CH, c % 2, 0:GROUP], -1.0,
                                             w[o:o + CH, tt, :], ALU.mult, ALU.subtract).then_inc(sa_kept, 1)
                    if c < NC - 1:
                        dve.wait_ge(d_ready, c + 1)
                        do(dve.tensor_tensor(t[:].rearrange("p j v -> p (j v)"), m.ps[:, 2 + c % 2, 0:GROUP],
                                             state[:, c].rearrange("p j v -> p (j v)"), ALU.add))
                        dve.wait_ge(pm_ready, c + 1)
                        dve.tensor_tensor(state[:, c + 1], t[:], pm[:, c], ALU.mult).then_inc(s_ready, 1)
                        dve.wait_ge(s_ready, c + 2)
                group_norm_rows(m, dve, do, 4, o_ready, y, stats, mv, LNX_EPS, var_ready, rs_ready, rs, y_ready)
                dve.wait_ge(y_turned, TT)
                for j in range(2):
                    do(dve.tensor_scalar(yl[:, j, :], m.ps[:, j, :], cols[:, C_LG + j:C_LG + j + 1],
                                         cols[:, C_LB + j:C_LB + j + 1], ALU.mult, ALU.add))
                do(dve.tensor_tensor(yl[:], yl[:], bonus[:], ALU.add))
                dve.tensor_tensor(m.mixT[:, 4:6, :], yl[:], gate[:], ALU.mult)


def group_norm_rows(m, dve, do, bank, o_ready, y, stats, mv, eps, var_ready, rs_ready, rs, y_ready):
    for tt in range(TT):
        dve.wait_ge(o_ready, tt + 1)
        do(dve.tensor_copy(y[:, tt, :], m.ps[:, bank + tt, 0:GROUP]))
        for h in range(4):
            do(dve.bn_stats(stats[:, tt, h, :], y[:, tt, h * HD:(h + 1) * HD]))
            do(dve.bn_aggr(mv[:, tt, h, :], stats[:, tt, h, :]))
    dve.tensor_scalar(mv[:, :, :, 1], mv[:, :, :, 1], eps, None, ALU.add).then_inc(var_ready, 1)
    dve.wait_ge(rs_ready, 1)
    for tt in range(TT):
        y3 = y[:, tt, :].rearrange("p (h d) -> p h d", h=4)
        do(dve.tensor_tensor(y3, y3, mv[:, tt, :, 0:1].to_broadcast([P, 4, HD]), ALU.subtract))
        dve.tensor_tensor(y3, y3, rs[:, tt, :].unsqueeze(2).to_broadcast([P, 4, HD]), ALU.mult).then_inc(y_ready, 1)


def rwkv_mixer(m, l, A, cols):
    with ExitStack() as ctx:
        rho, kap, bet, khat, gate, bonus = (m.sbuf(ctx, "rw_" + n, [P, 2, SEQ])
                                            for n in ("rho", "kap", "bet", "khat", "gate", "bonus"))
        kap_tok, bet_tok, kh_tok, v_tok = (m.sbuf(ctx, "rw_" + n, [P, TT, GROUP])
                                           for n in ("kap_tok", "bet_tok", "kh_tok", "v_tok"))
        pend = m.sbuf(ctx, "rw_pend", [P, 2, NC])
        with ExitStack() as c2:
            mixed = m.sbuf(c2, "rw_mixed", [P, 9, SEQ])
            rwkv_project(m, mixed, cols)
            rwkv_prepare(m, l, A, cols, mixed, rho, kap, bet, khat, gate, bonus, pend)
            turn_stage(m, [(kap, kap_tok), (bet, bet_tok), (khat, kh_tok), (mixed[:, 4:6], v_tok)])
        uT = m.sbuf(ctx, "rw_uT", [P, 2, SEQ])
        w = m.sbuf(ctx, "rw_w", [P, TT, GROUP])
        rwkv_inverse(m, kap, bet, khat, kap_tok, v_tok, uT, w)
        rwkv_scan(m, cols, rho, bet, khat, bet_tok, kh_tok, v_tok, uT, w, pend, gate, bonus)


def angles_stage(m, A, cos, sin):
    nc = m.nc
    loaded, step, ready, *_ = m.stage()
    MAGIC = 1.5 * 2.0 ** 23
    C1 = 6.28125
    C2 = float(np.float32(TWO_PI - C1))
    C3 = float(TWO_PI - C1 - C2)
    PI = 3.1415925
    with ExitStack() as ctx:
        pos_i = m.sbuf(ctx, "pos_i", [P, TT], I32)
        pos = m.sbuf(ctx, "pos", [P, TT])
        freq = m.sbuf(ctx, "freq", [P, 32])
        x, n, c = (m.sbuf(ctx, s, [P, TT, 32]) for s in ("x", "n", "c"))
        with nc.Block() as block:
            @block.sync
            def _(sp):
                m.clear_previous(sp)
                with nc.allow_non_contiguous_dma(reason="512 numbers, one for each token's partition"):
                    sp.dma_start(pos_i[:], A["positions_2"][0].rearrange("(t p) -> p t", p=P)).then_inc(loaded, 16)
                sp.dma_start(freq[:], m.table("inv_freq")).then_inc(loaded, 16)
                m.feed(sp, 0)

            @block.vector
            def _(dve):
                do = Step(dve, step)
                dve.wait_ge(loaded, 32)
                do(dve.tensor_copy(pos[:], pos_i[:]))
                for tt in range(TT):
                    do(dve.tensor_scalar(x[:, tt, :], freq[:], pos[:, tt:tt + 1], None, ALU.mult))
                do(dve.tensor_scalar(n[:], x[:], 1.0 / TWO_PI, None, ALU.mult))
                do(dve.tensor_scalar(n[:], n[:], MAGIC, None, ALU.add))
                do(dve.tensor_scalar(n[:], n[:], MAGIC, None, ALU.subtract))
                for k in (C1, C2, C3):
                    do(dve.scalar_tensor_tensor(x[:], n[:], -k, x[:], ALU.mult, ALU.add))
                do(dve.tensor_scalar(c[:], x[:], float(np.pi / 2), None, ALU.add))
                do(dve.tensor_scalar(n[:], c[:], float(np.pi), None, ALU.is_gt))
                do(dve.scalar_tensor_tensor(c[:], n[:], -TWO_PI, c[:], ALU.mult, ALU.add))
                do(dve.tensor_scalar(c[:], c[:], PI, -PI, ALU.min, ALU.max))
                dve.tensor_scalar(x[:], x[:], PI, -PI, ALU.min, ALU.max).then_inc(ready, 1)

            @block.scalar
            def _(act):
                act.wait_ge(ready, 1)
                act.activation(sin[:], x[:], ACT.Sin)
                act.activation(cos[:], c[:], ACT.Sin)


def ret_mixer(m, A):
    nc = m.nc
    with ExitStack() as ctx:
        qk = m.sbuf(ctx, "re_qk", [P, TT, 512])
        rot = m.sbuf(ctx, "re_rot", [P, TT, 512])
        qkT = m.sbuf(ctx, "re_qkT", [P, 4, SEQ])
        gate = m.sbuf(ctx, "re_gate", [P, 2, SEQ])
        v = m.sbuf(ctx, "re_v", [P, TT, GROUP])
        cos, sin = (m.sbuf(ctx, n, [P, TT, 32]) for n in ("cos", "sin"))
        decay = m.sbuf(ctx, "decay", [P, 4, SEQ])
        tmp = m.sbuf(ctx, "re_tmp", [P, 8, 32])
        scores = m.sbuf(ctx, "re_scores", [P, 2, TT, SEQ])
        y = m.sbuf(ctx, "re_y", [P, TT, GROUP])
        stats = m.sbuf(ctx, "stats", [P, TT, 4, 6])
        mv = m.sbuf(ctx, "mv", [P, TT, 4, 2])
        rs = m.sbuf(ctx, "rs", [P, TT, 4])
        half = m.sbuf(ctx, "half", [P, TT, 4])
        angles_stage(m, A, cos, sin)
        (loaded, tok_ready, tok_kept, tile_ready, tile_kept, rot_ready, turned, turn_kept, half_ready, *_) = m.stage()
        with nc.Block() as block:
            @block.sync
            def _(sp):
                m.clear_previous(sp)
                m.feed(sp, 2)

            @block.tensor
            def _(pe):
                project_tok(m, pe, m.take(pe, KT), m.hT, (0, 512), (4, 5, 6, 7), 0, tok_ready, tok_kept)
                released(m, pe, tok_ready, 4)
                w = m.take(pe, KT)
                project_tok(m, pe, w, m.hT, (0, GROUP), (4, 5, 6, 7), 4, tok_ready, tok_kept)
                project_cols(m, pe, w, [(GROUP, GROUP + P), (GROUP + P, 512)], (0, 1), 0, tile_ready, tile_kept)
                released(m, pe, tile_ready, 2)
                for tt in range(TT):
                    pe.wait_ge(rot_ready, tt + 1)
                    if tt >= 2:
                        pe.wait_ge(turn_kept, tt - 1)
                    for j in range(4):
                        mm = pe.transpose(m.ps[:, 2 + tt % 2, j * P:(j + 1) * P], rot[:, tt, j * P:(j + 1) * P],
                                          m.ident[:])
                    mm.then_inc(turned, 1)

            @block.scalar
            def _(act):
                for n in range(2):
                    act.wait_ge(tile_ready, n + 1)
                    act.activation(gate[:, n, :], m.ps[:, n, :], ACT.Silu).then_inc(tile_kept, 1)
                for tt in range(TT):
                    act.wait_ge(turned, tt + 1)
                    act.copy(qkT[:, :, tt * P:(tt + 1) * P],
                             m.ps[:, 2 + tt % 2, :].rearrange("p (j t) -> p j t", j=4)).then_inc(turn_kept, 1)

            @block.vector
            def _(dve):
                do = Step(dve, half_ready)
                for tt in range(TT):
                    dve.wait_ge(tok_ready, tt + 1)
                    dve.tensor_copy(qk[:, tt, :], m.ps[:, 4 + tt, :]).then_inc(tok_kept, 1)
                dve.wait_ge(tok_kept, 4)
                for tt in range(TT):
                    s = qk[:, tt, :].rearrange("p (h o e) -> p h o e", o=2, e=32)
                    d = rot[:, tt, :].rearrange("p (h o e) -> p h o e", o=2, e=32)
                    c = cos[:, tt].unsqueeze(1).to_broadcast([P, 8, 32])
                    n_ = sin[:, tt].unsqueeze(1).to_broadcast([P, 8, 32])
                    do(dve.tensor_tensor(d[:, :, 0], s[:, :, 0], c, ALU.mult))
                    do(dve.tensor_tensor(tmp[:], s[:, :, 1], n_, ALU.mult))
                    do(dve.tensor_tensor(d[:, :, 0], d[:, :, 0], tmp[:], ALU.subtract))
                    do(dve.tensor_tensor(d[:, :, 1], s[:, :, 0], n_, ALU.mult))
                    do(dve.tensor_tensor(tmp[:], s[:, :, 1], c, ALU.mult))
                    ins = dve.tensor_tensor(d[:, :, 1], d[:, :, 1], tmp[:], ALU.add)
                    ins.then_inc(rot_ready, 1)
                    dve.wait_ge(rot_ready, tt + 1)
                for tt in range(TT):
                    dve.wait_ge(tok_ready, 5 + tt)
                    dve.tensor_copy(v[:, tt, :], m.ps[:, 4 + tt, 0:GROUP]).then_inc(tok_kept, 1)

        (loaded, s_ready, s_kept, o_ready, var_ready, rs_ready, y_ready, y_turned, half_ready, step, *_) = m.stage()
        with nc.Block() as block:
            @block.sync
            def _(sp):
                m.clear_previous(sp)
                sp.dma_start(decay[:], m.decay).then_inc(loaded, 16)
                m.feed(sp, 0)

            @block.gpsimd
            def _(pool):
                nc.gpsimd.memset(half[:], -0.5).then_inc(half_ready, 1)
                pool.wait_ge(half_ready, 1)
                pool.wait_ge(var_ready, 1)
                nc.gpsimd.tensor_tensor(rs[:], mv[:, :, :, 1], half[:], ALU.pow).then_inc(rs_ready, 1)

            @block.tensor
            def _(pe):
                m.warm_up(pe, 7)
                for h in range(5):
                    if h < 4:
                        j, at = h // 2, h % 2 * HD
                        for J in range(TT):
                            n = 4 * h + J
                            if h:
                                pe.wait_ge(s_kept, n - 3)
                            pe.matmul(m.ps[:, J, J * P:], qkT[at:at + HD, 2 + j, J * P:(J + 1) * P],
                                      qkT[at:at + HD, j, J * P:], start=True, stop=True).then_inc(s_ready, 1)
                    if h:
                        g = h - 1
                        for tt in range(TT):
                            pe.wait_ge(s_kept, 4 * g + tt + 1)
                            for J in range(tt + 1):
                                mm = pe.matmul(m.ps[:, 4 + tt, g * HD:(g + 1) * HD],
                                               scores[:, g % 2, J, tt * P:(tt + 1) * P],
                                               v[:, J, g * HD:(g + 1) * HD], start=(J == 0), stop=(J == tt))
                            mm.then_inc(o_ready, 1)
                for tt in range(TT):
                    pe.wait_ge(y_ready, tt + 1)
                    for j in range(2):
                        mm = pe.transpose(m.ps[:, j, tt * P:(tt + 1) * P], y[:, tt, j * P:(j + 1) * P], m.ident[:])
                    mm.then_inc(y_turned, 1)

            @block.vector
            def _(dve):
                do = Step(dve, step)
                dve.wait_ge(loaded, 16)
                for h in range(4):
                    for J in range(TT):
                        dve.wait_ge(s_ready, 4 * h + J + 1)
                        if h >= 2:
                            dve.wait_ge(o_ready, 4 * (h - 1))
                        dve.scalar_tensor_tensor(scores[:, h % 2, J, J * P:], m.ps[:, J, J * P:], HD ** -0.5,
                                                 decay[:, h, 0:SEQ - J * P], ALU.mult, ALU.mult).then_inc(s_kept, 1)
                dve.wait_ge(o_ready, 12)
                for tt in range(TT):
                    dve.wait_ge(o_ready, 13 + tt)
                    do(dve.tensor_copy(y[:, tt, :], m.ps[:, 4 + tt, 0:GROUP]))
                    for h in range(4):
                        do(dve.bn_stats(stats[:, tt, h, :], y[:, tt, h * HD:(h + 1) * HD]))
                        do(dve.bn_aggr(mv[:, tt, h, :], stats[:, tt, h, :]))
                dve.tensor_scalar(mv[:, :, :, 1], mv[:, :, :, 1], LN_EPS, None, ALU.add).then_inc(var_ready, 1)
                dve.wait_ge(rs_ready, 1)
                for tt in range(TT):
                    y3 = y[:, tt, :].rearrange("p (h d) -> p h d", h=4)
                    do(dve.tensor_tensor(y3, y3, mv[:, tt, :, 0:1].to_broadcast([P, 4, HD]), ALU.subtract))
                    dve.tensor_tensor(y3, y3, rs[:, tt, :].unsqueeze(2).to_broadcast([P, 4, HD]),
                                      ALU.mult).then_inc(y_ready, 1)
                dve.wait_ge(y_turned, TT)
                for j in range(2):
                    dve.tensor_tensor(m.mixT[:, 6 + j, :], m.ps[:, j, :], gate[:, j, :], ALU.mult)


def halves(n):
    return [range(0, min(2, n)), range(2, n)]


class Swiglu:

    SLOT = 2 * D
    RING = 4

    def __init__(self, m, ctx, name, wg, wu, wd, sizes):
        self.ring = m.sbuf(ctx, name + "_ring", [P, self.RING, self.SLOT])
        self.m, self.wg, self.wu, self.wd, self.sizes = m, wg, wu, wd, sizes
        sem = lambda n: m.ctx.enter_context(m.nc.semaphore(f"{name}_{n}"))
        self.landed = [sem(f"landed{i}") for i in range(self.RING)]
        (self.w_hi, self.w_lo, self.gate_ready, self.gu_ready, self.silu_ready, self.gu_read, self.hid_hi, self.hid_lo,
         self.d_ready, self.d_kept) = (sem(n) for n in ("w_hi", "w_lo", "gate_ready", "gu_ready", "silu_ready", "gu_read", "hid_hi",
                                                      "hid_lo", "d_ready", "d_kept"))

    def src(self, e, g, p):
        n = len(self.sizes)
        e, g = (e + g // n, g % n)
        lo = sum(self.sizes[:g]) * P
        if p < 4:
            tiles = halves(self.sizes[g])[p // 2]
            w = (self.wg, self.wu)[p % 2](e)
            return w.rearrange("(k p) c -> p k c", p=P)[:, :, lo + tiles[0] * P:lo + (tiles[-1] + 1) * P]
        rows = self.wd(e)[lo:lo + self.sizes[g] * P]
        return rows.rearrange("(k p) c -> p k c", p=P)[:, :, (p - 4) * 512:(p - 3) * 512]

    def shape(self, g, p):
        size = self.sizes[g % len(self.sizes)]
        return (KT, len(halves(size)[p // 2]) * P) if p < 4 else (size, 512)

    def view(self, buffer, g, p):
        k, c = self.shape(g, p)
        return buffer[:, (6 * g + p) % self.RING, 0:k * c].rearrange("p (k c) -> p k c", k=k)

    def load(self, sp, e, g, p):
        self.m.nc.sync.dma_start(self.view(self.ring, g, p), self.src(e, g, p)
                                 ).then_inc(self.landed[(6 * g + p) % self.RING], 16)

    def first_loads(self, sp):
        for p in range(self.RING):
            self.load(sp, 0, 0, p)


def swiglu_stage(m, F, turns, per_turn=1, gates=None):
    nc = m.nc
    step, gate_ready, *_ = m.stage()
    sizes = F.sizes * per_turn
    NG, NT = len(sizes), sum(sizes)
    before = [sum(sizes[:g]) for g in range(NG)]
    assert NG % 2 == 0 and NT % 2 == 0 and 6 * NG % F.RING == 0

    def run(eng, body):
        body(0, True)
        if turns > 1:
            with eng.Fori(1, turns) as r:
                body(r, False)

    with ExitStack() as ctx:
        x_hi, x_lo = m.xT[:, 0], m.xT[:, 1]
        w_hi, w_lo = (m.sbuf(ctx, n, [P, F.RING, F.SLOT], F32R) for n in ("w_hi", "w_lo"))
        silu = m.sbuf(ctx, "silu", [P, 2, SEQ])
        prod = m.sbuf(ctx, "prod", [P, 2, SEQ])
        hid = m.sbuf(ctx, "hid", [P, 2, 2, 4, SEQ], F32R)
        gate = m.sbuf(ctx, "gate", [P, per_turn, TT]) if gates is not None else None

        def wait_slot_used(eng, r, g, p):
            g, p = divmod(6 * g + p - F.RING, 6)
            size = sizes[g]
            if p < 4:
                eng.wait_ge(F.gu_ready, NT * r + (before[g] if g >= 0 else -size) + min(size, 2 * (p // 2 + 1)))
            else:
                eng.wait_ge(F.d_ready, 8 * (NG * r + g) + 4 * (p - 3))

        with nc.Block() as block:
            @block.sync
            def _(sp):
                m.clear_previous(sp)

                def body(r, first):
                    for g in range(NG):
                        for p in range(6):
                            if first and g == 0 and p < F.RING:
                                continue
                            c = 6 * (NG * r + g) + p
                            sp.wait_ge(F.w_lo, c - F.RING + 1)
                            F.load(sp, per_turn * r, g, p)
                run(sp, body)

            @block.tensor
            def _(pe):
                def products(out, pairs):
                    for j, ((l_hi, l_lo), (r_hi, r_lo)) in enumerate(pairs):
                        pe.matmul(out, l_hi, r_hi, start=(j == 0), stop=False)
                        pe.matmul(out, l_hi, r_lo, start=False, stop=False)
                        mm = pe.matmul(out, l_lo, r_hi, start=False, stop=(j == len(pairs) - 1))
                    return mm

                def body(r, first):
                    for g, size in enumerate(sizes):
                        G = NG * r + g
                        for half, tiles in enumerate(halves(size)):
                            for i in tiles:
                                t = before[g] + i
                                T = NT * r + t
                                if not (first and t < 2):
                                    pe.wait_ge(F.gu_read, T - 1)
                                for p, bank in ((2 * half, t % 2), (2 * half + 1, 2 + t % 2)):
                                    if i == tiles[0]:
                                        pe.wait_ge(F.w_lo, 6 * G + p + 1)
                                    at = slice((i - tiles[0]) * P, (i - tiles[0] + 1) * P)
                                    hi, lo = F.view(w_hi, g, p), F.view(w_lo, g, p)
                                    mm = products(m.ps[:, bank, :],
                                                  [((hi[:, j, at], lo[:, j, at]), (x_hi[:, j, :], x_lo[:, j, :]))
                                                   for j in range(KT)])
                                    mm.then_inc(F.gate_ready if bank < 2 else F.gu_ready, 1)
                        for q in range(2 * TT):
                            nh, tt = divmod(q, TT)
                            if q % TT == 0:
                                pe.wait_ge(F.w_lo, 6 * G + 4 + nh + 1)
                            if not (first and g == 0 and q < 4):
                                pe.wait_ge(F.d_kept, 8 * G + q - 3)
                            hi, lo = F.view(w_hi, g, 4 + nh), F.view(w_lo, g, 4 + nh)
                            for i in range(size):
                                if q == 0:
                                    pe.wait_ge(F.hid_hi, NT * r + before[g] + i + 1)
                                at = slice(tt * P, (tt + 1) * P)
                                x = [hid[:, g % 2, part, i, at] for part in range(2)]
                                out = m.ps[:, 4 + q % 4, :]
                                pe.matmul(out, x[0], hi[:, i, :], start=(i == 0), stop=False)
                                pe.matmul(out, x[0], lo[:, i, :], start=False, stop=False)
                                if q == 0:
                                    pe.wait_ge(F.hid_lo, NT * r + before[g] + i + 1)
                                mm = pe.matmul(out, x[1], hi[:, i, :], start=False, stop=(i == size - 1))
                            mm.then_inc(F.d_ready, 1)
                run(pe, body)

            @block.scalar
            def _(act):
                def body(r, first):
                    for g, size in enumerate(sizes):
                        G = NG * r + g

                        def split(*places):
                            for p in places:
                                slot, round_ = (6 * g + p) % F.RING, (6 * g + p) // F.RING
                                act.wait_ge(F.landed[slot], 16 * (6 * NG // F.RING * r + round_ + 1))
                                if not (first and g == 0 and p < F.RING):
                                    wait_slot_used(act, r, g, p)
                                act.copy(F.view(w_hi, g, p), F.view(F.ring, g, p)).then_inc(F.w_hi, 1)

                        split(0, 1, 2, 3)
                        for half, tiles in enumerate(halves(size)):
                            for i in tiles:
                                t = before[g] + i
                                T = NT * r + t
                                act.wait_ge(F.gate_ready, T + 1)
                                if not (first and t < 2):
                                    act.wait_ge(F.gu_read, T - 1)
                                act.activation(silu[:, t % 2, :], m.ps[:, t % 2, :],
                                               ACT.Silu).then_inc(F.silu_ready, 1)
                                act.wait_ge(F.gu_read, T + 1)
                                if i == 0 and not (first and g < 2):
                                    act.wait_ge(F.d_ready, 8 * (G - 1))
                                act.copy(hid[:, g % 2, 0, i, :], prod[:, t % 2, :]).then_inc(F.hid_hi, 1)
                            if half == 0:
                                split(4, 5)
                run(act, body)

            @block.vector
            def _(dve):
                do = Step(dve, step)
                def split(r, g, *places):
                    for p in places:
                        dve.wait_ge(F.w_hi, 6 * (NG * r + g) + p + 1)
                        dve.tensor_tensor(F.view(w_lo, g, p), F.view(F.ring, g, p), F.view(w_hi, g, p).bitcast(F32),
                                          ALU.subtract).then_inc(F.w_lo, 1)

                def body(r, first):
                    if gates is not None:
                        if not first:
                            dve.wait_ge(F.d_kept, 8 * NG * r)
                        for i in range(per_turn):
                            copy = dve.tensor_copy(gate[:, i:i + 1, :].rearrange("p o t -> p t o"),
                                                   gates[:, :, bass.ds(per_turn * r + i, 1)])
                        copy.then_inc(gate_ready, 1)
                    split(r, 0, 0, 1, 2, 3)
                    if first and gates is None:
                        h = m.h[:].rearrange("p t d -> p (t d)")
                        do(dve.tensor_scalar(h, h, ALPHA, None, ALU.mult))
                    for g, size in enumerate(sizes):
                        G = NG * r + g
                        for half, tiles in enumerate(halves(size)):
                            for i in tiles:
                                t = before[g] + i
                                T = NT * r + t
                                dve.wait_ge(F.silu_ready, T + 1)
                                dve.wait_ge(F.gu_ready, T + 1)
                                if not (first and t < 2):
                                    dve.wait_ge(F.hid_lo, T - 1)
                                dve.tensor_tensor(prod[:, t % 2, :], m.ps[:, 2 + t % 2, :], silu[:, t % 2, :],
                                                  ALU.mult).then_inc(F.gu_read, 1)
                                dve.wait_ge(F.hid_hi, T + 1)
                                dve.tensor_tensor(hid[:, g % 2, 1, i, :], prod[:, t % 2, :],
                                                  hid[:, g % 2, 0, i, :].bitcast(F32),
                                                  ALU.subtract).then_inc(F.hid_lo, 1)
                            if half == 0:
                                split(r, g, 4, 5)
                        if g < NG - 1:
                            split(r, g + 1, 0, 1)
                        if g == 0 and gates is not None:
                            dve.wait_ge(gate_ready, r + 1)
                        for q in range(2 * TT):
                            nh, tt = divmod(q, TT)
                            n = 8 * G + q
                            dve.wait_ge(F.d_ready, n + 1)
                            if not (first and g == 0):
                                dve.wait_ge(F.d_kept, n - 7)
                            h = m.h[:, tt, nh * 512:(nh + 1) * 512]
                            if gates is None:
                                dve.tensor_tensor(h, h, m.ps[:, 4 + q % 4, :], ALU.add).then_inc(F.d_kept, 1)
                            else:
                                dve.scalar_tensor_tensor(h, m.ps[:, 4 + q % 4, :],
                                                         gate[:, g // len(F.sizes), tt:tt + 1], h, ALU.mult,
                                                         ALU.add).then_inc(F.d_kept, 1)
                        if g < NG - 1:
                            split(r, g + 1, 2, 3)
                run(dve, body)


def router_stage(m, w, w_loaded, gates):
    nc = m.nc
    ready, shifted, ex_ready, step, *_ = m.stage()
    E = EXPERTS
    with ExitStack() as ctx:
        lg, p, pick, t, iota = (m.sbuf(ctx, n, [P, TT, E]) for n in ("lg", "p", "pick", "t", "iota"))
        first = m.sbuf(ctx, "first", [P, TT, E])
        mx, s = (m.sbuf(ctx, n, [P, TT]) for n in ("mx", "s"))
        wide = lambda c: c[:].unsqueeze(2).to_broadcast([P, TT, E])
        with nc.Block() as block:
            @block.sync
            def _(sp):
                m.clear_previous(sp)

            @block.tensor
            def _(pe):
                pe.wait_ge(w_loaded, 16)
                for tt in range(TT):
                    for n in range(2 * KT):
                        j, part = divmod(n, 2)
                        mm = pe.matmul(m.ps[:, 0, tt * E:(tt + 1) * E],
                                       m.xT[:, part, j, tt * P:(tt + 1) * P].bitcast(F32), w[:, j, :],
                                       start=(n == 0), stop=(n == 2 * KT - 1))
                mm.then_inc(ready, 1)

            @block.scalar
            def _(act):
                act.wait_ge(shifted, 1)
                act.activation(p[:], lg[:], ACT.Exp).then_inc(ex_ready, 1)

            @block.vector
            def _(dve):
                do = Step(dve, step)
                h = m.h[:].rearrange("p t d -> p (t d)")
                do(dve.tensor_scalar(h, h, ALPHA, None, ALU.mult))
                for e in range(E):
                    do(dve.memset(iota[:, :, e:e + 1], float(e)))
                dve.wait_ge(ready, 1)
                do(dve.tensor_copy(lg[:].rearrange("p t e -> p (t e)"), m.ps[:, 0, 0:TT * E]))
                do(dve.reduce_max(mx[:], lg[:], AX.X))
                dve.tensor_tensor(lg[:], lg[:], wide(mx), ALU.subtract).then_inc(shifted, 1)
                dve.wait_ge(ex_ready, 1)
                do(dve.reduce_sum(s[:], p[:], AX.X))
                do(dve.reciprocal(s[:], s[:]))
                do(dve.tensor_tensor(p[:], p[:], wide(s), ALU.mult))
                do(dve.tensor_copy(lg[:], p[:]))
                for k in range(2):
                    do(dve.reduce_max(mx[:], lg[:], AX.X))
                    do(dve.tensor_tensor(t[:], lg[:], wide(mx), ALU.is_equal))
                    do(dve.tensor_scalar(pick[:], t[:], -float(E), float(E), ALU.mult, ALU.add))
                    do(dve.tensor_tensor(pick[:], pick[:], iota[:], ALU.add))
                    do(dve.tensor_reduce(s[:], pick[:], AX.X, ALU.min))
                    do(dve.tensor_tensor(t[:], iota[:], wide(s), ALU.is_equal))
                    if k == 0:
                        do(dve.tensor_copy(first[:], t[:]))
                        do(dve.scalar_tensor_tensor(lg[:], t[:], -2.0, lg[:], ALU.mult, ALU.add))
                do(dve.tensor_tensor(t[:], t[:], first[:], ALU.add))
                do(dve.tensor_tensor(p[:], p[:], t[:], ALU.mult))
                do(dve.reduce_sum(s[:], p[:], AX.X))
                do(dve.reciprocal(s[:], s[:]))
                dve.tensor_tensor(gates[:], p[:], wide(s), ALU.mult)


def feed_forward(m, ctx, l, A):
    if l % 2 == 0:
        w = lambda name: lambda e: A[name][l // 2]
        return Swiglu(m, ctx, f"dense{l}", w("ffn_w_gate_2"), w("ffn_w_up_2"), w("ffn_w_down_2"), [4, 4, 4, 4, 3, 3])
    w = lambda name: lambda e: A[name][l // 2, bass.ds(e, 1)].rearrange("a r c -> (a r) c")
    return Swiglu(m, ctx, f"moe{l}", w("moe_w_gate_2"), w("moe_w_up_2"), w("moe_w_down_2"), [4, 4, 3])


def moe_ffn(m, F, w, w_loaded):
    with ExitStack() as ctx:
        gates = m.sbuf(ctx, "gates", [P, TT, EXPERTS])
        router_stage(m, w, w_loaded, gates)
        swiglu_stage(m, F, EXPERTS // 2, 2, gates)


def second_block_layer(m, l, A, out):
    w_in = A["w_in_2"][l]
    c = lambda lo, n=512: rows_chunk(w_in, (lo, lo + n))
    m.plan = [c(HGRN), c(HGRN + 512), c(GLA), c(GLA + 512, 272), c(RWKV), c(RWKV + 512), c(RWKV + D, 32),
              c(RET), c(RET + 512), rows_chunk(A["w_out_2"][l], (0, 512)), rows_chunk(A["w_out_2"][l], (512, D))]
    with ExitStack() as ctx:
        m.mixer_buffers(ctx)
        cols = m.sbuf(ctx, "cols", [P, C_N])
        lb = m.sbuf(ctx, "lb", [P, 4])
        params_stage(m, l, A, cols, lb)
        hgrn_mixer(m, cols, lb)
        gla_mixer(m, l, A, cols)
        rwkv_mixer(m, l, A, cols)
        ret_mixer(m, A)
        out_stage(m)
        end_ring_stage(m)
    with ExitStack() as ctx:
        m.xT = m.sbuf(ctx, "xT", [P, 2, KT, SEQ], F32R)
        F = feed_forward(m, ctx, l, A)
        if l % 2 == 0:
            norm_stage(m, A["ln1_g_2"][l], A["ln1_b_2"][l], parts=True, start_loads=F.first_loads)
            swiglu_stage(m, F, 1)
        else:
            router = m.sbuf(ctx, "router", [P, KT, EXPERTS])
            router_loaded = ctx.enter_context(m.nc.semaphore("router_loaded"))

            def start_loads(sp):
                m.nc.sync.dma_start(router[:], A["moe_router_2"][l // 2].rearrange("(k p) e -> p k e", p=P)
                                    ).then_inc(router_loaded, 16)
                F.first_loads(sp)

            norm_stage(m, A["ln1_g_2"][l], A["ln1_b_2"][l], parts=True, start_loads=start_loads)
            moe_ffn(m, F, router, router_loaded)
    norm_stage(m, A["ln2_g_2"][l], A["ln2_b_2"][l], store=out)


def build_program(nc, A, out, tables, decay):
    A = dict(A)
    A["rpb_pad"] = nc.dram_tensor("rpb_pad", [HEADS, 15, 2 * GRID_W - 1], F32, kind="Internal").ap()
    with ExitStack() as ctx:
        m = Machine(nc, ctx, tables)
        m.decay = decay
        first_load_stage(m, A["x"][0])
        with ExitStack() as first:
            m.first_block_buffers(first)
            norm_stage(m, A["ln_in_g"], A["ln_in_b"], parts=True)
            turn = m.turn
            with nc.Fori(0, DEPTH) as l:
                first_block_layer(m, l, A)
                if m.turn != turn:
                    idle_stage(m)
        m.second_block_buffers(ctx)
        turn_h_stage(m)
        for l in range(DEPTH):
            second_block_layer(m, l, A, out[0] if l == DEPTH - 1 else None)


_INS = ["x", "ln_in_g", "ln_in_b", "w_in", "b_in", "na_rpb", "q_norm_g", "k_norm_g", "sg_ln_g", "sg_ln_b", "sg_w",
        "sg_b", "w_br_a", "w_br_b", "w_br_c", "w_out", "b_out", "ln_post_g", "ln_post_b", "positions_2", "w_in_2",
        "w_out_2", "ln1_g_2", "ln1_b_2", "ln2_g_2", "ln2_b_2", "hgrn_lb_logits_2", "hgrn_norm_g_2", "gla_gate_w2_2",
        "gla_gate_b_2", "gla_norm_g_2", "rwkv_mu_2", "rwkv_w0_2", "rwkv_w2_2", "rwkv_a0_2", "rwkv_a2_2",
        "rwkv_g2_2", "rwkv_k_k_2", "rwkv_k_a_2", "rwkv_r_k_2", "rwkv_lnx_g_2", "rwkv_lnx_b_2", "rwkv_v0_2",
        "rwkv_v1_2", "rwkv_v2_2", "ffn_w_gate_2", "ffn_w_up_2", "ffn_w_down_2", "moe_router_2", "moe_w_gate_2",
        "moe_w_up_2", "moe_w_down_2"]


def kernel(**inputs):
    import concourse.bacc as _bacc
    from concourse import mybir as _mybir
    from concourse.bass_utils import run_bass_kernel_spmd as _run

    nc = _bacc.Bacc("TRN2", target_bir_lowering=False, num_devices=1)
    arrays, args = {}, {}

    def given(name, a):
        a = np.ascontiguousarray(a)
        arrays[f"in_{name}"] = a
        return nc.dram_tensor(f"in_{name}", a.shape, _mybir.dt.from_np(a.dtype), kind="ExternalInput").ap()

    for name in _INS:
        args[name] = given(name, inputs[name])
    tables, decay = given("tables", make_tables()), given("decay", make_decay_table())
    out = nc.dram_tensor("out_0", (1, SEQ, D), F32, kind="ExternalOutput").ap()
    build_program(nc, args, out, tables, decay)
    r = _run(nc, [arrays], core_ids=[0])
    return r.results[0]["out_0"]
```
